# Optimizing a Trainium2 kernel written in Bass

```python
import jax, jax.numpy as jnp
from jax import lax
import numpy as np

D_MODEL = 1024
BATCH = 1
SEQ = 128
DEPTH = 1
DEC_BATCH = 1
DEC_SEQ = 1024
PAST_LEN = 128

GRID_W = 64
H_A = 8
N_A = 64
D_A = H_A * N_A
H_B = 8
N_B = 64
D_B = H_B * N_B
LORA_W = 64
LORA_A = 64
LORA_G = 128
D_A_COLS = 3 * D_A + LORA_W + LORA_A + LORA_G
D_IN = D_A_COLS + 3 * D_B
WIN_R = 8
WIN_C = 16
N_EXPERTS = 16
EC_FACTOR = 2
D_EXPERT = 2816
RMS_EPS = 1e-6
GN_EPS = 64e-5
ATTN_SCALE = N_B ** -0.5
NEG_INF = -1e30

kernel_name = 'hybrid_rwkv7_natten_ec_diffusion_step'

def rmsnorm(x, g):
    xf = x.astype(jnp.float32)
    y = xf * lax.rsqrt(jnp.mean(xf * xf, axis=-1, keepdims=True) + RMS_EPS)
    return y.astype(x.dtype) * g

def adaln(cond, w_mod, b_mod):
    mod = jax.nn.silu(cond) @ w_mod + b_mod
    return tuple(m[:, None, :] for m in jnp.split(mod, 6, axis=-1))

def centred_shift(p, mu_prev, mu_next):
    zero = jnp.zeros_like(p[:, :1])
    p_prev = jnp.concatenate([zero, p[:, :-1]], axis=1)
    p_next = jnp.concatenate([p[:, 1:], zero], axis=1)
    return p + mu_prev * (p_prev - p) + mu_next * (p_next - p)

def rwkv_scan(r, decay, k, v, kk, a, s0, reverse):
    xs = tuple(jnp.moveaxis(t.astype(jnp.float32), 1, 0) for t in (r, decay, k, v, kk, a))

    def step(s, inp):
        r_t, w_t, k_t, v_t, kk_t, a_t = inp
        sa = jnp.einsum('bhvk,bhk->bhv', s, -kk_t)
        s = (s * w_t[:, :, None, :] + sa[..., None] * (kk_t * a_t)[:, :, None, :]
             + v_t[..., None] * k_t[:, :, None, :])
        return s, jnp.einsum('bhvk,bhk->bhv', s, r_t)

    s_fin, ys = lax.scan(step, s0.astype(jnp.float32), xs, reverse=reverse)
    return jnp.moveaxis(ys, 0, 1), s_fin

def rwkv_mixer(pa, s0, w0, w_up, a0, a_up, g_up, k_k, k_a, r_k, gn_g, gn_b):
    b, t, _ = pa.shape
    idx = [D_A, 2 * D_A, 3 * D_A, 3 * D_A + LORA_W, 3 * D_A + LORA_W + LORA_A]
    r, k, v, wlo, alo, glo = jnp.split(pa, idx, axis=-1)
    heads = lambda z: z.reshape(b, t, H_A, N_A)
    kkf = heads((k * k_k).astype(jnp.float32))
    kk = kkf * lax.rsqrt(jnp.sum(kkf * kkf, axis=-1, keepdims=True) + 1e-12)
    g = jax.nn.sigmoid(glo) @ g_up
    ys, bonuses, finals = [], [], []
    for d, rev in enumerate((False, True)):
        w_log = -jax.nn.softplus(-(w0[d] + jnp.tanh(wlo) @ w_up[d]).astype(jnp.float32)) - 0.5
        decay = jnp.exp(-jnp.exp(w_log))
        a = jax.nn.sigmoid(a0[d] + alo @ a_up[d])
        kd = k * (1 + (a - 1) * k_a)
        y, s_fin = rwkv_scan(heads(r), heads(decay), heads(kd), heads(v), kk, heads(a), s0[:, d], rev)
        ys.append(y)
        bonuses.append(jnp.sum((heads(r) * heads(kd) * r_k).astype(jnp.float32), axis=-1, keepdims=True))
        finals.append(s_fin)
    yf = ys[0] + ys[1]
    mu = jnp.mean(yf, axis=-1, keepdims=True)
    var = jnp.mean(jnp.square(yf - mu), axis=-1, keepdims=True)
    yn = ((yf - mu) * lax.rsqrt(var + GN_EPS)).reshape(b, t, D_A).astype(pa.dtype)
    y = yn * gn_g + gn_b
    y = y + ((bonuses[0] + bonuses[1]).astype(pa.dtype) * heads(v)).reshape(b, t, D_A)
    return y * g, jnp.stack(finals, axis=1).astype(pa.dtype)

def context_attention(q, k, v):
    b, t, _, _ = q.shape
    s = jnp.einsum('bqhn,bkhn->bhqk', q, k).astype(jnp.float32) * ATTN_SCALE
    p = jax.nn.softmax(s, axis=-1).astype(v.dtype)
    return jnp.einsum('bhqk,bkhn->bqhn', p, v).reshape(b, t, D_B)

def neighbourhood_attention(q, k, v, ctx_k, ctx_v, rpb):
    b, t, h, n = q.shape
    rows = t // GRID_W
    wr = min(WIN_R, rows)
    r_ids = jnp.arange(rows)
    row_start = jnp.clip(r_ids - wr // 2, 0, rows - wr)
    key_rows = row_start[:, None] + jnp.arange(wr)[None, :]
    kg = k.reshape(b, rows, GRID_W, h, n)[:, key_rows].reshape(b, rows, wr * GRID_W, h, n)
    vg = v.reshape(b, rows, GRID_W, h, n)[:, key_rows].reshape(b, rows, wr * GRID_W, h, n)
    qr = q.reshape(b, rows, GRID_W, h, n)
    s_loc = jnp.einsum('brqhn,brkhn->bhrqk', qr, kg).astype(jnp.float32) * ATTN_SCALE
    c_ids = jnp.arange(GRID_W)
    col_start = jnp.clip(c_ids - WIN_C // 2, 0, GRID_W - WIN_C)
    key_col = jnp.arange(wr * GRID_W) % GRID_W
    mask = (key_col[None, :] >= col_start[:, None]) & (key_col[None, :] < col_start[:, None] + WIN_C)
    dr_idx = key_rows - r_ids[:, None] + WIN_R - 1
    dc_idx = jnp.clip(c_ids[None, :] - c_ids[:, None] + WIN_C - 1, 0, 2 * WIN_C - 2)
    bias = rpb[:, dr_idx[:, None, :, None], dc_idx[None, :, None, :]]
    bias = bias.reshape(h, rows, GRID_W, wr * GRID_W).astype(jnp.float32)
    s_loc = jnp.where(mask, s_loc + bias[None], NEG_INF)
    s_ctx = jnp.einsum('brqhn,blhn->bhrql', qr, ctx_k).astype(jnp.float32) * ATTN_SCALE
    p = jax.nn.softmax(jnp.concatenate([s_loc, s_ctx], axis=-1), axis=-1).astype(v.dtype)
    n_loc = wr * GRID_W
    o = (jnp.einsum('bhrqk,brkhn->brqhn', p[..., :n_loc], vg)
         + jnp.einsum('bhrql,blhn->brqhn', p[..., n_loc:], ctx_v))
    return o.reshape(b, t, D_B)

def expert_choice_ffn(h, router, e_gate, e_up, e_down):
    b, t, _ = h.shape
    cap = EC_FACTOR * t // N_EXPERTS
    aff = jax.nn.softmax(jnp.einsum('btd,de->bte', h, router).astype(jnp.float32), axis=-1)
    gate, idx = lax.top_k(jnp.swapaxes(aff, 1, 2), cap)
    bidx = jnp.arange(b)[:, None, None]
    xe = h[bidx, idx]
    hid = jax.nn.silu(jnp.einsum('becd,edf->becf', xe, e_gate)) * jnp.einsum('becd,edf->becf', xe, e_up)
    ye = jnp.einsum('becf,efd->becd', hid, e_down) * gate[..., None].astype(h.dtype)
    return jnp.zeros_like(h).at[bidx, idx].add(ye)

def trunk_layer(x, cond, s0, attend, norm1_g, norm2_g, w_mod, b_mod, w_in, mu_prev, mu_next,
                w0, w_up, a0, a_up, g_up, k_k, k_a, r_k, gn_g, gn_b, w_out,
                router, e_gate, e_up, e_down):
    b, t, _ = x.shape
    sh1, sc1, gt1, sh2, sc2, gt2 = adaln(cond, w_mod, b_mod)
    h = rmsnorm(x, norm1_g) * (1 + sc1) + sh1
    proj = jnp.einsum('btd,de->bte', h, w_in)
    pa = centred_shift(proj[..., :D_A_COLS], mu_prev, mu_next)
    qkv = proj[..., D_A_COLS:].reshape(b, t, 3, H_B, N_B)
    q, k, v = qkv[:, :, 0], qkv[:, :, 1], qkv[:, :, 2]
    ya, s_fin = rwkv_mixer(pa, s0, w0, w_up, a0, a_up, g_up, k_k, k_a, r_k, gn_g, gn_b)
    yb = attend(q, k, v)
    x = x + gt1 * jnp.einsum('bte,ed->btd', jnp.concatenate([ya, yb], axis=-1), w_out)
    h = rmsnorm(x, norm2_g) * (1 + sc2) + sh2
    x = x + gt2 * expert_choice_ffn(h, router, e_gate, e_up, e_down)
    return x, k, v, s_fin

def setup_inputs(seed: int = 0) -> dict:
    key = jax.random.key(seed)
    ks = jax.random.split(key, 40)
    nrm = lambda i, shape, s: jax.random.normal(ks[i], shape, jnp.float32) * s
    return {
        'x_prompt': nrm(0, (BATCH, SEQ, D_MODEL), 1.0),
        'x_sample': nrm(1, (DEC_BATCH, DEC_SEQ, D_MODEL), 1.0),
        'cache_na_k': nrm(2, (DEC_BATCH, DEPTH, PAST_LEN, H_B, N_B), 1.0),
        'cache_na_v': nrm(3, (DEC_BATCH, DEPTH, PAST_LEN, H_B, N_B), 1.0),
        'state_rwkv': nrm(4, (DEC_BATCH, DEPTH, 2, H_A, N_A, N_A), 0.5),
        'c': nrm(5, (DEC_BATCH, D_MODEL), 1.0),
        'c_ctx': nrm(6, (D_MODEL,), 1.0),
        'final_norm_g': 1.0 + nrm(7, (D_MODEL,), 0.05),
        'norm1_g': 1.0 + nrm(8, (DEPTH, D_MODEL), 0.05),
        'norm2_g': 1.0 + nrm(9, (DEPTH, D_MODEL), 0.05),
        'w_mod': nrm(10, (DEPTH, D_MODEL, 6 * D_MODEL), D_MODEL ** -0.5),
        'b_mod': nrm(11, (DEPTH, 6 * D_MODEL), 0.01),
        'w_in': nrm(12, (DEPTH, D_MODEL, D_IN), D_MODEL ** -0.5),
        'mu_prev': jax.random.uniform(ks[13], (DEPTH, D_A_COLS), jnp.float32, 0.0, 0.5),
        'mu_next': jax.random.uniform(ks[14], (DEPTH, D_A_COLS), jnp.float32, 0.0, 0.5),
        'w0': nrm(15, (DEPTH, 2, D_A), 0.5),
        'w_up': nrm(16, (DEPTH, 2, LORA_W, D_A), LORA_W ** -0.5),
        'a0': nrm(17, (DEPTH, 2, D_A), 0.5),
        'a_up': nrm(18, (DEPTH, 2, LORA_A, D_A), LORA_A ** -0.5),
        'g_up': nrm(19, (DEPTH, LORA_G, D_A), LORA_G ** -0.5),
        'k_k': 0.85 + nrm(20, (DEPTH, D_A), 0.05),
        'k_a': 1.0 + nrm(21, (DEPTH, D_A), 0.05),
        'r_k': nrm(22, (DEPTH, H_A, N_A), 0.1),
        'gn_g': 1.0 + nrm(23, (DEPTH, D_A), 0.05),
        'gn_b': nrm(24, (DEPTH, D_A), 0.01),
        'rpb': nrm(25, (DEPTH, H_B, 2 * WIN_R - 1, 2 * WIN_C - 1), 0.1),
        'w_out': nrm(26, (DEPTH, D_MODEL, D_MODEL), D_MODEL ** -0.5),
        'router': nrm(27, (DEPTH, D_MODEL, N_EXPERTS), D_MODEL ** -0.5),
        'e_gate': nrm(28, (DEPTH, N_EXPERTS, D_MODEL, D_EXPERT), D_MODEL ** -0.5),
        'e_up': nrm(29, (DEPTH, N_EXPERTS, D_MODEL, D_EXPERT), D_MODEL ** -0.5),
        'e_down': nrm(30, (DEPTH, N_EXPERTS, D_EXPERT, D_MODEL), D_EXPERT ** -0.5),
    }

def reference(x_prompt, x_sample, cache_na_k, cache_na_v, state_rwkv, c, c_ctx, final_norm_g,
              norm1_g, norm2_g, w_mod, b_mod, w_in, mu_prev, mu_next, w0, w_up, a0, a_up, g_up,
              k_k, k_a, r_k, gn_g, gn_b, rpb, w_out, router, e_gate, e_up, e_down):
    xp = x_prompt
    xs = x_sample
    new_k, new_v, new_s = [], [], []
    for l in range(DEPTH):
        lw = (norm1_g[l], norm2_g[l], w_mod[l], b_mod[l], w_in[l], mu_prev[l], mu_next[l],
              w0[l], w_up[l], a0[l], a_up[l], g_up[l], k_k[l], k_a[l], r_k[l], gn_g[l], gn_b[l],
              w_out[l], router[l], e_gate[l], e_up[l], e_down[l])
        s0_ctx = jnp.zeros((xp.shape[0], 2, H_A, N_A, N_A), jnp.float32)
        xp, k_ctx, v_ctx, s_ctx = trunk_layer(xp, c_ctx[None, :], s0_ctx, context_attention, *lw)
        new_k.append(k_ctx)
        new_v.append(v_ctx)
        new_s.append(s_ctx)
        ck, cv, rl = cache_na_k[:, l], cache_na_v[:, l], rpb[l]
        attend_latent = lambda q, k, v, ck=ck, cv=cv, rl=rl: neighbourhood_attention(q, k, v, ck, cv, rl)
        xs, _, _, _ = trunk_layer(xs, c, state_rwkv[:, l], attend_latent, *lw)
    y_prompt = rmsnorm(xp, final_norm_g)
    y_sample = rmsnorm(xs, final_norm_g)
    return (y_prompt, y_sample, jnp.stack(new_k, axis=1), jnp.stack(new_v, axis=1), jnp.stack(new_s, axis=1))


_drawn_inputs = setup_inputs


def setup_inputs(seed=0):
    import zlib

    import numpy as np

    out = dict(_drawn_inputs(seed))
    spreads = {}
    factors = {'state_rwkv': 6.437, 'b_mod': 2.846, 'gn_g': 2.879, 'gn_b': 23.551, 'rpb': 3.77}
    for name, (base, spread) in spreads.items():
        noise = np.random.default_rng([zlib.crc32(name.encode()), seed]).standard_normal(out[name].shape)
        drawn = base * np.exp(spread * noise) if base else spread * noise
        out[name] = __import__('jax').numpy.asarray(drawn.astype(out[name].dtype))
    for name, factor in factors.items():
        out[name] = (out[name] * factor).astype(out[name].dtype)
    return out
```

```python
from contextlib import ExitStack

import concourse.bass as bass
from concourse import mybir

F32 = mybir.dt.float32
BF16 = mybir.dt.bfloat16
I32 = mybir.dt.int32
U32 = mybir.dt.uint32
ALU = mybir.AluOpType
ACT = mybir.ActivationFunctionType
AX = mybir.AxisListType

P = 128
D = 1024
KD = D // P
NS = 1024
NP = 128
NT = NS + NP
TILES = NT // P
HEADS = 8
HN = 64
DA = HEADS * HN
PAIRS = HEADS // 2
ACOLS = 3 * DA + 256
DIN = ACOLS + 3 * DA
GRID = 64
WR, WC = 8, 16
NE = 16
FE = 2816
FB = FE // P
CAP = 2 * NS // NE
CAPP = 2 * NP // NE
TOK = CAP + CAPP
EPS = 1e-6
GN_EPS = 64e-5
KK_EPS = 1e-12
SCALE = HN ** -0.5
NEG = -1e30
DECAY = 0.6065306597126334
PIECES = [(0, 512), (512, 512), (1024, 128)]
V_MUP, V_MUN, V_W0, V_A0, V_KK, V_KA, V_RK, V_GG, V_GB = 0, 12, 24, 32, 40, 44, 48, 52, 56
V_MUPL, V_MUNL, V_C, V_G1, V_ROWS = 60, 62, 64, 80, 88
SH1, SC1, GT1, SH2, SC2, GT2 = range(6)


class Chip:

    def __init__(self, nc, ctx):
        self.nc, self.ctx, self.dram, self.sems = nc, ctx, {}, []
        self.passed = nc.alloc_semaphore("passed")
        self.bank = [ctx.enter_context(nc.psum_tensor(f"bank{i}", [P, 512], F32)) for i in range(8)]

    def sb(self, name, shape, dt=F32, ctx=None):
        return (ctx or self.ctx).enter_context(self.nc.sbuf_tensor(name, shape, dt))

    def sem(self, name):
        self.sems.append(self.nc.alloc_semaphore(name))
        return self.sems[-1]

    def hold(self, eng, sem, value):
        eng.wait_ge(sem, value)
        eng.sem_inc(self.passed, 1)

    def next_stage(self):
        self.nc.all_engine_barrier()
        self.nc.clear_and_free_semaphores(self.sems)
        self.nc.all_engine_barrier()
        self.sems = []


class Link:

    def __init__(self, eng, sem, chip=None):
        self.eng, self.sem, self.base, self.count, self.chip = eng, sem, 0, 0, chip

    def __call__(self, ins):
        self.count += 1
        ins.then_inc(self.sem, 1)
        if self.chip:
            self.chip.hold(self.eng, self.sem, self.base + self.count)
        else:
            self.eng.wait_ge(self.sem, self.base + self.count)

    def enter(self, i, per):
        self.start, self.per = self.base + self.count, per
        self.base, self.count = i * per + self.start, 0

    def leave(self, times):
        assert self.count == self.per, (self.sem, self.count)
        self.base, self.count = self.start + times * self.per, 0


def rows_view(ap, n, row=0):
    return bass.AP(tensor=ap.tensor, offset=row * P, ap=[[P, n], [1, P]])


def modulation(K, A):
    nc = K.nc
    CH = 1024
    NCH = 6 * D // CH
    ctx = ExitStack()
    with ctx:
        vrows = K.sb("vrows", [V_ROWS, P], ctx=ctx)
        brows = K.sb("brows", [48, P], ctx=ctx)
        bmodT = K.sb("bmodT", [P, 48], ctx=ctx)
        sig = K.sb("cond_sig", [P, 16], ctx=ctx)
        cond = K.sb("cond", [P, KD, 2], ctx=ctx)
        wbuf = [K.sb(f"wmod{i}", [P, KD, CH], ctx=ctx) for i in range(3)]
        rowi = K.sb("rowi", [P, P], I32, ctx=ctx)
        coli = K.sb("coli", [P, P], I32, ctx=ctx)
        xori = K.sb("xori", [P, P], I32, ctx=ctx)
        xorf = K.sb("xorf", [P, P], ctx=ctx)
        low = K.sb("low", [P, 2, P], ctx=ctx)
        cmp = K.sb("cmp", [P, P], ctx=ctx)
        mrows = K.sb("mrows", [96, P], ctx=ctx)
        rows_in = K.sem("m_rows_in")
        w_in = [K.sem(f"m_w_in{i}") for i in range(3)]
        g_chain = K.sem("m_pool_chain")
        consts = K.sem("m_consts")
        v_t = K.sem("m_vec_transposed")
        v_chain = K.sem("m_dve_chain")
        vec_ok = K.sem("m_vec_ok")
        sig_ok = K.sem("m_sig_ok")
        cond_ok = K.sem("m_cond_ok")
        mm_ok = K.sem("m_mod_mm")
        mod_ok = K.sem("m_mod_ok")
        mt_ok = K.sem("m_modT_ok")
        mrow_ok = K.sem("m_rows_ok")
        out_ok = K.sem("m_rows_stored")

        with nc.Block() as block:
            @block.sync
            def _(sp):
                for name, row, n, src in (
                        ("mu_prev", V_MUP, 12, 0), ("mu_next", V_MUN, 12, 0), ("w0", V_W0, 8, 0),
                        ("a0", V_A0, 8, 0), ("k_k", V_KK, 4, 0), ("k_a", V_KA, 4, 0), ("r_k", V_RK, 4, 0),
                        ("gn_g", V_GG, 4, 0), ("gn_b", V_GB, 4, 0), ("mu_prev", V_MUPL, 2, 12),
                        ("mu_next", V_MUNL, 2, 12), ("c", V_C, 8, 0), ("c_ctx", V_C + 8, 8, 0),
                        ("norm1_g", V_G1, 8, 0)):
                    sp.dma_start(vrows[row:row + n, :], rows_view(A[name], n, src)).then_inc(rows_in, 16)
                sp.dma_start(brows[:, :], rows_view(A["b_mod"], 48)).then_inc(rows_in, 16)
                wv = A["w_mod"].rearrange("l (k p) n -> p (l k) n", p=P)
                for c in range(NCH):
                    if c >= 3:
                        sp.wait_ge(mm_ok, c - 2)
                    sp.dma_start(wbuf[c % 3][:, :, :], wv[:, :, c * CH:(c + 1) * CH]).then_inc(w_in[c % 3], 16)
                sp.wait_ge(mrow_ok, 1)
                sp.dma_start(rows_view(K.dram["mod_rows"], 96), mrows[:, :]).then_inc(out_ok, 16)
                sp.wait_ge(out_ok, 16)

            @block.gpsimd
            def _(pool):
                link = Link(pool, g_chain)
                pool.memset(K.zero[:, :], 0.0)
                for col, value in ((0, EPS), (1, KK_EPS), (2, GN_EPS)):
                    pool.memset(K.eps[:, col:col + 1], value)
                link(pool.memset(K.ident[:, :], 0.0))
                link(pool.affine_select(out=K.ident[:, :], in_=K.ident[:, :], compare_op=ALU.not_equal, fill=1.0,
                                        base=0, pattern=[[-1, P]], channel_multiplier=1))
                pool.memset(K.head_ones[:, :], 0.0)
                pool.memset(K.head_mask[:, :], 0.0)
                link(pool.memset(low[:, :, :], 1.0))
                for h in range(2):
                    link(pool.memset(K.head_ones[h * HN:(h + 1) * HN, h * HN:(h + 1) * HN], 1.0))
                    link(pool.memset(K.head_mask[h * HN:(h + 1) * HN, h * HN:(h + 1) * HN], 1.0))
                link(pool.affine_select(out=low[:, 0, :], in_=low[:, 0, :], compare_op=ALU.is_gt, fill=0.0,
                                        base=0, pattern=[[-1, P]], channel_multiplier=1))
                link(pool.affine_select(out=low[:, 1, :], in_=low[:, 1, :], compare_op=ALU.is_gt, fill=0.0,
                                        base=0, pattern=[[1, P]], channel_multiplier=-1))
                link(pool.memset(K.causal[:, :, :, :], 1.0))
                for d, sign in ((0, 1), (1, -1)):
                    for q in range(4):
                        v = K.causal[:, d, q, :]
                        pool.affine_select(out=v, in_=v, compare_op=ALU.is_ge if q % 2 else ALU.is_gt, fill=0.0,
                                           base=0, pattern=[[sign, P]], channel_multiplier=-sign)
                pool.memset(K.scan_keep[:, :], 1.0)
                link(pool.iota(rowi[:, :], [[0, P]], base=0, channel_multiplier=1))
                pool.memset(K.scan_keep[:, :].rearrange("p (c t) -> p c t", t=P)[:, :, 0:1], 0.0)
                pool.iota(coli[:, :], [[1, P]], base=0, channel_multiplier=0).then_inc(consts, 1)

            @block.vector
            def _(dve):
                link = Link(dve, v_chain)
                dve.wait_ge(v_t, 1)
                nc.vector.tensor_copy(K.vecT[:, :], K.bank[0][:, 0:V_ROWS])
                link(nc.vector.tensor_copy(bmodT[:, :], K.bank[0][:, 128:176]))
                nc.vector.memset(cmp[:, :], 0.0).then_inc(vec_ok, 1)
                dve.wait_ge(sig_ok, 1)
                cv = K.vecT[:, V_C:V_C + 16].rearrange("p (s k) -> p k s", s=2)
                nc.vector.tensor_tensor(cond[:, :, :], cv, sig[:, :].rearrange("p (s k) -> p k s", s=2),
                                        ALU.mult).then_inc(cond_ok, 1)
                dve.wait_ge(consts, 1)
                link(nc.vector.tensor_tensor(xori[:, :], rowi[:, :], coli[:, :], ALU.bitwise_xor))
                link(nc.vector.tensor_copy(xorf[:, :], xori[:, :]))
                for lev in range(7):
                    link(nc.vector.tensor_scalar(cmp[:, :], xorf[:, :], float(2 ** (lev + 1)), None, ALU.is_lt))
                    link(nc.vector.scalar_tensor_tensor(cmp[:, :], xorf[:, :], float(2 ** lev), cmp[:, :],
                                                        ALU.is_ge, ALU.mult))
                    for d in range(2):
                        link(nc.vector.tensor_tensor(K.level[:, d, lev, :], cmp[:, :], low[:, d, :], ALU.mult))
                for c in range(NCH):
                    dve.wait_ge(mm_ok, c + 1)
                    b = bmodT[:, c * 8:(c + 1) * 8].unsqueeze(2).broadcast_to([P, 8, 2])
                    link(nc.vector.tensor_tensor(K.modT[:, c * 8:(c + 1) * 8, :],
                                                 K.bank[2 + c % 2][:, 0:16].rearrange("p (b s) -> p b s", s=2),
                                                 b, ALU.add))
                g = K.vecT[:, V_G1:V_G1 + 8].unsqueeze(2).broadcast_to([P, 8, 2])
                link(nc.vector.tensor_scalar(K.s1[:, :, :], K.modT[:, SC1 * 8:SC1 * 8 + 8, :], 1.0, None, ALU.add))
                link(nc.vector.tensor_tensor(K.s1[:, :, :], K.s1[:, :, :], g, ALU.mult))
                nc.vector.memset(cmp[:, :], 0.0).then_inc(mod_ok, 1)
                dve.wait_ge(mt_ok, 1)
                nc.vector.tensor_copy(mrows[:, :], K.bank[1][0:96, 0:P]).then_inc(mrow_ok, 1)

            @block.scalar
            def _(act):
                act.wait_ge(vec_ok, 1)
                nc.scalar.activation(sig[:, :], K.vecT[:, V_C:V_C + 16], ACT.Sigmoid).then_inc(sig_ok, 1)

            @block.tensor
            def _(pe):
                pe.wait_ge(rows_in, 16 * 15)
                pe.wait_ge(g_chain, 2)
                nc.tensor.transpose(K.bank[0][:, 0:V_ROWS], vrows[:, :], K.ident[0:V_ROWS, 0:V_ROWS])
                nc.tensor.transpose(K.bank[0][:, 128:176], brows[:, :], K.ident[0:48, 0:48]).then_inc(v_t, 1)
                pe.wait_ge(cond_ok, 1)
                for c in range(NCH):
                    pe.wait_ge(w_in[c % 3], 16 * (c // 3 + 1))
                    if c >= 2:
                        pe.wait_ge(v_chain, 31 + c - 1)
                    for b in range(8):
                        for k in range(KD):
                            last = nc.tensor.matmul(K.bank[2 + c % 2][:, 2 * b:2 * b + 2],
                                                    wbuf[c % 3][:, k, b * P:(b + 1) * P], cond[:, k, :],
                                                    start=(k == 0), stop=(k == KD - 1))
                    last.then_inc(mm_ok, 1)
                pe.wait_ge(mod_ok, 1)
                nc.tensor.transpose(K.bank[1][0:96, 0:P], K.modT[:, :, :].rearrange("p b s -> p (b s)"),
                                    K.ident[:, :]).then_inc(mt_ok, 1)


def norm1(K, A):
    nc = K.nc
    ctx = ExitStack()
    with ctx:
        xt = [K.sb(f"n1_x{i}", [P, D], ctx=ctx) for i in range(3)]
        xn = [K.sb(f"n1_xn{i}", [P, D], ctx=ctx) for i in range(2)]
        junk = K.sb("n1_junk", [P, D], ctx=ctx)
        ss = K.sb("n1_ss", [P, 3, TILES], ctx=ctx)
        x_in = [K.sem(f"n1_x_in{i}") for i in range(3)]
        sq_ok = K.sem("n1_sumsq")
        ms_ok = K.sem("n1_meansq")
        rt_ok = K.sem("n1_root")
        rc_ok = K.sem("n1_recip")
        xn_ok = K.sem("n1_xn_ok")
        t_ok = K.sem("n1_transposed")
        d_ok = K.sem("n1_dve_half")
        a_ok = K.sem("n1_act_half")
        with nc.Block() as block:
            @block.sync
            def _(sp):
                for i in range(TILES):
                    if i >= 3:
                        sp.wait_ge(xn_ok, i - 2)
                    src = A["x_sample"][0, i * P:(i + 1) * P, :] if i < 8 else A["x_prompt"][0, :, :]
                    sp.dma_start(xt[i % 3][:, :], src).then_inc(x_in[i % 3], 16)

            @block.scalar
            def _(act):
                def squares(i):
                    act.wait_ge(x_in[i % 3], 16 * (i // 3 + 1))
                    nc.scalar.activation(junk[:, :], xt[i % 3][:, :], ACT.Square,
                                         accum_out=ss[:, 0, i:i + 1]).then_inc(sq_ok, 1)
                    act.wait_ge(ms_ok, i + 1)
                    nc.scalar.activation(ss[:, 1, i:i + 1], ss[:, 2, i:i + 1], ACT.Sqrt).then_inc(rt_ok, 1)
                squares(0)
                for i in range(TILES):
                    if i + 1 < TILES:
                        squares(i + 1)
                    s = 0 if i < 8 else 1
                    act.wait_ge(t_ok, 2 * i + 2)
                    for k in range(4, 8):
                        last = nc.scalar.activation(K.hT[:, k, i * P:(i + 1) * P],
                                                    K.bank[4 + i % 4][:, (k - 4) * P:(k - 3) * P], ACT.Identity,
                                                    scale=K.s1[:, k, s:s + 1], bias=K.modT[:, SH1 * 8 + k, s:s + 1])
                    last.then_inc(a_ok, 1)

            @block.vector
            def _(dve):
                def normalise(i):
                    dve.wait_ge(sq_ok, i + 1)
                    nc.vector.tensor_scalar(ss[:, 2, i:i + 1], ss[:, 0, i:i + 1], 1.0 / D, EPS, ALU.mult,
                                            ALU.add).then_inc(ms_ok, 1)
                    dve.wait_ge(rt_ok, i + 1)
                    nc.vector.reciprocal(ss[:, 0, i:i + 1], ss[:, 1, i:i + 1]).then_inc(rc_ok, 1)
                    dve.wait_ge(rc_ok, i + 1)
                    if i >= 2:
                        dve.wait_ge(t_ok, 2 * (i - 1))
                    nc.vector.tensor_scalar(xn[i % 2][:, :], xt[i % 3][:, :], ss[:, 0, i:i + 1], None,
                                            ALU.mult).then_inc(xn_ok, 1)
                normalise(0)
                for i in range(TILES):
                    if i + 1 < TILES:
                        normalise(i + 1)
                    s = 0 if i < 8 else 1
                    dve.wait_ge(t_ok, 2 * i + 1)
                    for k in range(4):
                        last = nc.vector.tensor_scalar(K.hT[:, k, i * P:(i + 1) * P],
                                                       K.bank[i % 4][:, k * P:(k + 1) * P],
                                                       K.s1[:, k, s:s + 1], K.modT[:, SH1 * 8 + k, s:s + 1],
                                                       ALU.mult, ALU.add)
                    last.then_inc(d_ok, 1)

            @block.tensor
            def _(pe):
                for i in range(TILES):
                    pe.wait_ge(xn_ok, i + 1)
                    if i >= 4:
                        pe.wait_ge(d_ok, i - 3)
                        pe.wait_ge(a_ok, i - 3)
                    for k in range(KD):
                        last = nc.tensor.transpose(K.bank[(0 if k < 4 else 4) + i % 4][:, (k % 4) * P:(k % 4 + 1) * P],
                                                   xn[i % 2][:, k * P:(k + 1) * P], K.ident[:, :])
                        if k % 4 == 3:
                            last.then_inc(t_ok, 1)


def rwkv(K, A):
    nc = K.nc
    ctx = ExitStack()
    PW = NT + 3
    SAMPLE, PROMPT = 1, NS + 2
    LV = 6
    GR = TILES
    BLK = 3 * PAIRS
    with ctx:
        def sb(name, shape, dt=F32):
            return K.sb("r_" + name, shape, dt, ctx=ctx)

        wblk = [sb(f"w{i}", [P, KD, P]) for i in range(2)]
        lora = sb("lora", [P, NT])
        sigg = sb("sigg", [P, NT])
        wup = [sb(f"wup{d}", [P, P]) for d in range(2)]
        gup = sb("gup", [P, P])
        pv = sb("pairvec", [P, 15])
        pc = sb("pairconst", [P, 4])
        lc = sb("loraconst", [P, 2])
        raw = sb("raw", [P, PW])
        r, k, v, kk, kds, t0, t1, sig, aa = (sb(n, [P, NT]) for n in
                                             ("r", "k", "v", "kk", "kds", "t0", "t1", "sig", "aa"))
        R, Q, B, KB = ([sb(f"{n}{d}", [P, NT]) for d in range(2)] for n in "RQBK")
        mid = sb("mid", [P, 2, 2, TILES])
        e1 = sb("e1", [P, 2, TILES])
        e12 = sb("e12", [P, 2, TILES])
        tok = [sb(f"tok{d}", [P, 4, P]) for d in range(2)]
        M = [[sb(f"M{d}{h}", [P, 4, P]) for h in range(2)] for d in range(2)]
        T = [sb(f"T{d}", [P, 2, P]) for d in range(2)]
        W = [sb(f"W{d}", [P, 2, P]) for d in range(2)]
        X = [sb(f"X{d}", [P, 2, P]) for d in range(2)]
        XT = [sb(f"XT{d}", [P, P]) for d in range(2)]
        PV = [sb(f"PV{d}", [P, P]) for d in range(2)]
        U = [sb(f"U{d}", [P, P]) for d in range(2)]
        S = [sb(f"S{d}", [P, P]) for d in range(2)]
        ST = [sb(f"ST{d}", [P, P]) for d in range(2)]
        bank = K.bank

        def sem(name):
            return K.sem("r_" + name)

        w_in = [sem(f"w_in{i}") for i in range(2)]
        up_in, st_in = sem("up_in"), sem("state_in")
        proj = sem("projected")
        rawd = sem("raw_copied")
        shifted = sem("shifted")
        lora_ok = sem("lora_ok")
        v_chain = sem("dve_chain")
        sq_ok, norm_ps, norm_ok, norm_used = sem("ksq_ok"), sem("norm_psum"), sem("norm_ok"), sem("norm_used")
        gate_ps, gate_ok = sem("gate_psum"), sem("gate_ok")
        bonus_in, bonus_ps, y_sum = sem("bonus_in"), sem("bonus_psum"), sem("y_sum")
        mean_ps, centred, sqd = sem("mean_psum"), sem("centred"), sem("y_squared")
        var_ps, root_ok, prep_ok, pair_ok = sem("var_psum"), sem("root_ok"), sem("prep_ok"), sem("pair_ok")
        wg_ps, ag_ps, wg_ok, ag_ok = sem("wgate_psum"), sem("agate_psum"), sem("wgate_ok"), sem("agate_ok")
        exps_in, exps_ok, gates_used = sem("exps_in"), sem("exps_ok"), sem("gates_used")
        st_t = sem("state_transposed")
        st_out, st_st = sem("state_out"), sem("state_stored")
        tr, tr_ok = sem("tokmajor_psum"), sem("tokmajor_ok")
        mm, mm_ok, w0_ok = sem("M_psum"), sem("M_ok"), sem("W0_ok")
        xt, xt_ok, pps, p_ok = sem("XT_psum"), sem("XT_ok"), sem("PV_psum"), sem("PV_ok")
        ups, u_ok, ops, o_ok = sem("U_psum"), sem("U_ok"), sem("Y_psum"), sem("Y_ok")
        sps, s_ok = sem("S_psum"), sem("S_ok")
        tps, tt_ok = sem("T_psum"), sem("T_copied")
        xps, x_ok, yps, y_ok = sem("X_psum"), sem("X_ok"), sem("TX_psum"), sem("TX_ok")
        VL = 76
        w_in_v = A["w_in"].rearrange("l (k p) n -> p (l k) n", p=P)
        NG = 2 * (GR + 1)

        def chunk_of(d, g):
            return g if g == 8 or d == 0 else 7 - g

        with nc.Block() as block:
            @block.sync
            def _(sp):
                for i in range(2):
                    c = (BLK + i) * P
                    sp.dma_start(wblk[i][:, :, :], w_in_v[:, :, c:c + P]).then_inc(w_in[i], 16)
                with sp.Fori(0, PAIRS) as p:
                    for i in range(3):
                        sp.wait_ge(proj, p * 3 + (3 if i == 2 else 2))
                        sp.dma_start(wblk[i % 2][:, :, :],
                                     w_in_v[:, :, bass.ds(p * P + i * DA, P)]).then_inc(w_in[i % 2], 16)
                    sp.wait_ge(pair_ok, p + 1)
                    for d in range(2):
                        sp.dma_start(wup[d][0:HN, :], A["w_up"][0, d, :, bass.ds(p * P, P)]).then_inc(up_in, 16)
                        sp.dma_start(wup[d][HN:P, :], A["a_up"][0, d, :, bass.ds(p * P, P)]).then_inc(up_in, 16)
                    sp.dma_start(gup[:, :], A["g_up"][0, :, bass.ds(p * P, P)]).then_inc(up_in, 16)
                    for d in range(2):
                        for h in range(2):
                            sp.dma_start(ST[d][h * HN:(h + 1) * HN, h * HN:(h + 1) * HN],
                                         A["state_rwkv"][0, 0, d, bass.ds(p * 2 + h, 1), :, :]
                                         .rearrange("a v k -> (a v) k")).then_inc(st_in, 16)
                    sp.wait_ge(st_out, p * 2 + 2)
                    for d in range(2):
                        for h in range(2):
                            sp.dma_start(A["new_s"][0, 0, d, bass.ds(p * 2 + h, 1), :, :]
                                         .rearrange("a v k -> (a v) k"),
                                         ST[d][h * HN:(h + 1) * HN, h * HN:(h + 1) * HN]).then_inc(st_st, 16)
                    K.hold(sp, st_st, p * 64 + 64)

            @block.tensor
            def _(pe):
                def project(buf, first):
                    for c, (at, n) in enumerate(PIECES):
                        for kc in range(KD):
                            last = nc.tensor.matmul(bank[first + c][:, 0:n], wblk[buf][:, kc, :],
                                                    K.hT[:, kc, at:at + n], start=(kc == 0), stop=(kc == KD - 1))
                    last.then_inc(proj, 1)

                def full(lhsT, rhs, first):
                    for c, (at, n) in enumerate(PIECES):
                        last = nc.tensor.matmul(bank[first + c][:, 0:n], lhsT, rhs[:, at:at + n],
                                                start=True, stop=True)
                    return last

                for i in range(2):
                    pe.wait_ge(w_in[i], 16)
                    project(i, 3 * i)
                with pe.Fori(0, PAIRS) as p:
                    pe.wait_ge(pair_ok, p + 1)
                    pe.wait_ge(rawd, p * 3 + 2)
                    pe.wait_ge(w_in[0], p * 32 + 32)
                    project(0, 0)
                    pe.wait_ge(w_in[1], p * 16 + 32)
                    project(1, 3)
                    pe.wait_ge(rawd, p * 3 + 3)
                    pe.wait_ge(w_in[0], p * 32 + 48)
                    project(0, 0)
                    pe.wait_ge(rawd, p * 3 + 4)
                    pe.wait_ge(sq_ok, p + 1)
                    full(K.head_ones[:, :], t0, 3).then_inc(norm_ps, 1)
                    pe.wait_ge(lora_ok, 2)
                    pe.wait_ge(up_in, p * 80 + 80)
                    pe.wait_ge(rawd, p * 3 + 5)
                    for d in range(2):
                        if d:
                            pe.wait_ge(wg_ok, p * 2 + 1)
                        full(wup[d][0:HN, :], lora[0:HN, :], 0).then_inc(wg_ps, 1)
                        if d:
                            pe.wait_ge(ag_ok, p * 2 + 1)
                        else:
                            pe.wait_ge(norm_ok, p + 1)
                        full(wup[d][HN:P, :], lora[HN:P, :], 3).then_inc(ag_ps, 1)
                    pe.wait_ge(st_in, p * 64 + 64)
                    for d in range(2):
                        last = nc.tensor.transpose(bank[6][:, d * P:(d + 1) * P], ST[d][:, :], K.ident[:, :])
                    last.then_inc(st_t, 1)
                    pe.wait_ge(prep_ok, p + 1)
                    pe.wait_ge(s_ok, p * NG + 2)
                    for g in range(GR):
                        def gv(per, i, g=g):
                            return p * (GR * per) + (g * per + i)
                        for d in range(2):
                            at = chunk_of(d, g) * P
                            for q, src in enumerate((Q[d], B[d], KB[d], v)):
                                last = nc.tensor.transpose(bank[6 + d][:, q * P:(q + 1) * P], src[:, at:at + P],
                                                           K.ident[:, :])
                            last.then_inc(tr, 1)
                        if g:
                            pe.wait_ge(o_ok, gv(2, 0))
                        for d in range(2):
                            at = chunk_of(d, g) * P
                            for h in range(2):
                                hs = slice(h * HN, (h + 1) * HN)
                                for q, (a, b) in enumerate(((B, Q), (B, R), (KB, Q), (KB, R))):
                                    last = nc.tensor.matmul(bank[2 * d + h][:, q * P:(q + 1) * P],
                                                            a[d][hs, at:at + P], b[d][hs, at:at + P],
                                                            start=True, stop=True)
                                last.then_inc(mm, 1)
                        pe.wait_ge(s_ok, p * NG + (2 * g + 2))
                        for lev in range(1, LV + 1):
                            for d in range(2):
                                if lev == 1:
                                    pe.wait_ge(w0_ok, gv(2, d + 1))
                                    src = W[d]
                                else:
                                    pe.wait_ge(y_ok, gv(2 * LV, 2 * (lev - 2) + d + 1))
                                    src = T[d]
                                for h in range(2):
                                    last = nc.tensor.transpose(bank[4 + d][:, h * P:(h + 1) * P], src[:, h, :],
                                                               K.ident[:, :])
                                last.then_inc(tps, 1)
                                if lev > 1:
                                    for h in range(2):
                                        last = nc.tensor.matmul(bank[d][:, h * P:(h + 1) * P], M[d][h][:, 0, :],
                                                                T[d][:, h, :], start=True, stop=True)
                                    last.then_inc(xps, 1)
                            if lev == 1:
                                for d in range(2):
                                    pe.wait_ge(tt_ok, gv(2 * LV, d + 1))
                                    for h in range(2):
                                        last = nc.tensor.matmul(bank[d][:, h * P:(h + 1) * P], M[d][h][:, 0, :],
                                                                T[d][:, h, :], start=True, stop=True)
                                    last.then_inc(xps, 1)
                                pe.wait_ge(mm_ok, gv(4, 4))
                            for d in range(2):
                                pe.wait_ge(x_ok, gv(2 * LV, 2 * (lev - 1) + d + 1))
                                pe.wait_ge(tt_ok, gv(2 * LV, 2 * (lev - 1) + d + 1))
                                for h in range(2):
                                    lt, rt = (W[d], X[d]) if lev < LV else (X[d], W[d])
                                    last = nc.tensor.matmul(bank[2 + d][:, h * P:(h + 1) * P], lt[:, h, :],
                                                            rt[:, h, :], start=True, stop=True)
                                last.then_inc(yps, 1)
                        pe.wait_ge(tr_ok, gv(2, 2))
                        for d in range(2):
                            for h in range(2):
                                hs = slice(h * HN, (h + 1) * HN)
                                last = nc.tensor.matmul(bank[7][:, d * P + h * HN:d * P + (h + 1) * HN],
                                                        M[d][h][:, 2, :], tok[d][:, 3, hs], start=True, stop=True)
                            last.then_inc(pps, 1)
                        for d in range(2):
                            pe.wait_ge(y_ok, gv(2 * LV, 2 * (LV - 1) + d + 1))
                            for h in range(2):
                                hs = slice(h * HN, (h + 1) * HN)
                                last = nc.tensor.matmul(bank[6][hs, d * P:(d + 1) * P], tok[d][:, 0, hs],
                                                        W[d][:, h, :], start=True, stop=True)
                            last.then_inc(xt, 1)
                        for d in range(2):
                            pe.wait_ge(s_ok, p * NG + (2 * g + d + 1))
                            pe.wait_ge(xt_ok, gv(2, d + 1))
                            pe.wait_ge(p_ok, gv(2, d + 1))
                            nc.tensor.matmul(bank[d][:, 0:P], XT[d][:, :], S[d][:, :], start=True, stop=False)
                            for h in range(2):
                                hs = slice(h * HN, (h + 1) * HN)
                                last = nc.tensor.matmul(bank[d][:, hs], W[d][:, h, :], PV[d][:, hs],
                                                        start=False, stop=(h == 1))
                            last.then_inc(ups, 1)
                        for d in range(2):
                            at = chunk_of(d, g) * P
                            nc.tensor.matmul(bank[2 + d][:, 0:P], S[d][:, :], R[d][:, at:at + P],
                                             start=True, stop=False)
                            for h in range(2):
                                hs = slice(h * HN, (h + 1) * HN)
                                nc.tensor.matmul(bank[2 + d][hs, 0:P], tok[d][:, 3, hs], M[d][h][:, 3, :],
                                                 start=False, stop=False)
                            pe.wait_ge(u_ok, gv(2, d + 1))
                            for h in range(2):
                                hs = slice(h * HN, (h + 1) * HN)
                                last = nc.tensor.matmul(bank[2 + d][hs, 0:P], U[d][:, hs], M[d][h][:, 1, :],
                                                        start=False, stop=True)
                            last.then_inc(ops, 1)
                            nc.tensor.matmul(bank[4 + d][:, 0:P], tok[d][:, 1, :], U[d][:, :],
                                             start=True, stop=False)
                            nc.tensor.matmul(bank[4 + d][:, 0:P], tok[d][:, 2, :], tok[d][:, 3, :],
                                             start=False, stop=True).then_inc(sps, 1)
                    pe.wait_ge(s_ok, p * NG + NG)
                    for d in range(2):
                        last = nc.tensor.transpose(bank[6][:, d * P:(d + 1) * P], S[d][:, :], K.ident[:, :])
                    last.then_inc(st_t, 1)
                    pe.wait_ge(o_ok, p * (2 * GR) + 2 * GR)
                    full(gup[:, :], sigg, 0).then_inc(gate_ps, 1)
                    pe.wait_ge(bonus_in, p + 1)
                    full(K.head_ones[:, :], aa, 3).then_inc(bonus_ps, 1)
                    pe.wait_ge(y_sum, p + 1)
                    pe.wait_ge(gate_ok, p + 1)
                    full(K.head_ones[:, :], t0, 0).then_inc(mean_ps, 1)
                    pe.wait_ge(sqd, p + 1)
                    full(K.head_ones[:, :], t1, 3).then_inc(var_ps, 1)

            @block.scalar
            def _(act):
                def copy_raw(first):
                    for c, (at, m) in enumerate(PIECES):
                        dst = at + SAMPLE if at < NS else PROMPT
                        last = nc.scalar.activation(raw[:, dst:dst + m], bank[first + c][:, 0:m], ACT.Copy)
                    last.then_inc(rawd, 1)

                def full(out, first, func, **kw):
                    for c, (at, m) in enumerate(PIECES):
                        last = nc.scalar.activation(out[:, at:at + m], bank[first + c][:, 0:m], func, **kw)
                    return last

                def flat(ap):
                    return ap.rearrange("p a b -> p (a b)")

                act.wait_ge(shifted, 1)
                act.wait_ge(proj, 1)
                copy_raw(0)
                act.wait_ge(shifted, 2)
                nc.scalar.activation(lora[0:HN, :], lora[0:HN, :], ACT.Tanh).then_inc(lora_ok, 1)
                act.wait_ge(proj, 2)
                copy_raw(3)
                act.wait_ge(shifted, 3)
                nc.scalar.activation(sigg[:, :], sigg[:, :], ACT.Sigmoid).then_inc(lora_ok, 1)
                with act.Fori(0, PAIRS) as p:
                    for i in range(3):
                        act.wait_ge(proj, p * 3 + (3 + i))
                        act.wait_ge(shifted, p * 3 + (3 + i))
                        copy_raw(3 if i == 1 else 0)
                    act.wait_ge(norm_ps, p + 1)
                    full(sig, 3, ACT.Sqrt, bias=K.eps[:, 1:2]).then_inc(norm_ok, 1)
                    act.wait_ge(norm_used, p + 1)
                    for d in range(2):
                        if d:
                            act.wait_ge(gates_used, p * 2 + 1)
                        act.wait_ge(wg_ps, p * 2 + (d + 1))
                        full(sig, 0, ACT.Sigmoid, bias=pv[:, 6 + d:7 + d]).then_inc(wg_ok, 1)
                        act.wait_ge(ag_ps, p * 2 + (d + 1))
                        full(aa, 3, ACT.Sigmoid, bias=pv[:, 8 + d:9 + d]).then_inc(ag_ok, 1)
                        act.wait_ge(exps_in, p * 2 + (d + 1))
                        nc.scalar.activation(R[d][:, :], t0[:, :], ACT.Exp, scale=-DECAY)
                        nc.scalar.activation(Q[d][:, :], t1[:, :], ACT.Exp, scale=-DECAY)
                        nc.scalar.activation(B[d][:, :], t0[:, :], ACT.Exp, scale=DECAY)
                        nc.scalar.activation(e1[:, d, :], mid[:, d, 0, :], ACT.Exp, scale=-DECAY)
                        nc.scalar.activation(e12[:, d, :], mid[:, d, 1, :], ACT.Exp,
                                             scale=-DECAY).then_inc(exps_ok, 1)
                    for g in range(GR):
                        def gv(per, i, g=g):
                            return p * (GR * per) + (g * per + i)
                        for d in range(2):
                            act.wait_ge(tr, gv(2, d + 1))
                            nc.scalar.activation(flat(tok[d][:, :, :]), bank[6 + d][:, :], ACT.Copy).then_inc(tr_ok, 1)
                        for lev in range(1, LV + 1):
                            for d in range(2):
                                act.wait_ge(tps, gv(2 * LV, 2 * (lev - 1) + d + 1))
                                dst = T[d] if lev == 1 else W[d]
                                nc.scalar.activation(flat(dst[:, :, :]), bank[4 + d][:, 0:2 * P],
                                                     ACT.Copy).then_inc(tt_ok, 1)
                        act.wait_ge(xt, gv(2, 2))
                        for d in range(2):
                            nc.scalar.activation(XT[d][:, :], bank[6][:, d * P:(d + 1) * P],
                                                 ACT.Copy).then_inc(xt_ok, 1)
                        for d in range(2):
                            act.wait_ge(ops, gv(2, d + 1))
                            at = chunk_of(d, g) * P
                            nc.scalar.activation((t0, t1)[d][:, at:at + P], bank[2 + d][:, 0:P],
                                                 ACT.Copy).then_inc(o_ok, 1)
                    act.wait_ge(gate_ps, p + 1)
                    full(sig, 0, ACT.Copy).then_inc(gate_ok, 1)
                    act.wait_ge(centred, p + 1)
                    nc.scalar.activation(t1[:, :], t0[:, :], ACT.Square).then_inc(sqd, 1)
                    act.wait_ge(var_ps, p + 1)
                    full(kk, 3, ACT.Sqrt, bias=K.eps[:, 2:3], scale=1.0 / HN).then_inc(root_ok, 1)

            @block.vector
            def _(dve):
                link = Link(dve, v_chain)
                V = nc.vector
                V.memset(raw[:, :], 0.0).then_inc(shifted, 1)
                V.memset(ST[0][:, :], 0.0)
                V.memset(ST[1][:, :], 0.0).then_inc(pair_ok, 1)
                link(V.tensor_tensor(lc[:, :], K.vecT[:, V_MUPL:V_MUPL + 2], K.vecT[:, V_MUNL:V_MUNL + 2], ALU.add))
                link(V.tensor_scalar(lc[:, :], lc[:, :], -1.0, 1.0, ALU.mult, ALU.add))

                def shift(out, c0, mp, mn):
                    for s, at, n in ((SAMPLE, 0, NS), (PROMPT, NS, NP)):
                        last = V.tensor_scalar(out[:, at:at + n], raw[:, s:s + n], c0, None, ALU.mult)
                    link(last)
                    for s, at, n in ((SAMPLE, 0, NS), (PROMPT, NS, NP)):
                        last = V.scalar_tensor_tensor(out[:, at:at + n], raw[:, s - 1:s - 1 + n], mp,
                                                      out[:, at:at + n], ALU.mult, ALU.add)
                    link(last)
                    for s, at, n in ((SAMPLE, 0, NS), (PROMPT, NS, NP)):
                        last = V.scalar_tensor_tensor(out[:, at:at + n], raw[:, s + 1:s + 1 + n], mn,
                                                      out[:, at:at + n], ALU.mult, ALU.add)
                    last.then_inc(shifted, 1)

                for i, out in enumerate((lora, sigg)):
                    dve.wait_ge(rawd, i + 1)
                    shift(out, lc[:, i:i + 1], K.vecT[:, V_MUPL + i:V_MUPL + i + 1],
                          K.vecT[:, V_MUNL + i:V_MUNL + i + 1])
                tot = lambda ap, at: ap[:, :].rearrange("p (c t) -> p c t", t=P)[:, :, at:at + 1]
                wide = lambda ap: ap[:, :].rearrange("p (c t) -> p c t", t=P)
                with dve.Fori(0, PAIRS) as p:
                    link.enter(p, VL)
                    link(V.tensor_copy(pv[:, :], K.vecT[:, 0:60].rearrange("p (v q) -> p v q", q=PAIRS)
                                       [:, :, bass.ds(p, 1)].rearrange("p v q -> p (v q)")))
                    link(V.tensor_tensor(pc[:, 0:3], pv[:, 0:3], pv[:, 3:6], ALU.add))
                    link(V.tensor_scalar(pc[:, 0:3], pc[:, 0:3], -1.0, 1.0, ALU.mult, ALU.add))
                    link(V.tensor_scalar(pc[:, 3:4], pv[:, 11:12], -1.0, 1.0, ALU.mult, ALU.add))
                    for i, out in enumerate((r, k, v)):
                        dve.wait_ge(rawd, p * 3 + (3 + i))
                        shift(out, pc[:, i:i + 1], pv[:, i:i + 1], pv[:, 3 + i:4 + i])
                        dve.wait_ge(shifted, p * 3 + (4 + i))
                        if i == 1:
                            link(V.tensor_scalar(kk[:, :], k[:, :], pv[:, 10:11], None, ALU.mult))
                            V.tensor_tensor(t0[:, :], kk[:, :], kk[:, :], ALU.mult).then_inc(sq_ok, 1)
                    dve.wait_ge(norm_ok, p + 1)
                    V.reciprocal(t1[:, :], sig[:, :]).then_inc(norm_used, 1)
                    dve.wait_ge(norm_used, p + 1)
                    link(V.tensor_tensor(kk[:, :], kk[:, :], t1[:, :], ALU.mult))
                    for d in range(2):
                        dve.wait_ge(wg_ok, p * 2 + (d + 1))
                        link(V.tensor_tensor_scan(t0[:, :], K.scan_keep[:, :], sig[:, :], 0.0, ALU.mult, ALU.add))
                        if d:
                            link(V.tensor_tensor(t1[:, :], sig[:, :], t0[:, :], ALU.subtract))
                            link(V.tensor_tensor(wide(t1), wide(t1), tot(t0, P - 1).broadcast_to([P, TILES, P]), ALU.add))
                            cs, mi, to = t1, P // 2, 0
                        else:
                            cs, mi, to = t0, P // 2 - 1, P - 1
                        V.tensor_copy(mid[:, d, 0, :].unsqueeze(2), tot(cs, mi))
                        link(V.tensor_tensor(mid[:, d, 1, :].unsqueeze(2), tot(cs, to), tot(cs, mi), ALU.subtract))
                        if d == 0:
                            link(V.tensor_tensor(mid[:, d, 1, 0:7], mid[:, d, 1, 0:7], mid[:, d, 0, 1:8], ALU.add))
                        else:
                            link(V.tensor_tensor(mid[:, d, 1, 1:8], mid[:, d, 1, 1:8], mid[:, d, 0, 0:7], ALU.add))
                        link(V.tensor_tensor(wide(t0), wide(cs), mid[:, d, 0, :].unsqueeze(2).broadcast_to([P, TILES, P]),
                                             ALU.subtract))
                        V.tensor_tensor(t1[:, :], t0[:, :], sig[:, :], ALU.subtract).then_inc(exps_in, 1)
                        dve.wait_ge(exps_ok, p * 2 + (d + 1))
                        link(V.tensor_tensor(KB[d][:, :], B[d][:, :], k[:, :], ALU.mult))
                        link(V.tensor_tensor(B[d][:, :], B[d][:, :], kk[:, :], ALU.mult))
                        link(V.tensor_tensor(B[d][:, :], B[d][:, :], aa[:, :], ALU.mult))
                        link(V.tensor_tensor(R[d][:, :], R[d][:, :], r[:, :], ALU.mult))
                        link(V.tensor_tensor(Q[d][:, :], Q[d][:, :], kk[:, :], ALU.mult))
                        link(V.tensor_scalar(aa[:, :], aa[:, :], pv[:, 11:12], pc[:, 3:4], ALU.mult, ALU.add))
                        link(V.tensor_tensor(KB[d][:, :], KB[d][:, :], aa[:, :], ALU.mult))
                        if d == 0:
                            V.tensor_copy(kds[:, :], aa[:, :]).then_inc(gates_used, 1)
                        else:
                            V.tensor_tensor(kds[:, :], kds[:, :], aa[:, :], ALU.add).then_inc(gates_used, 1)
                        dve.wait_ge(gates_used, p * 2 + (d + 1))
                    V.memset(pc[:, 0:1], 0.0).then_inc(prep_ok, 1)
                    dve.wait_ge(st_t, p * 2 + 1)
                    for d in range(2):
                        c = chunk_of(d, 0)
                        V.tensor_scalar(S[d][:, :], bank[6][:, d * P:(d + 1) * P], e1[:, d, c:c + 1], None,
                                        ALU.mult).then_inc(s_ok, 1)
                    for g in range(GR):
                        def gv(per, i, g=g):
                            return p * (GR * per) + (g * per + i)
                        for d in range(2):
                            for h in range(2):
                                dve.wait_ge(mm, gv(4, 2 * d + h + 1))
                                V.tensor_tensor(M[d][h][:, :, :], bank[2 * d + h][:, :].rearrange("p (q t) -> p q t", t=P),
                                                K.causal[:, d, :, :], ALU.mult).then_inc(mm_ok, 1)
                        for d in range(2):
                            dve.wait_ge(mm_ok, gv(4, 2 * d + 2))
                            for h in range(2):
                                last = V.scalar_tensor_tensor(W[d][:, h, :], M[d][h][:, 0, :], -1.0,
                                                              K.level[:, 1 - d, 0, :], ALU.mult, ALU.mult)
                            link(last)
                            V.tensor_tensor(W[d][:, :, :], W[d][:, :, :],
                                            K.ident[:, :].unsqueeze(1).broadcast_to([P, 2, P]), ALU.add).then_inc(w0_ok, 1)
                        for lev in range(1, LV + 1):
                            for d in range(2):
                                dve.wait_ge(xps, gv(2 * LV, 2 * (lev - 1) + d + 1))
                                V.tensor_tensor(X[d][:, :, :], bank[d][:, 0:2 * P].rearrange("p (h t) -> p h t", t=P),
                                                K.level[:, d, lev, :].unsqueeze(1).broadcast_to([P, 2, P]),
                                                ALU.mult).then_inc(x_ok, 1)
                            for d in range(2):
                                dve.wait_ge(yps, gv(2 * LV, 2 * (lev - 1) + d + 1))
                                dst = T[d] if lev < LV else W[d]
                                V.tensor_tensor(dst[:, :, :], dst[:, :, :],
                                                bank[2 + d][:, 0:2 * P].rearrange("p (h t) -> p h t", t=P),
                                                ALU.subtract).then_inc(y_ok, 1)
                        for d in range(2):
                            dve.wait_ge(pps, gv(2, 2))
                            V.tensor_copy(PV[d][:, :], bank[7][:, d * P:(d + 1) * P]).then_inc(p_ok, 1)
                        for d in range(2):
                            dve.wait_ge(ups, gv(2, d + 1))
                            V.tensor_scalar(U[d][:, :], bank[d][:, 0:P], -1.0, None, ALU.mult).then_inc(u_ok, 1)
                        for d in range(2):
                            c = chunk_of(d, g)
                            dve.wait_ge(sps, gv(2, d + 1))
                            if g == GR - 2:
                                V.memset(S[d][:, :], 0.0).then_inc(s_ok, 1)
                                continue
                            V.tensor_scalar(S[d][:, :], S[d][:, :], e12[:, d, c:c + 1], None, ALU.mult)
                            link(V.scalar_tensor_tensor(ST[d][:, :], bank[4 + d][:, 0:P], e12[:, d, c:c + 1],
                                                        K.head_mask[:, :], ALU.mult, ALU.mult))
                            V.tensor_tensor(S[d][:, :], S[d][:, :], ST[d][:, :], ALU.add).then_inc(s_ok, 1)
                    dve.wait_ge(st_t, p * 2 + 2)
                    for d in range(2):
                        V.tensor_copy(ST[d][:, :], bank[6][:, d * P:(d + 1) * P]).then_inc(st_out, 1)
                    link(V.tensor_tensor(kds[:, :], kds[:, :], k[:, :], ALU.mult))
                    V.scalar_tensor_tensor(aa[:, :], r[:, :], pv[:, 12:13], kds[:, :], ALU.mult,
                                           ALU.mult).then_inc(bonus_in, 1)
                    dve.wait_ge(bonus_ps, p + 1)
                    for c, (at, n) in enumerate(PIECES):
                        last = V.tensor_tensor(kds[:, at:at + n], v[:, at:at + n], bank[3 + c][:, 0:n], ALU.mult)
                    link(last)
                    dve.wait_ge(o_ok, p * (2 * GR) + 2 * GR)
                    V.tensor_tensor(t0[:, :], t0[:, :], t1[:, :], ALU.add).then_inc(y_sum, 1)
                    dve.wait_ge(mean_ps, p + 1)
                    for c, (at, n) in enumerate(PIECES):
                        last = V.scalar_tensor_tensor(t0[:, at:at + n], bank[c][:, 0:n], -1.0 / HN, t0[:, at:at + n],
                                                      ALU.mult, ALU.add)
                    last.then_inc(centred, 1)
                    dve.wait_ge(root_ok, p + 1)
                    link(V.reciprocal(t1[:, :], kk[:, :]))
                    link(V.tensor_tensor(t0[:, :], t0[:, :], t1[:, :], ALU.mult))
                    link(V.tensor_scalar(t0[:, :], t0[:, :], pv[:, 13:14], pv[:, 14:15], ALU.mult, ALU.add))
                    link(V.tensor_tensor(t0[:, :], t0[:, :], kds[:, :], ALU.add))
                    V.tensor_tensor(K.yA[:, bass.ds(p, 1), :].rearrange("p a t -> p (a t)"), t0[:, :], sig[:, :],
                                    ALU.mult).then_inc(pair_ok, 1)
                    link.leave(PAIRS)


def attention(K, A):
    nc = K.nc
    ctx = ExitStack()
    ROWS = NS // GRID
    SLOTS = 2 * WR
    TABW = P
    HD = HEADS * (2 * WR - 1)
    units = []
    for u in range(ROWS // 2):
        even, odd = (min(max(x - WR // 2, 0), ROWS - WR) for x in (2 * u, 2 * u + 1))
        nrows = odd + WR - even
        units.append((u, even, nrows, even - 2 * u + WR - 1))
    units.append((ROWS // 2, None, 0, 0))
    seq = [(u, h) for u in units for h in range(2)]
    NU = len(seq)
    with ctx:
        def sb(name, shape, dt=F32):
            return K.sb("t_" + name, shape, dt, ctx=ctx)

        def sem(name):
            return K.sem("t_" + name)

        wblk = [sb(f"w{i}", [P, KD, P]) for i in range(3)]
        q, k, v = (sb(n, [P, NT]) for n in "qkv")
        vtok = sb("vtok", [P, TILES, P])
        kout = sb("kout", [P, P])
        ckrow = sb("ckrow", [P, P])
        ck = sb("ck", [P, P])
        cv = sb("cv", [P, P])
        prow = sb("prow", [HD, TABW])
        tab = sb("tab", [P, 2, SLOTS, GRID])
        tab9 = sb("tab9", [P, 2, WR + 1, GRID])
        s = [sb(f"s{i}", [P, 704]) for i in range(2)]
        pr = [sb(f"p{i}", [P, 704]) for i in range(2)]
        pt = [sb(f"pt{i}", [P, 6, P]) for i in range(2)]
        st = sb("stats", [P, 3, NU])
        o = [sb(f"o{i}", [P, P]) for i in range(2)]
        bank = K.bank
        w_in = [sem(f"w_in{i}") for i in range(3)]
        c_in = sem("cache_in")
        rp_in, sp_ok, tab_in, tab_ok, tab_base = sem("rpb_in"), sem("spread_ok"), sem("tab_in"), sem("tab_ok"), sem("prow_ok")
        proj, t_ps, t_ok = sem("proj"), sem("tok_psum"), sem("tok_ok")
        q_ok, k_ok, v_ok = sem("q_ok"), sem("k_ok"), sem("v_ok")
        kv_st = sem("kv_stored")
        v_chain, g_chain = sem("dve_chain"), sem("pool_chain")
        s_ps, s_ok, m_ok, e_ok = sem("score_psum"), sem("score_ok"), sem("max_ok"), sem("exp_ok")
        r_ok, pt_ps, pta_ok, ptv_ok = sem("recip_ok"), sem("PT_psum"), sem("PT_act"), sem("PT_dve")
        o_ps, o_ok, ot_ps, ot_ok = sem("O_psum"), sem("O_ok"), sem("OT_psum"), sem("OT_ok")
        pair_ok = sem("pair_ok")
        w_in_v = A["w_in"].rearrange("l (k p) n -> p (l k) n", p=P)
        L = HD * TABW

        def table(u, h):
            _, even, nrows, slot = u
            if nrows == WR + 1:
                return tab9[:, h, :, :].rearrange("p r c -> p (r c)")
            return tab[:, h, slot:slot + WR, :].rearrange("p r c -> p (r c)")

        with nc.Block() as block:
            @block.sync
            def _(sp):
                sp.wait_ge(tab_base, 1)
                sp.dma_start(prow[:, 48:48 + 2 * WC - 1],
                             A["rpb"].rearrange("l h a b -> (l h a) b")).then_inc(rp_in, 16)
                sp.wait_ge(rp_in, 16)
                sp.dma_start(bass.AP(tensor=K.dram["spread"].tensor, offset=0, ap=[[TABW, HD], [L, GRID], [1, TABW]]),
                             prow[:, :].unsqueeze(1).broadcast_to([HD, GRID, TABW])).then_inc(sp_ok, 16)
                sp.wait_ge(sp_ok, 16)
                with sp.Fori(0, PAIRS) as p:
                    sp.wait_ge(proj, p * 3 + 1)
                    for i in range(3):
                        sp.dma_start(wblk[i][:, :, :], w_in_v[:, :, bass.ds(p * P + (ACOLS + i * DA), P)])\
                          .then_inc(w_in[i], 16)
                    K.hold(sp, pair_ok, p + 1)
                    sp.dma_start(ckrow[:, :], A["cache_na_k"].rearrange("a b t h n -> (a b t) (h n)")
                                 [:, bass.ds(p * P, P)]).then_inc(c_in, 16)
                    sp.dma_start(cv[:, :], A["cache_na_v"].rearrange("a b t h n -> (a b t) (h n)")
                                 [:, bass.ds(p * P, P)]).then_inc(c_in, 16)
                    sv = bass.AP(tensor=K.dram["spread"].tensor, offset=GRID - 1,
                                 ap=[[L - 1, GRID], [TABW, HD], [1, GRID]])
                    for h in range(2):
                        for half in range(2):
                            sp.dma_start(tab[half * GRID:(half + 1) * GRID, h, half:half + SLOTS - 1, :],
                                         sv[:, bass.ds(p * 2 * (SLOTS - 1) + h * (SLOTS - 1), SLOTS - 1), :])\
                              .then_inc(tab_in, 16)
                    sp.wait_ge(t_ok, p * 3 + 3)
                    sp.dma_start(A["new_v"].rearrange("a b t h n -> (a b t) (h n)")[:, bass.ds(p * P, P)],
                                 vtok[:, TILES - 1, :]).then_inc(kv_st, 16)
                    sp.dma_start(A["new_k"].rearrange("a b t h n -> (a b t) (h n)")[:, bass.ds(p * P, P)],
                                 kout[:, :]).then_inc(kv_st, 16)
                    K.hold(sp, kv_st, p * 32 + 32)

            @block.gpsimd
            def _(pool):
                link = Link(pool, g_chain, K)
                pool.memset(prow[:, :], 0.0).then_inc(tab_base, 1)
                with pool.Fori(0, PAIRS) as p:
                    link.enter(p, 9)
                    K.hold(pool, tab_in, p * 64 + 64)
                    for half in range(2):
                        rows = slice(half * GRID, (half + 1) * GRID)
                        at = (SLOTS - 1) * (1 - half)
                        link(pool.memset(tab[rows, :, at:at + 1, :], NEG))
                    for half in range(2):
                        t = tab[half * GRID:(half + 1) * GRID, :, :, :].rearrange("p h r c -> p (h r) c")
                        link(pool.affine_select(out=t[:, :, 0:GRID - WC], in_=t[:, :, 0:GRID - WC],
                                                  compare_op=ALU.is_ge, fill=NEG, base=WC // 2,
                                                  pattern=[[0, 2 * SLOTS], [1, GRID - WC]], channel_multiplier=-1))
                    for half in range(2):
                        t = tab[half * GRID:(half + 1) * GRID, :, :, :].rearrange("p h r c -> p (h r) c")
                        link(pool.affine_select(out=t[:, :, WC:GRID], in_=t[:, :, WC:GRID],
                                                  compare_op=ALU.is_ge, fill=NEG, base=WC // 2 - 1 - WC,
                                                  pattern=[[0, 2 * SLOTS], [-1, GRID - WC]], channel_multiplier=1))
                    link(pool.tensor_copy(tab9[0:GRID, :, 0:WR, :], tab[0:GRID, :, 3:3 + WR, :]))
                    link(pool.tensor_copy(tab9[GRID:P, :, 1:WR + 1, :], tab[GRID:P, :, 4:4 + WR, :]))
                    link(pool.memset(tab9[0:GRID, :, WR:WR + 1, :], NEG))
                    pool.memset(tab9[GRID:P, :, 0:1, :], NEG).then_inc(tab_ok, 1)
                    K.hold(pool, tab_ok, p + 1)
                    K.hold(pool, pair_ok, p + 2)
                    link.leave(PAIRS)

            @block.tensor
            def _(pe):
                with pe.Fori(0, PAIRS) as p:
                    pe.wait_ge(pair_ok, p + 1)
                    for i in range(3):
                        pe.wait_ge(w_in[i], p * 16 + 16)
                        if i == 2:
                            pe.wait_ge(q_ok, p + 1)
                        first = 0 if i != 1 else 3
                        for c, (at, n) in enumerate(PIECES):
                            for kc in range(KD):
                                last = nc.tensor.matmul(bank[first + c][:, 0:n], wblk[i][:, kc, :],
                                                        K.hT[:, kc, at:at + n], start=(kc == 0), stop=(kc == KD - 1))
                        last.then_inc(proj, 1)
                    pe.wait_ge(k_ok, p + 1)
                    pe.wait_ge(v_ok, p + 1)
                    pe.wait_ge(c_in, p * 32 + 32)
                    for t in range(TILES):
                        last = nc.tensor.transpose(bank[3 + t // 4][:, (t % 4) * P:(t % 4 + 1) * P],
                                                   v[:, t * P:(t + 1) * P], K.ident[:, :])
                    nc.tensor.transpose(bank[5][:, P:2 * P], k[:, NS:NT], K.ident[:, :])
                    nc.tensor.transpose(bank[5][:, 2 * P:3 * P], ckrow[:, :], K.ident[:, :]).then_inc(t_ps, 1)
                    pe.wait_ge(t_ok, p * 3 + 3)

                    def scores(i):
                        (u, even, nrows, _), h = seq[i]
                        hs = slice(h * HN, (h + 1) * HN)
                        a, b = bank[2 * (i % 2)], bank[2 * (i % 2) + 1]
                        if i >= 2:
                            pe.wait_ge(s_ok, p * NU + (i - 1))
                        qs = q[hs, u * P:(u + 1) * P]
                        if even is None:
                            last = nc.tensor.matmul(a[:, 0:P], qs, k[hs, NS:NT], start=True, stop=True)
                        else:
                            at = even * GRID
                            nc.tensor.matmul(a[:, :], qs, k[hs, at:at + 512], start=True, stop=True)
                            last = nc.tensor.matmul(b[:, 0:P], qs, ck[hs, :], start=True, stop=True)
                            if nrows > WR:
                                last = nc.tensor.matmul(b[:, P:P + GRID], qs, k[hs, at + 512:at + 576],
                                                        start=True, stop=True)
                        last.then_inc(s_ps, 1)

                    def blocks(i):
                        (u, even, nrows, _), h = seq[i]
                        hs = slice(h * HN, (h + 1) * HN)
                        if even is None:
                            return [(0, P, vtok[:, TILES - 1, hs], 0)]
                        t = even // 2
                        out = [(P * (b + 1), P, vtok[:, t + b, hs], b) for b in range(4)] + [(0, P, cv[:, hs], 4)]
                        if nrows > WR:
                            out.append((P * 5, GRID, vtok[0:GRID, t + 4, hs], 5))
                        return out

                    def heads_out(i):
                        u = seq[i][0][0]
                        pe.wait_ge(o_ok, p * NU + (i + 1))
                        nc.tensor.transpose(bank[7][:, P:2 * P], o[u % 2][:, :], K.ident[:, :]).then_inc(ot_ps, 1)

                    scores(0)
                    for i in range(NU):
                        if i + 1 < NU:
                            scores(i + 1)
                        (u, even, nrows, _), h = seq[i]
                        if h == 0 and i:
                            heads_out(i - 1)
                        pe.wait_ge(e_ok, p * NU + (i + 1))
                        if i:
                            pe.wait_ge(pta_ok, p * NU + i)
                            pe.wait_ge(ptv_ok, p * NU + i)
                        for at, n, _, b in blocks(i):
                            last = nc.tensor.transpose(bank[4 + b // 4][0:n, (b % 4) * P:(b % 4 + 1) * P],
                                                       pr[i % 2][:, at:at + n], K.ident[:, :])
                        last.then_inc(pt_ps, 1)
                        pe.wait_ge(pta_ok, p * NU + (i + 1))
                        pe.wait_ge(ptv_ok, p * NU + (i + 1))
                        if i >= 2:
                            pe.wait_ge(o_ok, p * NU + (i - 1))
                            if h == 1:
                                pe.wait_ge(ot_ok, p * (NU // 2) + u)
                        todo = blocks(i)
                        for j, (at, n, vals, b) in enumerate(todo):
                            last = nc.tensor.matmul(bank[6 + h][:, 0:HN], pt[i % 2][0:n, b, :], vals,
                                                    start=(j == 0), stop=(j == len(todo) - 1))
                        last.then_inc(o_ps, 1)
                    heads_out(NU - 1)

            @block.scalar
            def _(act):
                with act.Fori(0, PAIRS) as p:
                    act.wait_ge(proj, p * 3 + 3)
                    for c, (at, n) in enumerate(PIECES):
                        last = nc.scalar.activation(k[:, at:at + n], bank[3 + c][:, 0:n], ACT.Copy)
                    last.then_inc(k_ok, 1)
                    act.wait_ge(t_ps, p + 1)
                    nc.scalar.activation(vtok[:, 0:4, :].rearrange("p a b -> p (a b)"), bank[3][:, :],
                                         ACT.Copy).then_inc(t_ok, 1)
                    for i in range(NU):
                        (u, even, nrows, _), h = seq[i]
                        n = P if even is None else nrows * GRID + P
                        act.wait_ge(m_ok, p * NU + (i + 1))
                        if i >= 2:
                            act.wait_ge(pt_ps, p * NU + (i - 1))
                        nc.scalar.activation(pr[i % 2][:, 0:n], s[i % 2][:, 0:n], ACT.Exp, bias=st[:, 0, i:i + 1],
                                             accum_out=st[:, 1, i:i + 1]).then_inc(e_ok, 1)
                        act.wait_ge(pt_ps, p * NU + (i + 1))
                        w = P if even is None else 512
                        nc.scalar.activation(pt[i % 2][:, 0:w // P, :].rearrange("p a b -> p (a b)"), bank[4][:, 0:w],
                                             ACT.Copy).then_inc(pta_ok, 1)
                        if h == 0 and i:
                            act.wait_ge(ot_ps, p * (NU // 2) + u)
                            nc.scalar.activation(K.yB[:, bass.ds(p, 1), (u - 1) * P:u * P].rearrange("p a t -> p (a t)"),
                                                 bank[7][:, P:2 * P], ACT.Copy).then_inc(ot_ok, 1)
                    act.wait_ge(ot_ps, p * (NU // 2) + NU // 2)
                    nc.scalar.activation(K.yB[:, bass.ds(p, 1), NS:NT].rearrange("p a t -> p (a t)"),
                                         bank[7][:, P:2 * P], ACT.Copy).then_inc(ot_ok, 1)

            @block.vector
            def _(dve):
                V = nc.vector
                link = Link(dve, v_chain)
                link(V.memset(st[:, :, :], 0.0))
                V.memset(st[:, 0, 0:1], 0.0).then_inc(proj, 1)
                V.memset(st[:, 0, 1:2], 0.0).then_inc(pair_ok, 1)
                with dve.Fori(0, PAIRS) as p:
                    link.enter(p, NU)
                    dve.wait_ge(proj, p * 3 + 2)
                    for c, (at, n) in enumerate(PIECES):
                        last = V.tensor_scalar(q[:, at:at + n], bank[c][:, 0:n], SCALE, None, ALU.mult)
                    last.then_inc(q_ok, 1)
                    dve.wait_ge(proj, p * 3 + 4)
                    for c, (at, n) in enumerate(PIECES):
                        last = V.tensor_copy(v[:, at:at + n], bank[c][:, 0:n])
                    last.then_inc(v_ok, 1)
                    dve.wait_ge(t_ps, p + 1)
                    V.tensor_copy(vtok[:, 4:8, :].rearrange("p a b -> p (a b)"), bank[4][:, :]).then_inc(t_ok, 1)
                    V.tensor_copy(vtok[:, 8, :], bank[5][:, 0:P])
                    V.tensor_copy(kout[:, :], bank[5][:, P:2 * P])
                    V.tensor_copy(ck[:, :], bank[5][:, 2 * P:3 * P]).then_inc(t_ok, 1)
                    dve.wait_ge(tab_ok, p + 1)

                    def biased(i):
                        (u, even, nrows, slot), h = seq[i]
                        a, b, out = bank[2 * (i % 2)], bank[2 * (i % 2) + 1], s[i % 2]
                        dve.wait_ge(s_ps, p * NU + (i + 1))
                        if i >= 2:
                            dve.wait_ge(e_ok, p * NU + (i - 1))
                        if even is None:
                            n = P
                            V.tensor_copy(out[:, 0:P], a[:, 0:P]).then_inc(s_ok, 1)
                        else:
                            n = P + nrows * GRID
                            t = table(seq[i][0], h)
                            V.tensor_tensor(out[:, P:P + 512], a[:, :], t[:, 0:512], ALU.add)
                            if nrows > WR:
                                V.tensor_tensor(out[:, P + 512:n], b[:, P:P + GRID], t[:, 512:576], ALU.add)
                            V.tensor_copy(out[:, 0:P], b[:, 0:P]).then_inc(s_ok, 1)
                        dve.wait_ge(s_ok, p * NU + (i + 1))
                        V.tensor_reduce(st[:, 0, i:i + 1], out[:, 0:n], AX.X, ALU.max, negate=True).then_inc(m_ok, 1)

                    biased(0)
                    for i in range(NU):
                        if i + 1 < NU:
                            biased(i + 1)
                        (u, even, nrows, _), h = seq[i]
                        dve.wait_ge(pt_ps, p * NU + (i + 1))
                        if even is None:
                            V.memset(st[0:1, 0, 0:1], 0.0).then_inc(ptv_ok, 1)
                        else:
                            if nrows > WR:
                                V.tensor_copy(pt[i % 2][0:GRID, 5, :], bank[5][0:GRID, P:2 * P])
                            V.tensor_copy(pt[i % 2][:, 4, :], bank[5][:, 0:P]).then_inc(ptv_ok, 1)
                        link(V.reciprocal(st[:, 2, i:i + 1], st[:, 1, i:i + 1]))
                        dve.wait_ge(o_ps, p * NU + (i + 1))
                        if i >= 4 and h == 0:
                            dve.wait_ge(ot_ps, p * (NU // 2) + (u - 1))
                        V.tensor_scalar(o[u % 2][:, h * HN:(h + 1) * HN], bank[6 + h][:, 0:HN], st[:, 2, i:i + 1], None,
                                        ALU.mult).then_inc(o_ok, 1)
                    dve.wait_ge(ot_ok, p * (NU // 2) + NU // 2)
                    V.memset(st[:, 0, 0:1], 0.0).then_inc(pair_ok, 1)
                    link.leave(PAIRS)


def mod_row(K, part, s):
    return bass.AP(tensor=K.dram["mod_rows"].tensor, offset=(2 * KD * part + s) * P, ap=[[0, P], [2 * P, KD], [1, P]])


def output(K, A):
    nc = K.nc
    ctx = ExitStack()
    with ctx:
        def sb(name, shape, dt=F32):
            return K.sb("o_" + name, shape, dt, ctx=ctx)

        def sem(name):
            return K.sem("o_" + name)

        wo = sb("wo", [P, KD, D])
        router = sb("router", [P, KD, NE])
        gt1, s2, sh2 = (sb(n, [P, 2, D]) for n in ("gt1", "s2", "sh2"))
        g2 = sb("g2", [P, D])
        xt = [sb(f"x{i}", [P, D]) for i in range(2)]
        h2 = [sb(f"h2{i}", [P, D]) for i in range(2)]
        junk = sb("junk", [P, D])
        h2T = sb("h2T", [P, KD, P])
        st = sb("stats", [P, 6, TILES])
        aff = sb("aff", [P, NE])
        bank = K.bank
        wo_in, row_in, x_in = [sem(f"wo_in{i}") for i in range(2)], sem("rows_in"), [sem(f"x_in{i}") for i in range(2)]
        v_chain, x2_ok, sq_ok, ms_ok, rt_ok, h2_ok = (sem(n) for n in ("dve_chain", "x2", "sumsq", "meansq", "root", "h2"))
        o_ps, h_ps, hta_ok, htv_ok, l_ps, max_ok, exp_ok, aff_ok, at_ps, at_ok = (
            sem(n) for n in ("out_psum", "h2T_psum", "h2T_act", "h2T_dve", "logit_psum", "max", "exp", "aff", "affT_psum",
                             "affT"))
        h2_st, z_st = sem("h2_stored"), sem("ffn_zeroed")
        x2 = K.x2

        with nc.Block() as block:
            def store(sp, i):
                sp.wait_ge(h2_ok, i + 1)
                dst = K.dram["h2d"][i * P:(i + 1) * P, :] if i < 8 else K.dram["h2p"][:, :]
                sp.dma_start(dst, h2[i % 2][:, :]).then_inc(h2_st, 16)

            @block.sync
            def _(sp):
                wv = A["w_out"].rearrange("l (k p) n -> p (l k) n", p=P)
                for j in range(2):
                    sp.dma_start(wo[:, 4 * j:4 * j + 4, :], wv[:, 4 * j:4 * j + 4, :]).then_inc(wo_in[j], 16)
                for s in range(2):
                    for part, dst in ((GT1, gt1), (SC2, s2), (SH2, sh2)):
                        sp.dma_start(dst[:, s, :], mod_row(K, part, s)).then_inc(row_in, 16)
                sp.dma_start(g2[:, :], bass.AP(tensor=A["norm2_g"].tensor, offset=0, ap=[[0, P], [1, D]]))\
                  .then_inc(row_in, 16)
                sp.dma_start(router[:, :, :], A["router"].rearrange("l (k p) e -> p (l k) e", p=P))\
                  .then_inc(row_in, 16)
                for i in range(TILES):
                    if i >= 2:
                        sp.wait_ge(x2_ok, i - 1)
                    src = A["x_sample"][0, i * P:(i + 1) * P, :] if i < 8 else A["x_prompt"][0, :, :]
                    sp.dma_start(xt[i % 2][:, :], src).then_inc(x_in[i % 2], 16)
                    dst = K.dram["ffn"][i * P:(i + 1) * P, :] if i < 8 else K.dram["ffnp"][:, :]
                    sp.dma_start(dst, K.zero[:, :]).then_inc(z_st, 16)
                    if i:
                        store(sp, i - 1)
                store(sp, TILES - 1)
                sp.wait_ge(h2_st, 16 * TILES)
                sp.wait_ge(z_st, 16 * TILES)

            @block.tensor
            def _(pe):
                def product(i):
                    for j in range(2):
                        if i == 0:
                            for w in wo_in:
                                pe.wait_ge(w, 16)
                        elif i >= 2:
                            pe.wait_ge(x2_ok, i - 1)
                        for kc in range(KD):
                            y = K.yA[:, kc, i * P:(i + 1) * P] if kc < PAIRS else K.yB[:, kc - PAIRS, i * P:(i + 1) * P]
                            last = nc.tensor.matmul(bank[2 * (i % 2) + j][:, :], y, wo[:, kc, j * 512:(j + 1) * 512],
                                                    start=(kc == 0), stop=(kc == KD - 1))
                    last.then_inc(o_ps, 1)
                product(0)
                for i in range(TILES):
                    if i + 1 < TILES:
                        product(i + 1)
                    pe.wait_ge(h2_ok, i + 1)
                    if i:
                        pe.wait_ge(hta_ok, i)
                        pe.wait_ge(htv_ok, i)
                    for k in range(KD):
                        last = nc.tensor.transpose(bank[4 + k // 4][:, (k % 4) * P:(k % 4 + 1) * P],
                                                   h2[i % 2][:, k * P:(k + 1) * P], K.ident[:, :])
                    last.then_inc(h_ps, 1)
                    pe.wait_ge(hta_ok, i + 1)
                    pe.wait_ge(htv_ok, i + 1)
                    if i == 0:
                        pe.wait_ge(row_in, 16 * 8)
                    else:
                        pe.wait_ge(aff_ok, i)
                    for k in range(KD):
                        last = nc.tensor.matmul(bank[6][:, 0:NE], h2T[:, k, :], router[:, k, :], start=(k == 0),
                                                stop=(k == KD - 1))
                    last.then_inc(l_ps, 1)
                    pe.wait_ge(aff_ok, i + 1)
                    if i:
                        pe.wait_ge(at_ok, i)
                    nc.tensor.transpose(bank[7][0:NE, 0:P], aff[:, :], K.ident[:, :]).then_inc(at_ps, 1)

            @block.scalar
            def _(act):
                for i in range(TILES):
                    act.wait_ge(x2_ok, i + 1)
                    nc.scalar.activation(junk[:, :], x2[:, i, :], ACT.Square, accum_out=st[:, 0, i:i + 1])\
                      .then_inc(sq_ok, 1)
                    act.wait_ge(ms_ok, i + 1)
                    nc.scalar.activation(st[:, 2, i:i + 1], st[:, 1, i:i + 1], ACT.Sqrt).then_inc(rt_ok, 1)
                    act.wait_ge(h_ps, i + 1)
                    nc.scalar.activation(h2T[:, 0:4, :].rearrange("p a b -> p (a b)"), bank[4][:, :], ACT.Copy)\
                      .then_inc(hta_ok, 1)
                    act.wait_ge(max_ok, i + 1)
                    nc.scalar.activation(aff[:, :], bank[6][:, 0:NE], ACT.Exp, bias=st[:, 3, i:i + 1],
                                         accum_out=st[:, 4, i:i + 1]).then_inc(exp_ok, 1)
                    act.wait_ge(at_ps, i + 1)
                    nc.scalar.activation(K.affT[:, i * P:(i + 1) * P], bank[7][0:NE, 0:P], ACT.Copy).then_inc(at_ok, 1)

            @block.vector
            def _(dve):
                V = nc.vector
                link = Link(dve, v_chain)
                dve.wait_ge(row_in, 16 * 8)
                link(V.tensor_scalar(s2[:, :, :], s2[:, :, :], 1.0, None, ALU.add))
                link(V.tensor_tensor(s2[:, :, :], s2[:, :, :], g2[:, :].unsqueeze(1).broadcast_to([P, 2, D]), ALU.mult))

                def residual(i):
                    s = 0 if i < 8 else 1
                    dve.wait_ge(o_ps, i + 1)
                    dve.wait_ge(x_in[i % 2], 16 * (i // 2 + 1))
                    for j in range(2):
                        c = slice(j * 512, (j + 1) * 512)
                        last = V.tensor_tensor(x2[:, i, c], bank[2 * (i % 2) + j][:, :], gt1[:, s, c], ALU.mult)
                    link(last)
                    V.tensor_tensor(x2[:, i, :], x2[:, i, :], xt[i % 2][:, :], ALU.add).then_inc(x2_ok, 1)

                residual(0)
                for i in range(TILES):
                    s = 0 if i < 8 else 1
                    dve.wait_ge(sq_ok, i + 1)
                    V.tensor_scalar(st[:, 1, i:i + 1], st[:, 0, i:i + 1], 1.0 / D, EPS, ALU.mult, ALU.add)\
                     .then_inc(ms_ok, 1)
                    if i + 1 < TILES:
                        residual(i + 1)
                    dve.wait_ge(rt_ok, i + 1)
                    link(V.reciprocal(st[:, 5, i:i + 1], st[:, 2, i:i + 1]))
                    if i >= 2:
                        dve.wait_ge(h2_st, 16 * (i - 1))
                    link(V.scalar_tensor_tensor(h2[i % 2][:, :], x2[:, i, :], st[:, 5, i:i + 1], s2[:, s, :], ALU.mult,
                                                ALU.mult))
                    V.tensor_tensor(h2[i % 2][:, :], h2[i % 2][:, :], sh2[:, s, :], ALU.add).then_inc(h2_ok, 1)
                    dve.wait_ge(h_ps, i + 1)
                    V.tensor_copy(h2T[:, 4:8, :].rearrange("p a b -> p (a b)"), bank[5][:, :]).then_inc(htv_ok, 1)
                    dve.wait_ge(l_ps, i + 1)
                    V.tensor_reduce(st[:, 3, i:i + 1], bank[6][:, 0:NE], AX.X, ALU.max, negate=True).then_inc(max_ok, 1)
                    dve.wait_ge(exp_ok, i + 1)
                    link(V.reciprocal(st[:, 1, i:i + 1], st[:, 4, i:i + 1]))
                    V.tensor_scalar(aff[:, :], aff[:, :], st[:, 1, i:i + 1], None, ALU.mult).then_inc(aff_ok, 1)


def topk(K, A):
    nc = K.nc
    ctx = ExitStack()
    with ctx:
        val = K.sb("k_val", [NE, TOK], ctx=ctx)
        idx = K.sb("k_idx", [NE, TOK], U32, ctx=ctx)
        idxf = K.sb("k_idxf", [NE, TOK], ctx=ctx)
        chain, picked, turned = K.sem("k_chain"), K.sem("k_picked"), K.sem("k_turned")
        with nc.Block() as block:
            @block.vector
            def _(dve):
                V = nc.vector
                link = Link(dve, chain)
                V.memset(K.idx[:, :], 0)
                V.memset(K.idxp[:, :], 0)
                for at, n, col, cap in ((0, NS, 0, CAP), (NS, NP, CAP, CAPP)):
                    a = K.affT[:, at:at + n]
                    for b in range(cap // 8):
                        c = slice(col + 8 * b, col + 8 * b + 8)
                        link(V.max(val[:, c], a))
                        link(V.max_index(idx[:, c], val[:, c], a))
                        link(V.match_replace(a, val[:, c], a, -1.0))
                V.tensor_copy(idxf[:, :], idx[:, :]).then_inc(picked, 1)
                dve.wait_ge(turned, 1)
                V.tensor_copy(K.idx[:, 0:NE], K.bank[0][:, 0:NE])
                V.tensor_copy(K.gate[:, :], K.bank[0][:, NE:2 * NE])
                V.tensor_copy(K.idxp[:, 0:NE], K.bank[1][0:CAPP, 0:NE])
                link(V.tensor_copy(K.gatep[:, :], K.bank[1][0:CAPP, NE:2 * NE]))

            @block.tensor
            def _(pe):
                pe.wait_ge(picked, 1)
                for j, src in enumerate((idxf, val)):
                    c = slice(j * NE, (j + 1) * NE)
                    nc.tensor.transpose(K.bank[0][:, c], src[:, 0:CAP], K.ident[0:NE, 0:NE])
                    last = nc.tensor.transpose(K.bank[1][0:CAPP, c], src[:, CAP:TOK], K.ident[0:NE, 0:NE])
                last.then_inc(turned, 1)


def experts(K, A):
    nc = K.nc
    ctx = ExitStack()
    DEPTH = 11
    assert FB % DEPTH == 0
    HR = 4
    PER_BANK = 3
    with ctx:
        def sb(name, shape, dt=F32):
            return K.sb("e_" + name, shape, dt, ctx=ctx)

        def sem(name):
            return K.sem("e_" + name)

        wg = sb("wg", [P, DEPTH, KD, P])
        wu = sb("wu", [P, DEPTH, KD, P])
        wd = sb("wd", [P, DEPTH, D])
        xe, xp = sb("xe", [P, D]), sb("xp", [CAPP, D])
        xT = sb("xT", [P, KD, TOK])
        sg = [sb(f"sg{i}", [P, TOK]) for i in range(2)]
        tm = [sb(f"tm{i}", [P, TOK]) for i in range(2)]
        hid = sb("hid", [P, HR, TOK])
        yT = sb("yT", [P, KD, TOK])
        ye, yp = sb("ye", [P, D]), sb("yp", [CAPP, D])
        gi, si = sb("gi", [P, 1], U32), sb("si", [P, 1], U32)
        gip, sip = sb("gip", [CAPP, 1], U32), sb("sip", [CAPP, 1], U32)
        gc, gcp = sb("gc", [P, 1]), sb("gcp", [CAPP, 1])
        bank = K.bank
        w_in = [sem(f"w_in{i}") for i in range(DEPTH)]
        used = sem("w_used")
        i_ok, x_in, x_ps, xa_ok, xv_ok = sem("idx_ok"), sem("x_in"), sem("xT_psum"), sem("xT_act"), sem("xT_dve")
        gu_ps, sg_ok, tm_ok, hid_ok = sem("gu_psum"), sem("sigmoid"), sem("tm"), sem("hid")
        d_ps, ya_ok, yv_ok, y_ps, sa_ok, sv_ok = (sem(n) for n in ("down_psum", "yT_act", "yT_dve", "y_psum", "y_act",
                                                                   "y_dve"))
        free, sc = sem("y_free"), sem("scattered")

        with nc.Block() as block:
            @block.sync
            def _(sp):
                gv = A["e_gate"].rearrange("l e (k p) f -> p (l e) k f", p=P)
                uv = A["e_up"].rearrange("l e (k p) f -> p (l e) k f", p=P)
                dv = A["e_down"].rearrange("l e (b p) n -> p (l e) b n", p=P)
                with sp.Fori(0, NE) as e:
                    for b in range(FB):
                        s = b % DEPTH
                        sp.wait_ge(used, e * FB + (b + 1))
                        sp.dma_start(wg[:, s, :, :], gv[:, bass.ds(e, 1), :, b * P:(b + 1) * P]
                                     .rearrange("p e k f -> p (e k) f")).then_inc(w_in[s], 16)
                        sp.dma_start(wu[:, s, :, :], uv[:, bass.ds(e, 1), :, b * P:(b + 1) * P]
                                     .rearrange("p e k f -> p (e k) f")).then_inc(w_in[s], 16)
                        sp.dma_start(wd[:, s, :], dv[:, bass.ds(e, 1), b, :].rearrange("p e n -> p (e n)"))\
                          .then_inc(w_in[s], 16)

            @block.gpsimd
            def _(pool):
                def gather():
                    for dst, src, ix in ((xe, K.dram["h2d"], gi), (xp, K.dram["h2p"], gip)):
                        pool.indirect_dma_start(out=dst[:, :], out_offset=None, in_=src[:, :],
                                                in_offset=bass.IndirectOffsetOnAxis(ap=ix[:, :], axis=0))\
                            .then_inc(x_in, 16)

                pool.tensor_copy(gi[:, :], K.idx[:, 0:1])
                pool.tensor_copy(gip[:, :], K.idxp[:, 0:1]).then_inc(i_ok, 1)
                pool.wait_ge(i_ok, 1)
                gather()
                pool.sem_inc(free, 1)
                with pool.Fori(0, NE) as e:
                    K.hold(pool, x_in, e * 32 + 32)
                    pool.tensor_copy(gi[:, :], K.idx[:, bass.ds(e + 1, 1)])
                    pool.tensor_copy(gip[:, :], K.idxp[:, bass.ds(e + 1, 1)])
                    pool.tensor_copy(si[:, :], K.idx[:, bass.ds(e, 1)])
                    pool.tensor_copy(gc[:, :], K.gate[:, bass.ds(e, 1)])
                    pool.tensor_copy(gcp[:, :], K.gatep[:, bass.ds(e, 1)])
                    pool.tensor_copy(sip[:, :], K.idxp[:, bass.ds(e, 1)]).then_inc(i_ok, 1)
                    K.hold(pool, i_ok, e + 2)
                    K.hold(pool, x_ps, e + 1)
                    gather()
                    K.hold(pool, sa_ok, e * 2 + 2)
                    K.hold(pool, sv_ok, e * 2 + 2)
                    for src, dst, ix in ((ye, K.dram["ffn"], si), (yp, K.dram["ffnp"], sip)):
                        pool.indirect_dma_start(out=dst[:, :], out_offset=bass.IndirectOffsetOnAxis(ap=ix[:, :], axis=0),
                                                in_=src[:, :], in_offset=None, compute_op=ALU.add).then_inc(sc, 16)
                    K.hold(pool, sc, e * 32 + 32)
                    pool.sem_inc(free, 1)
                pool.wait_ge(x_in, 32 * (NE + 1))

            @block.tensor
            def _(pe):
                pe.sem_inc(used, DEPTH)
                with pe.Fori(0, NE) as e:
                    pe.wait_ge(x_in, e * 32 + 32)
                    pe.wait_ge(free, e + 1)
                    for k in range(KD):
                        b, c = 3 + k // PER_BANK, (k % PER_BANK) * TOK
                        nc.tensor.transpose(bank[b][:, c:c + CAP], xe[:, k * P:(k + 1) * P], K.ident[:, :])
                        last = nc.tensor.transpose(bank[b][:, c + CAP:c + TOK], xp[:, k * P:(k + 1) * P],
                                                   K.ident[0:CAPP, 0:CAPP])
                    last.then_inc(x_ps, 1)
                    pe.wait_ge(xa_ok, e + 1)
                    pe.wait_ge(xv_ok, e + 1)

                    def gate_up(b):
                        s = b % DEPTH
                        pe.wait_ge(w_in[s], e * 96 + 48 * (b // DEPTH + 1))
                        if b >= 2:
                            pe.wait_ge(hid_ok, e * FB + (b - 1))
                        for j, w in enumerate((wg, wu)):
                            for k in range(KD):
                                last = nc.tensor.matmul(bank[6 + b % 2][:, j * TOK:(j + 1) * TOK], w[:, s, k, :],
                                                        xT[:, k, :], start=(k == 0), stop=(k == KD - 1))
                        last.then_inc(gu_ps, 1)

                    def down(b):
                        s = b % DEPTH
                        pe.wait_ge(hid_ok, e * FB + (b + 1))
                        for k in range(KD):
                            c = (k % PER_BANK) * TOK
                            last = nc.tensor.matmul(bank[k // PER_BANK][:, c:c + TOK], wd[:, s, k * P:(k + 1) * P],
                                                    hid[:, b % HR, :], start=(b == 0 and k % PER_BANK == 0),
                                                    stop=(b == FB - 1), skip_group_check=True)
                        last.then_inc(used, 1)

                    gate_up(0)
                    for b in range(1, FB):
                        gate_up(b)
                        down(b - 1)
                    down(FB - 1)
                    pe.wait_ge(ya_ok, e + 1)
                    pe.wait_ge(yv_ok, e + 1)
                    for j in range(2):
                        for k in range(4):
                            src = yT[:, 4 * j + k, :]
                            c = slice(k * P, (k + 1) * P)
                            nc.tensor.transpose(bank[3 + 2 * j][:, c], src[:, 0:CAP], K.ident[:, :])
                            last = nc.tensor.transpose(bank[4 + 3 * j][0:CAPP, c], src[:, CAP:TOK], K.ident[:, :])
                        last.then_inc(y_ps, 1)

            @block.scalar
            def _(act):
                with act.Fori(0, NE) as e:
                    act.wait_ge(x_ps, e + 1)
                    nc.scalar.activation(xT[:, 0:3, :].rearrange("p a b -> p (a b)"), bank[3][:, 0:3 * TOK], ACT.Copy)\
                      .then_inc(xa_ok, 1)
                    for b in range(FB):
                        act.wait_ge(gu_ps, e * FB + (b + 1))
                        nc.scalar.activation(sg[b % 2][:, :], bank[6 + b % 2][:, 0:TOK], ACT.Sigmoid).then_inc(sg_ok, 1)
                    act.wait_ge(used, (e + 1) * FB + DEPTH)
                    nc.scalar.activation(yT[:, 6:8, :].rearrange("p a b -> p (a b)"), bank[2][:, 0:2 * TOK], ACT.Copy)\
                      .then_inc(ya_ok, 1)
                    act.wait_ge(free, e + 1)
                    act.wait_ge(i_ok, e + 2)
                    for j in range(2):
                        act.wait_ge(y_ps, e * 2 + (j + 1))
                        nc.scalar.activation(yp[:, j * 512:(j + 1) * 512], bank[4 + 3 * j][0:CAPP, :], ACT.Copy,
                                             scale=gcp[:, :]).then_inc(sa_ok, 1)

            @block.vector
            def _(dve):
                V = nc.vector
                with dve.Fori(0, NE) as e:
                    dve.wait_ge(x_ps, e + 1)
                    V.tensor_copy(xT[:, 3:6, :].rearrange("p a b -> p (a b)"), bank[4][:, 0:3 * TOK])
                    V.tensor_copy(xT[:, 6:8, :].rearrange("p a b -> p (a b)"), bank[5][:, 0:2 * TOK]).then_inc(xv_ok, 1)
                    for b in range(FB):
                        dve.wait_ge(sg_ok, e * FB + (b + 1))
                        V.tensor_tensor(tm[b % 2][:, :], bank[6 + b % 2][:, 0:TOK], sg[b % 2][:, :], ALU.mult).then_inc(tm_ok, 1)
                        dve.wait_ge(tm_ok, e * FB + (b + 1))
                        V.tensor_tensor(hid[:, b % HR, :], bank[6 + b % 2][:, TOK:2 * TOK], tm[b % 2][:, :],
                                        ALU.mult)\
                         .then_inc(hid_ok, 1)
                    dve.wait_ge(used, (e + 1) * FB + DEPTH)
                    for j in range(2):
                        last = V.tensor_copy(yT[:, 3 * j:3 * j + 3, :].rearrange("p a b -> p (a b)"),
                                             bank[j][:, 0:3 * TOK])
                    last.then_inc(yv_ok, 1)
                    dve.wait_ge(free, e + 1)
                    dve.wait_ge(i_ok, e + 2)
                    for j in range(2):
                        dve.wait_ge(y_ps, e * 2 + (j + 1))
                        V.tensor_scalar(ye[:, j * 512:(j + 1) * 512], bank[3 + 2 * j][:, :], gc[:, :], None,
                                        ALU.mult).then_inc(sv_ok, 1)


def final(K, A):
    nc = K.nc
    ctx = ExitStack()
    with ctx:
        def sb(name, shape, dt=F32):
            return K.sb("f_" + name, shape, dt, ctx=ctx)

        def sem(name):
            return K.sem("f_" + name)

        gt2 = sb("gt2", [P, 2, D])
        gf = sb("gf", [P, D])
        f = [sb(f"f{i}", [P, D]) for i in range(4)]
        junk = sb("junk", [P, D])
        st = sb("stats", [P, 4, TILES])
        rows, f_in = sem("rows_in"), [sem(f"f_in{i}") for i in range(4)]
        chain, x_ok, sq_ok, ms_ok, rt_ok, y_ok = (sem(n) for n in ("chain", "x3", "sumsq", "meansq", "root", "y"))
        y_st = [sem(f"y_stored{i}") for i in range(4)]
        with nc.Block() as block:
            @block.sync
            def _(sp):
                for s in range(2):
                    sp.dma_start(gt2[:, s, :], mod_row(K, GT2, s)).then_inc(rows, 16)
                sp.dma_start(gf[:, :], bass.AP(tensor=A["final_norm_g"].tensor, offset=0, ap=[[0, P], [1, D]]))\
                  .then_inc(rows, 16)
                for i in range(TILES):
                    if i >= 4:
                        sp.wait_ge(y_st[i % 4], 16 * (i // 4))
                    src = K.dram["ffn"][i * P:(i + 1) * P, :] if i < 8 else K.dram["ffnp"][:, :]
                    sp.dma_start(f[i % 4][:, :], src).then_inc(f_in[i % 4], 16)

            @block.scalar
            def _(act):
                for i in range(TILES + 1):
                    if i < TILES:
                        act.wait_ge(x_ok, i + 1)
                        nc.scalar.activation(junk[:, :], K.x2[:, i, :], ACT.Square, accum_out=st[:, 0, i:i + 1])\
                          .then_inc(sq_ok, 1)
                        act.wait_ge(ms_ok, i + 1)
                        nc.scalar.activation(st[:, 2, i:i + 1], st[:, 1, i:i + 1], ACT.Sqrt).then_inc(rt_ok, 1)
                    if i:
                        t = i - 1
                        act.wait_ge(y_ok, t + 1)
                        dst = A["y_sample"][0, t * P:(t + 1) * P, :] if t < 8 else A["y_prompt"][0, :, :]
                        act.dma_start(dst, f[t % 4][:, :]).then_inc(y_st[t % 4], 16)
                for i in range(4):
                    act.wait_ge(y_st[i], 16 * len(range(i, TILES, 4)))

            @block.vector
            def _(dve):
                V = nc.vector
                link = Link(dve, chain)
                dve.wait_ge(rows, 48)

                def add(i):
                    s = 0 if i < 8 else 1
                    dve.wait_ge(f_in[i % 4], 16 * (i // 4 + 1))
                    link(V.tensor_tensor(f[i % 4][:, :], f[i % 4][:, :], gt2[:, s, :], ALU.mult))
                    V.tensor_tensor(K.x2[:, i, :], K.x2[:, i, :], f[i % 4][:, :], ALU.add).then_inc(x_ok, 1)
                    dve.wait_ge(sq_ok, i + 1)
                    V.tensor_scalar(st[:, 1, i:i + 1], st[:, 0, i:i + 1], 1.0 / D, EPS, ALU.mult, ALU.add)\
                     .then_inc(ms_ok, 1)

                add(0)
                for i in range(TILES):
                    if i + 1 < TILES:
                        add(i + 1)
                    dve.wait_ge(rt_ok, i + 1)
                    link(V.reciprocal(st[:, 3, i:i + 1], st[:, 2, i:i + 1]))
                    V.scalar_tensor_tensor(f[i % 4][:, :], K.x2[:, i, :], st[:, 3, i:i + 1], gf[:, :], ALU.mult,
                                           ALU.mult).then_inc(y_ok, 1)


def trunk(nc, A):
    ctx = ExitStack()
    with ctx:
        K = Chip(nc, ctx)
        for name, shape in (("mod_rows", (96, P)), ("spread", (GRID, HEADS * (2 * WR - 1) * P)), ("h2d", (NS, D)),
                            ("h2p", (NP, D)), ("ffn", (NS, D)), ("ffnp", (NP, D))):
            K.dram[name] = nc.dram_tensor("scratch_" + name, shape, F32, kind="Internal").ap()
        K.ident = K.sb("ident", [P, P])
        K.eps = K.sb("eps", [P, 3])
        K.zero = K.sb("zero", [P, D])
        K.vecT = K.sb("vecT", [P, V_ROWS])
        K.modT = K.sb("modT", [P, 48, 2])
        K.s1 = K.sb("s1", [P, KD, 2])
        K.affT = K.sb("affT", [NE, NT])
        K.idx = K.sb("idx", [P, NE + 1], U32)
        K.idxp = K.sb("idxp", [CAPP, NE + 1], U32)
        K.gate = K.sb("gate", [P, NE])
        K.gatep = K.sb("gatep", [CAPP, NE])
        big = K.sb("hT_x2", [P, KD * NT])
        K.hT = big[:, :].rearrange("p (k t) -> p k t", k=KD)
        K.x2 = big[:, :].rearrange("p (i n) -> p i n", i=TILES)
        mixed = ExitStack()
        with mixed:
            K.yA = K.sb("yA", [P, PAIRS, NT], ctx=mixed)
            scan = ExitStack()
            with scan:
                K.head_ones = K.sb("head_ones", [P, P], ctx=scan)
                K.head_mask = K.sb("head_mask", [P, P], ctx=scan)
                K.causal = K.sb("causal", [P, 2, 4, P], BF16, ctx=scan)
                K.level = K.sb("level", [P, 2, 7, P], BF16, ctx=scan)
                K.scan_keep = K.sb("scan_keep", [P, NT], BF16, ctx=scan)
                modulation(K, A)
                K.next_stage()
                norm1(K, A)
                K.next_stage()
                rwkv(K, A)
                K.next_stage()
            K.yB = K.sb("yB", [P, PAIRS, NT], ctx=mixed)
            attention(K, A)
            K.next_stage()
            output(K, A)
            K.next_stage()
        topk(K, A)
        K.next_stage()
        experts(K, A)
        K.next_stage()
        final(K, A)


_INS = ["x_prompt", "x_sample", "cache_na_k", "cache_na_v", "state_rwkv", "c", "c_ctx", "final_norm_g", "norm1_g",
        "norm2_g", "w_mod", "b_mod", "w_in", "mu_prev", "mu_next", "w0", "w_up", "a0", "a_up", "g_up", "k_k", "k_a",
        "r_k", "gn_g", "gn_b", "rpb", "w_out", "router", "e_gate", "e_up", "e_down"]
_OUTS = [("y_prompt", (1, NP, D)), ("y_sample", (1, NS, D)), ("new_k", (1, 1, NP, HEADS, HN)),
         ("new_v", (1, 1, NP, HEADS, HN)), ("new_s", (1, 1, 2, HEADS, HN, HN))]


def kernel(**inputs):
    import numpy as np
    import concourse.bacc as bacc
    from concourse.bass_utils import run_bass_kernel_spmd

    nc = bacc.Bacc("TRN2", target_bir_lowering=False, num_devices=1)
    arrays, A = {}, {}
    for name in _INS:
        a = np.ascontiguousarray(inputs[name])
        arrays["in_" + name] = a
        A[name] = nc.dram_tensor("in_" + name, a.shape, mybir.dt.from_np(a.dtype), kind="ExternalInput").ap()
    for name, shape in _OUTS:
        A[name] = nc.dram_tensor("out_" + name, shape, F32, kind="ExternalOutput").ap()
    trunk(nc, A)
    r = run_bass_kernel_spmd(nc, [arrays], core_ids=[0])
    return tuple(r.results[0]["out_" + name] for name, _ in _OUTS)
```

```python
from contextlib import ExitStack

import concourse.bass as bass
from concourse import mybir

F32 = mybir.dt.float32
BF16 = mybir.dt.bfloat16
I32 = mybir.dt.int32
U32 = mybir.dt.uint32
ALU = mybir.AluOpType
ACT = mybir.ActivationFunctionType
AX = mybir.AxisListType

P = 128
D = 1024
KD = D // P
NS = 1024
NP = 128
NT = NS + NP
TILES = NT // P
HEADS = 8
HN = 64
DA = HEADS * HN
PAIRS = HEADS // 2
ACOLS = 3 * DA + 256
DIN = ACOLS + 3 * DA
GRID = 64
WR, WC = 8, 16
NE = 16
FE = 2816
FB = FE // P
CAP = 2 * NS // NE
CAPP = 2 * NP // NE
TOK = CAP + CAPP
EPS = 1e-6
GN_EPS = 64e-5
KK_EPS = 1e-12
SCALE = HN ** -0.5
NEG = -1e30
DECAY = 0.6065306597126334
PIECES = [(0, 512), (512, 512), (1024, 128)]
V_MUP, V_MUN, V_W0, V_A0, V_KK, V_KA, V_RK, V_GG, V_GB = 0, 12, 24, 32, 40, 44, 48, 52, 56
V_MUPL, V_MUNL, V_C, V_G1, V_ROWS = 60, 62, 64, 80, 88
SH1, SC1, GT1, SH2, SC2, GT2 = range(6)


class Chip:

    def __init__(self, nc, ctx):
        self.nc, self.ctx, self.dram, self.sems = nc, ctx, {}, []
        self.passed = nc.alloc_semaphore("passed")
        self.bank = [ctx.enter_context(nc.psum_tensor(f"bank{i}", [P, 512], F32)) for i in range(8)]

    def sb(self, name, shape, dt=F32, ctx=None):
        return (ctx or self.ctx).enter_context(self.nc.sbuf_tensor(name, shape, dt))

    def sem(self, name):
        self.sems.append(self.nc.alloc_semaphore(name))
        return self.sems[-1]

    def hold(self, eng, sem, value):
        eng.wait_ge(sem, value)
        eng.sem_inc(self.passed, 1)

    def next_stage(self):
        self.nc.all_engine_barrier()
        self.nc.clear_and_free_semaphores(self.sems)
        self.nc.all_engine_barrier()
        self.sems = []


class Link:

    def __init__(self, eng, sem, chip=None):
        self.eng, self.sem, self.base, self.count, self.chip = eng, sem, 0, 0, chip

    def __call__(self, ins):
        self.count += 1
        ins.then_inc(self.sem, 1)
        if self.chip:
            self.chip.hold(self.eng, self.sem, self.base + self.count)
        else:
            self.eng.wait_ge(self.sem, self.base + self.count)

    def enter(self, i, per):
        self.start, self.per = self.base + self.count, per
        self.base, self.count = i * per + self.start, 0

    def leave(self, times):
        assert self.count == self.per, (self.sem, self.count)
        self.base, self.count = self.start + times * self.per, 0


def rows_view(ap, n, row=0):
    return bass.AP(tensor=ap.tensor, offset=row * P, ap=[[P, n], [1, P]])


def modulation(K, A):
    nc = K.nc
    CH = 512
    WB = 4
    NCH = 6 * D // CH
    ctx = ExitStack()
    with ctx:
        vrows = K.sb("vrows", [V_ROWS, P], ctx=ctx)
        brow = K.sb("brow", [2, 6 * D], ctx=ctx)
        mod = K.sb("mod", [2, 6 * D], ctx=ctx)
        sig = K.sb("cond_sig", [P, 16], ctx=ctx)
        cond = K.sb("cond", [P, KD, 2], ctx=ctx)
        wbuf = [K.sb(f"wmod{i}", [P, KD, CH], ctx=ctx) for i in range(WB)]
        rowi = K.sb("rowi", [P, P], I32, ctx=ctx)
        coli = K.sb("coli", [P, P], I32, ctx=ctx)
        xori = K.sb("xori", [P, P], I32, ctx=ctx)
        xorf = K.sb("xorf", [P, P], ctx=ctx)
        low = K.sb("low", [P, 2, P], ctx=ctx)
        cmp = K.sb("cmp", [P, P], ctx=ctx)
        rows_in = K.sem("m_rows_in")
        w_in = [K.sem(f"m_w_in{i}") for i in range(WB)]
        g_chain = K.sem("m_pool_chain")
        consts = K.sem("m_consts")
        v_t = K.sem("m_vec_transposed")
        v_chain = K.sem("m_dve_chain")
        vec_ok = K.sem("m_vec_ok")
        sig_ok = K.sem("m_sig_ok")
        cond_ok = K.sem("m_cond_ok")
        mm_ok = K.sem("m_mod_mm")
        mod_ok = K.sem("m_mod_ok")
        mt_ps = K.sem("m_modT_psum")
        out_ok = K.sem("m_rows_stored")

        with nc.Block() as block:
            @block.sync
            def _(sp):
                for name, row, n, src in (
                        ("mu_prev", V_MUP, 12, 0), ("mu_next", V_MUN, 12, 0), ("w0", V_W0, 8, 0),
                        ("a0", V_A0, 8, 0), ("k_k", V_KK, 4, 0), ("k_a", V_KA, 4, 0), ("r_k", V_RK, 4, 0),
                        ("gn_g", V_GG, 4, 0), ("gn_b", V_GB, 4, 0), ("mu_prev", V_MUPL, 2, 12),
                        ("mu_next", V_MUNL, 2, 12), ("c", V_C, 8, 0), ("c_ctx", V_C + 8, 8, 0),
                        ("norm1_g", V_G1, 8, 0)):
                    sp.dma_start(vrows[row:row + n, :], rows_view(A[name], n, src)).then_inc(rows_in, 16)
                sp.dma_start(brow[:, :], bass.AP(tensor=A["b_mod"].tensor, offset=0, ap=[[0, 2], [1, 6 * D]]))\
                  .then_inc(rows_in, 16)
                wv = A["w_mod"].rearrange("l (k p) n -> p (l k) n", p=P)
                for c in range(NCH):
                    if c >= WB:
                        sp.wait_ge(mm_ok, c - WB + 1)
                    sp.dma_start(wbuf[c % WB][:, :, :], wv[:, :, c * CH:(c + 1) * CH]).then_inc(w_in[c % WB], 16)
                for part in range(6):
                    sp.wait_ge(mod_ok, 2 * part + 2)
                    sp.dma_start(bass.AP(tensor=K.dram["mod_rows"].tensor, offset=part * 2 * D,
                                         ap=[[P, 2], [2 * P, KD], [1, P]]),
                                 mod[:, part * D:(part + 1) * D].rearrange("s (k p) -> s k p", p=P)).then_inc(out_ok, 16)
                sp.wait_ge(out_ok, 16 * 6)

            @block.gpsimd
            def _(pool):
                link = Link(pool, g_chain)
                pool.memset(K.zero[:, :], 0.0)
                for col, value in ((0, EPS), (1, KK_EPS), (2, GN_EPS)):
                    pool.memset(K.eps[:, col:col + 1], value)
                link(pool.memset(K.ident[:, :], 0.0))
                link(pool.affine_select(out=K.ident[:, :], in_=K.ident[:, :], compare_op=ALU.not_equal, fill=1.0,
                                        base=0, pattern=[[-1, P]], channel_multiplier=1))
                pool.memset(K.head_ones[:, :], 0.0)
                pool.memset(K.head_mask[:, :], 0.0)
                link(pool.memset(low[:, :, :], 1.0))
                for h in range(2):
                    link(pool.memset(K.head_ones[h * HN:(h + 1) * HN, h * HN:(h + 1) * HN], 1.0))
                    link(pool.memset(K.head_mask[h * HN:(h + 1) * HN, h * HN:(h + 1) * HN], 1.0))
                link(pool.affine_select(out=low[:, 0, :], in_=low[:, 0, :], compare_op=ALU.is_gt, fill=0.0,
                                        base=0, pattern=[[-1, P]], channel_multiplier=1))
                link(pool.affine_select(out=low[:, 1, :], in_=low[:, 1, :], compare_op=ALU.is_gt, fill=0.0,
                                        base=0, pattern=[[1, P]], channel_multiplier=-1))
                link(pool.memset(K.causal[:, :, :, :], 1.0))
                for d, sign in ((0, 1), (1, -1)):
                    for q in range(4):
                        v = K.causal[:, d, q, :]
                        pool.affine_select(out=v, in_=v, compare_op=ALU.is_ge if q % 2 else ALU.is_gt, fill=0.0,
                                           base=0, pattern=[[sign, P]], channel_multiplier=-sign)
                pool.memset(K.scan_keep[:, :], 1.0)
                link(pool.iota(rowi[:, :], [[0, P]], base=0, channel_multiplier=1))
                pool.memset(K.scan_keep[:, :].rearrange("p (c t) -> p c t", t=P)[:, :, 0:1], 0.0)
                pool.iota(coli[:, :], [[1, P]], base=0, channel_multiplier=0).then_inc(consts, 1)

            @block.vector
            def _(dve):
                link = Link(dve, v_chain)
                dve.wait_ge(v_t, 1)
                link(nc.vector.tensor_copy(K.vecT[:, :], K.bank[0][:, 0:V_ROWS]))
                nc.vector.memset(cmp[:, :], 0.0).then_inc(vec_ok, 1)
                dve.wait_ge(sig_ok, 1)
                cv = K.vecT[:, V_C:V_C + 16].rearrange("p (s k) -> p k s", s=2)
                nc.vector.tensor_tensor(cond[:, :, :], cv, sig[:, :].rearrange("p (s k) -> p k s", s=2),
                                        ALU.mult).then_inc(cond_ok, 1)
                def biased(c):
                    dve.wait_ge(mm_ok, c + 1)
                    n = slice(c * CH, (c + 1) * CH)
                    nc.vector.tensor_tensor(mod[:, n], K.bank[2 + c % 4][0:2, :], brow[:, n], ALU.add)\
                      .then_inc(mod_ok, 1)

                biased(0)
                biased(1)
                dve.wait_ge(consts, 1)
                link(nc.vector.tensor_tensor(xori[:, :], rowi[:, :], coli[:, :], ALU.bitwise_xor))
                link(nc.vector.tensor_copy(xorf[:, :], xori[:, :]))
                for lev in range(7):
                    link(nc.vector.tensor_scalar(cmp[:, :], xorf[:, :], float(2 ** (lev + 1)), None, ALU.is_lt))
                    link(nc.vector.scalar_tensor_tensor(cmp[:, :], xorf[:, :], float(2 ** lev), cmp[:, :],
                                                        ALU.is_ge, ALU.mult))
                    for d in range(2):
                        link(nc.vector.tensor_tensor(K.level[:, d, lev, :], cmp[:, :], low[:, d, :], ALU.mult))
                for c in range(2, 6):
                    biased(c)
                dve.wait_ge(mt_ps, 1)
                link(nc.vector.tensor_copy(K.modT[:, :, :], K.bank[0][:, 0:32].rearrange("p (b s) -> p b s", s=2)))
                g = K.vecT[:, V_G1:V_G1 + 8].unsqueeze(2).broadcast_to([P, 8, 2])
                link(nc.vector.tensor_scalar(K.s1[:, :, :], K.modT[:, SC1 * 8:SC1 * 8 + 8, :], 1.0, None, ALU.add))
                link(nc.vector.tensor_tensor(K.s1[:, :, :], K.s1[:, :, :], g, ALU.mult))
                for c in range(6, NCH):
                    biased(c)

            @block.scalar
            def _(act):
                act.wait_ge(vec_ok, 1)
                nc.scalar.activation(sig[:, :], K.vecT[:, V_C:V_C + 16], ACT.Sigmoid).then_inc(sig_ok, 1)

            @block.tensor
            def _(pe):
                pe.wait_ge(rows_in, 16 * 15)
                pe.wait_ge(g_chain, 2)
                nc.tensor.transpose(K.bank[0][:, 0:V_ROWS], vrows[:, :], K.ident[0:V_ROWS, 0:V_ROWS]).then_inc(v_t, 1)
                pe.wait_ge(cond_ok, 1)
                for c in range(NCH):
                    pe.wait_ge(w_in[c % WB], 16 * (c // WB + 1))
                    if c >= 4:
                        pe.wait_ge(mod_ok, c - 3)
                    for k in range(KD):
                        last = nc.tensor.matmul(K.bank[2 + c % 4][0:2, :], cond[:, k, :], wbuf[c % WB][:, k, :],
                                                start=(k == 0), stop=(k == KD - 1))
                    last.then_inc(mm_ok, 1)
                    if c == 5:
                        pe.wait_ge(mod_ok, 4)
                        for b in range(16):
                            last = nc.tensor.transpose(K.bank[0][:, 2 * b:2 * b + 2], mod[:, b * P:(b + 1) * P],
                                                       K.ident[0:2, 0:2])
                        last.then_inc(mt_ps, 1)


def norm1(K, A):
    nc = K.nc
    ctx = ExitStack()
    with ctx:
        xt = [K.sb(f"n1_x{i}", [P, D], ctx=ctx) for i in range(3)]
        xn = [K.sb(f"n1_xn{i}", [P, D], ctx=ctx) for i in range(2)]
        junk = K.sb("n1_junk", [P, D], ctx=ctx)
        ss = K.sb("n1_ss", [P, 3, TILES], ctx=ctx)
        x_in = [K.sem(f"n1_x_in{i}") for i in range(3)]
        sq_ok = K.sem("n1_sumsq")
        ms_ok = K.sem("n1_meansq")
        rt_ok = K.sem("n1_root")
        rc_ok = K.sem("n1_recip")
        xn_ok = K.sem("n1_xn_ok")
        t_ok = K.sem("n1_transposed")
        d_ok = K.sem("n1_dve_half")
        a_ok = K.sem("n1_act_half")
        with nc.Block() as block:
            @block.sync
            def _(sp):
                for i in range(TILES):
                    if i >= 3:
                        sp.wait_ge(xn_ok, i - 2)
                    src = A["x_sample"][0, i * P:(i + 1) * P, :] if i < 8 else A["x_prompt"][0, :, :]
                    sp.dma_start(xt[i % 3][:, :], src).then_inc(x_in[i % 3], 16)

            @block.scalar
            def _(act):
                def squares(i):
                    act.wait_ge(x_in[i % 3], 16 * (i // 3 + 1))
                    nc.scalar.activation(junk[:, :], xt[i % 3][:, :], ACT.Square,
                                         accum_out=ss[:, 0, i:i + 1]).then_inc(sq_ok, 1)
                    act.wait_ge(ms_ok, i + 1)
                    nc.scalar.activation(ss[:, 1, i:i + 1], ss[:, 2, i:i + 1], ACT.Sqrt).then_inc(rt_ok, 1)
                squares(0)
                for i in range(TILES):
                    if i + 1 < TILES:
                        squares(i + 1)
                    s = 0 if i < 8 else 1
                    act.wait_ge(t_ok, 2 * i + 2)
                    for k in range(4, 8):
                        last = nc.scalar.activation(K.hT[:, k, i * P:(i + 1) * P],
                                                    K.bank[4 + i % 4][:, (k - 4) * P:(k - 3) * P], ACT.Identity,
                                                    scale=K.s1[:, k, s:s + 1], bias=K.modT[:, SH1 * 8 + k, s:s + 1])
                    last.then_inc(a_ok, 1)

            @block.vector
            def _(dve):
                def normalise(i):
                    dve.wait_ge(sq_ok, i + 1)
                    nc.vector.tensor_scalar(ss[:, 2, i:i + 1], ss[:, 0, i:i + 1], 1.0 / D, EPS, ALU.mult,
                                            ALU.add).then_inc(ms_ok, 1)
                    dve.wait_ge(rt_ok, i + 1)
                    nc.vector.reciprocal(ss[:, 0, i:i + 1], ss[:, 1, i:i + 1]).then_inc(rc_ok, 1)
                    dve.wait_ge(rc_ok, i + 1)
                    if i >= 2:
                        dve.wait_ge(t_ok, 2 * (i - 1))
                    nc.vector.tensor_scalar(xn[i % 2][:, :], xt[i % 3][:, :], ss[:, 0, i:i + 1], None,
                                            ALU.mult).then_inc(xn_ok, 1)
                normalise(0)
                for i in range(TILES):
                    if i + 1 < TILES:
                        normalise(i + 1)
                    s = 0 if i < 8 else 1
                    dve.wait_ge(t_ok, 2 * i + 1)
                    for k in range(4):
                        last = nc.vector.tensor_scalar(K.hT[:, k, i * P:(i + 1) * P],
                                                       K.bank[i % 4][:, k * P:(k + 1) * P],
                                                       K.s1[:, k, s:s + 1], K.modT[:, SH1 * 8 + k, s:s + 1],
                                                       ALU.mult, ALU.add)
                    last.then_inc(d_ok, 1)

            @block.tensor
            def _(pe):
                for i in range(TILES):
                    pe.wait_ge(xn_ok, i + 1)
                    if i >= 4:
                        pe.wait_ge(d_ok, i - 3)
                        pe.wait_ge(a_ok, i - 3)
                    for k in range(KD):
                        last = nc.tensor.transpose(K.bank[(0 if k < 4 else 4) + i % 4][:, (k % 4) * P:(k % 4 + 1) * P],
                                                   xn[i % 2][:, k * P:(k + 1) * P], K.ident[:, :])
                        if k % 4 == 3:
                            last.then_inc(t_ok, 1)


def rwkv(K, A):
    nc = K.nc
    ctx = ExitStack()
    PW = NT + 3
    SAMPLE, PROMPT = 1, NS + 2
    LV = 6
    GR = TILES
    BLK = 3 * PAIRS
    with ctx:
        def sb(name, shape, dt=F32):
            return K.sb("r_" + name, shape, dt, ctx=ctx)

        wblk = [sb(f"w{i}", [P, KD, P]) for i in range(2)]
        lora = sb("lora", [P, NT])
        sigg = sb("sigg", [P, NT])
        wup = [sb(f"wup{d}", [P, P]) for d in range(2)]
        gup = sb("gup", [P, P])
        pv = sb("pairvec", [P, 15])
        pc = sb("pairconst", [P, 4])
        lc = sb("loraconst", [P, 2])
        raw = sb("raw", [P, PW])
        r, k, v, kk, kds, t0, t1, sig, aa = (sb(n, [P, NT]) for n in
                                             ("r", "k", "v", "kk", "kds", "t0", "t1", "sig", "aa"))
        R, Q, B, KB = ([sb(f"{n}{d}", [P, NT]) for d in range(2)] for n in "RQBK")
        mid = sb("mid", [P, 2, 2, TILES])
        e1 = sb("e1", [P, 2, TILES])
        e12 = sb("e12", [P, 2, TILES])
        tok = [sb(f"tok{d}", [P, 4, P]) for d in range(2)]
        M = [[sb(f"M{d}{h}", [P, 4, P]) for h in range(2)] for d in range(2)]
        T = [sb(f"T{d}", [P, 2, P]) for d in range(2)]
        W = [sb(f"W{d}", [P, 2, P]) for d in range(2)]
        X = [sb(f"X{d}", [P, 2, P]) for d in range(2)]
        XT = [sb(f"XT{d}", [P, P]) for d in range(2)]
        PV = [sb(f"PV{d}", [P, P]) for d in range(2)]
        U = [sb(f"U{d}", [P, P]) for d in range(2)]
        S = [sb(f"S{d}", [P, P]) for d in range(2)]
        ST = [sb(f"ST{d}", [P, P]) for d in range(2)]
        bank = K.bank

        def sem(name):
            return K.sem("r_" + name)

        w_in = [sem(f"w_in{i}") for i in range(2)]
        up_in, st_in = sem("up_in"), sem("state_in")
        proj = sem("projected")
        rawd = sem("raw_copied")
        shifted = sem("shifted")
        lora_ok = sem("lora_ok")
        v_chain = sem("dve_chain")
        sq_ok, norm_ps, norm_ok, norm_used = sem("ksq_ok"), sem("norm_psum"), sem("norm_ok"), sem("norm_used")
        gate_ps, gate_ok = sem("gate_psum"), sem("gate_ok")
        bonus_in, bonus_ps, y_sum = sem("bonus_in"), sem("bonus_psum"), sem("y_sum")
        mean_ps, centred, sqd = sem("mean_psum"), sem("centred"), sem("y_squared")
        var_ps, root_ok, prep_ok, pair_ok = sem("var_psum"), sem("root_ok"), sem("prep_ok"), sem("pair_ok")
        wg_ps, ag_ps, wg_ok, ag_ok = sem("wgate_psum"), sem("agate_psum"), sem("wgate_ok"), sem("agate_ok")
        exps_in, exps_ok, gates_used = sem("exps_in"), sem("exps_ok"), sem("gates_used")
        st_t = sem("state_transposed")
        st_out, st_st = sem("state_out"), sem("state_stored")
        tr, tr_ok = sem("tokmajor_psum"), sem("tokmajor_ok")
        mm, mm_ok, w0_ok = sem("M_psum"), sem("M_ok"), sem("W0_ok")
        xt, xt_ok, pps, p_ok = sem("XT_psum"), sem("XT_ok"), sem("PV_psum"), sem("PV_ok")
        ups, u_ok, ops, o_ok = sem("U_psum"), sem("U_ok"), sem("Y_psum"), sem("Y_ok")
        sps, s_ok = sem("S_psum"), sem("S_ok")
        tps, tt_ok = sem("T_psum"), sem("T_copied")
        xps, x_ok, yps, y_ok = sem("X_psum"), sem("X_ok"), sem("TX_psum"), sem("TX_ok")
        VL = 76
        w_in_v = A["w_in"].rearrange("l (k p) n -> p (l k) n", p=P)
        NG = 2 * (GR + 1)

        def chunk_of(d, g):
            return g if g == 8 or d == 0 else 7 - g

        with nc.Block() as block:
            @block.sync
            def _(sp):
                for i in range(2):
                    c = (BLK + i) * P
                    sp.dma_start(wblk[i][:, :, :], w_in_v[:, :, c:c + P]).then_inc(w_in[i], 16)
                with sp.Fori(0, PAIRS) as p:
                    for i in range(3):
                        sp.wait_ge(proj, p * 3 + (3 if i == 2 else 2))
                        sp.dma_start(wblk[i % 2][:, :, :],
                                     w_in_v[:, :, bass.ds(p * P + i * DA, P)]).then_inc(w_in[i % 2], 16)
                    sp.wait_ge(pair_ok, p + 1)
                    for d in range(2):
                        sp.dma_start(wup[d][0:HN, :], A["w_up"][0, d, :, bass.ds(p * P, P)]).then_inc(up_in, 16)
                        sp.dma_start(wup[d][HN:P, :], A["a_up"][0, d, :, bass.ds(p * P, P)]).then_inc(up_in, 16)
                    sp.dma_start(gup[:, :], A["g_up"][0, :, bass.ds(p * P, P)]).then_inc(up_in, 16)
                    for d in range(2):
                        for h in range(2):
                            sp.dma_start(ST[d][h * HN:(h + 1) * HN, h * HN:(h + 1) * HN],
                                         A["state_rwkv"][0, 0, d, bass.ds(p * 2 + h, 1), :, :]
                                         .rearrange("a v k -> (a v) k")).then_inc(st_in, 16)
                    sp.wait_ge(st_out, p * 2 + 2)
                    for d in range(2):
                        for h in range(2):
                            sp.dma_start(A["new_s"][0, 0, d, bass.ds(p * 2 + h, 1), :, :]
                                         .rearrange("a v k -> (a v) k"),
                                         ST[d][h * HN:(h + 1) * HN, h * HN:(h + 1) * HN]).then_inc(st_st, 16)
                    K.hold(sp, st_st, p * 64 + 64)

            @block.tensor
            def _(pe):
                def project(buf, first):
                    for c, (at, n) in enumerate(PIECES):
                        for kc in range(KD):
                            last = nc.tensor.matmul(bank[first + c][:, 0:n], wblk[buf][:, kc, :],
                                                    K.hT[:, kc, at:at + n], start=(kc == 0), stop=(kc == KD - 1))
                    last.then_inc(proj, 1)

                def full(lhsT, rhs, first):
                    for c, (at, n) in enumerate(PIECES):
                        last = nc.tensor.matmul(bank[first + c][:, 0:n], lhsT, rhs[:, at:at + n],
                                                start=True, stop=True)
                    return last

                for i in range(2):
                    pe.wait_ge(w_in[i], 16)
                    project(i, 3 * i)
                with pe.Fori(0, PAIRS) as p:
                    pe.wait_ge(pair_ok, p + 1)
                    pe.wait_ge(rawd, p * 3 + 2)
                    pe.wait_ge(w_in[0], p * 32 + 32)
                    project(0, 0)
                    pe.wait_ge(w_in[1], p * 16 + 32)
                    project(1, 3)
                    pe.wait_ge(rawd, p * 3 + 3)
                    pe.wait_ge(w_in[0], p * 32 + 48)
                    project(0, 0)
                    pe.wait_ge(rawd, p * 3 + 4)
                    pe.wait_ge(sq_ok, p + 1)
                    full(K.head_ones[:, :], t0, 3).then_inc(norm_ps, 1)
                    pe.wait_ge(lora_ok, 2)
                    pe.wait_ge(up_in, p * 80 + 80)
                    pe.wait_ge(rawd, p * 3 + 5)
                    for d in range(2):
                        if d:
                            pe.wait_ge(wg_ok, p * 2 + 1)
                        full(wup[d][0:HN, :], lora[0:HN, :], 0).then_inc(wg_ps, 1)
                        if d:
                            pe.wait_ge(ag_ok, p * 2 + 1)
                        else:
                            pe.wait_ge(norm_ok, p + 1)
                        full(wup[d][HN:P, :], lora[HN:P, :], 3).then_inc(ag_ps, 1)
                    pe.wait_ge(st_in, p * 64 + 64)
                    for d in range(2):
                        last = nc.tensor.transpose(bank[6][:, d * P:(d + 1) * P], ST[d][:, :], K.ident[:, :])
                    last.then_inc(st_t, 1)
                    pe.wait_ge(prep_ok, p + 1)
                    pe.wait_ge(s_ok, p * NG + 2)
                    for g in range(GR):
                        def gv(per, i, g=g):
                            return p * (GR * per) + (g * per + i)
                        for d in range(2):
                            at = chunk_of(d, g) * P
                            for q, src in enumerate((Q[d], B[d], KB[d], v)):
                                last = nc.tensor.transpose(bank[6 + d][:, q * P:(q + 1) * P], src[:, at:at + P],
                                                           K.ident[:, :])
                            last.then_inc(tr, 1)
                        if g:
                            pe.wait_ge(o_ok, gv(2, 0))
                        for d in range(2):
                            at = chunk_of(d, g) * P
                            for h in range(2):
                                hs = slice(h * HN, (h + 1) * HN)
                                for q, (a, b) in enumerate(((B, Q), (B, R), (KB, Q), (KB, R))):
                                    last = nc.tensor.matmul(bank[2 * d + h][:, q * P:(q + 1) * P],
                                                            a[d][hs, at:at + P], b[d][hs, at:at + P],
                                                            start=True, stop=True)
                                last.then_inc(mm, 1)
                        pe.wait_ge(s_ok, p * NG + (2 * g + 2))
                        for lev in range(1, LV + 1):
                            for d in range(2):
                                if lev == 1:
                                    pe.wait_ge(w0_ok, gv(2, d + 1))
                                    src = W[d]
                                else:
                                    pe.wait_ge(y_ok, gv(2 * LV, 2 * (lev - 2) + d + 1))
                                    src = T[d]
                                for h in range(2):
                                    last = nc.tensor.transpose(bank[4 + d][:, h * P:(h + 1) * P], src[:, h, :],
                                                               K.ident[:, :])
                                last.then_inc(tps, 1)
                                if lev > 1:
                                    for h in range(2):
                                        last = nc.tensor.matmul(bank[d][:, h * P:(h + 1) * P], M[d][h][:, 0, :],
                                                                T[d][:, h, :], start=True, stop=True)
                                    last.then_inc(xps, 1)
                            if lev == 1:
                                for d in range(2):
                                    pe.wait_ge(tt_ok, gv(2 * LV, d + 1))
                                    for h in range(2):
                                        last = nc.tensor.matmul(bank[d][:, h * P:(h + 1) * P], M[d][h][:, 0, :],
                                                                T[d][:, h, :], start=True, stop=True)
                                    last.then_inc(xps, 1)
                                pe.wait_ge(mm_ok, gv(4, 4))
                            for d in range(2):
                                pe.wait_ge(x_ok, gv(2 * LV, 2 * (lev - 1) + d + 1))
                                pe.wait_ge(tt_ok, gv(2 * LV, 2 * (lev - 1) + d + 1))
                                for h in range(2):
                                    lt, rt = (W[d], X[d]) if lev < LV else (X[d], W[d])
                                    last = nc.tensor.matmul(bank[2 + d][:, h * P:(h + 1) * P], lt[:, h, :],
                                                            rt[:, h, :], start=True, stop=True)
                                last.then_inc(yps, 1)
                        pe.wait_ge(tr_ok, gv(2, 2))
                        for d in range(2):
                            for h in range(2):
                                hs = slice(h * HN, (h + 1) * HN)
                                last = nc.tensor.matmul(bank[7][:, d * P + h * HN:d * P + (h + 1) * HN],
                                                        M[d][h][:, 2, :], tok[d][:, 3, hs], start=True, stop=True)
                            last.then_inc(pps, 1)
                        for d in range(2):
                            pe.wait_ge(y_ok, gv(2 * LV, 2 * (LV - 1) + d + 1))
                            for h in range(2):
                                hs = slice(h * HN, (h + 1) * HN)
                                last = nc.tensor.matmul(bank[6][hs, d * P:(d + 1) * P], tok[d][:, 0, hs],
                                                        W[d][:, h, :], start=True, stop=True)
                            last.then_inc(xt, 1)
                        for d in range(2):
                            pe.wait_ge(s_ok, p * NG + (2 * g + d + 1))
                            pe.wait_ge(xt_ok, gv(2, d + 1))
                            pe.wait_ge(p_ok, gv(2, d + 1))
                            nc.tensor.matmul(bank[d][:, 0:P], XT[d][:, :], S[d][:, :], start=True, stop=False)
                            for h in range(2):
                                hs = slice(h * HN, (h + 1) * HN)
                                last = nc.tensor.matmul(bank[d][:, hs], W[d][:, h, :], PV[d][:, hs],
                                                        start=False, stop=(h == 1))
                            last.then_inc(ups, 1)
                        for d in range(2):
                            at = chunk_of(d, g) * P
                            nc.tensor.matmul(bank[2 + d][:, 0:P], S[d][:, :], R[d][:, at:at + P],
                                             start=True, stop=False)
                            for h in range(2):
                                hs = slice(h * HN, (h + 1) * HN)
                                nc.tensor.matmul(bank[2 + d][hs, 0:P], tok[d][:, 3, hs], M[d][h][:, 3, :],
                                                 start=False, stop=False)
                            pe.wait_ge(u_ok, gv(2, d + 1))
                            for h in range(2):
                                hs = slice(h * HN, (h + 1) * HN)
                                last = nc.tensor.matmul(bank[2 + d][hs, 0:P], U[d][:, hs], M[d][h][:, 1, :],
                                                        start=False, stop=True)
                            last.then_inc(ops, 1)
                            nc.tensor.matmul(bank[4 + d][:, 0:P], tok[d][:, 1, :], U[d][:, :],
                                             start=True, stop=False)
                            nc.tensor.matmul(bank[4 + d][:, 0:P], tok[d][:, 2, :], tok[d][:, 3, :],
                                             start=False, stop=True).then_inc(sps, 1)
                    pe.wait_ge(s_ok, p * NG + NG)
                    for d in range(2):
                        last = nc.tensor.transpose(bank[6][:, d * P:(d + 1) * P], S[d][:, :], K.ident[:, :])
                    last.then_inc(st_t, 1)
                    pe.wait_ge(o_ok, p * (2 * GR) + 2 * GR)
                    full(gup[:, :], sigg, 0).then_inc(gate_ps, 1)
                    pe.wait_ge(bonus_in, p + 1)
                    full(K.head_ones[:, :], aa, 3).then_inc(bonus_ps, 1)
                    pe.wait_ge(y_sum, p + 1)
                    pe.wait_ge(gate_ok, p + 1)
                    full(K.head_ones[:, :], t0, 0).then_inc(mean_ps, 1)
                    pe.wait_ge(sqd, p + 1)
                    full(K.head_ones[:, :], t1, 3).then_inc(var_ps, 1)

            @block.scalar
            def _(act):
                def copy_raw(first):
                    for c, (at, m) in enumerate(PIECES):
                        dst = at + SAMPLE if at < NS else PROMPT
                        last = nc.scalar.activation(raw[:, dst:dst + m], bank[first + c][:, 0:m], ACT.Copy)
                    last.then_inc(rawd, 1)

                def full(out, first, func, **kw):
                    for c, (at, m) in enumerate(PIECES):
                        last = nc.scalar.activation(out[:, at:at + m], bank[first + c][:, 0:m], func, **kw)
                    return last

                def flat(ap):
                    return ap.rearrange("p a b -> p (a b)")

                act.wait_ge(shifted, 1)
                act.wait_ge(proj, 1)
                copy_raw(0)
                act.wait_ge(shifted, 2)
                nc.scalar.activation(lora[0:HN, :], lora[0:HN, :], ACT.Tanh).then_inc(lora_ok, 1)
                act.wait_ge(proj, 2)
                copy_raw(3)
                act.wait_ge(shifted, 3)
                nc.scalar.activation(sigg[:, :], sigg[:, :], ACT.Sigmoid).then_inc(lora_ok, 1)
                with act.Fori(0, PAIRS) as p:
                    for i in range(3):
                        act.wait_ge(proj, p * 3 + (3 + i))
                        act.wait_ge(shifted, p * 3 + (3 + i))
                        copy_raw(3 if i == 1 else 0)
                    act.wait_ge(norm_ps, p + 1)
                    full(sig, 3, ACT.Sqrt, bias=K.eps[:, 1:2]).then_inc(norm_ok, 1)
                    act.wait_ge(norm_used, p + 1)
                    for d in range(2):
                        if d:
                            act.wait_ge(gates_used, p * 2 + 1)
                        act.wait_ge(wg_ps, p * 2 + (d + 1))
                        full(sig, 0, ACT.Sigmoid, bias=pv[:, 6 + d:7 + d]).then_inc(wg_ok, 1)
                        act.wait_ge(ag_ps, p * 2 + (d + 1))
                        full(aa, 3, ACT.Sigmoid, bias=pv[:, 8 + d:9 + d]).then_inc(ag_ok, 1)
                        act.wait_ge(exps_in, p * 2 + (d + 1))
                        nc.scalar.activation(R[d][:, :], t0[:, :], ACT.Exp, scale=-DECAY)
                        nc.scalar.activation(Q[d][:, :], t1[:, :], ACT.Exp, scale=-DECAY)
                        nc.scalar.activation(B[d][:, :], t0[:, :], ACT.Exp, scale=DECAY)
                        nc.scalar.activation(e1[:, d, :], mid[:, d, 0, :], ACT.Exp, scale=-DECAY)
                        nc.scalar.activation(e12[:, d, :], mid[:, d, 1, :], ACT.Exp,
                                             scale=-DECAY).then_inc(exps_ok, 1)
                    for g in range(GR):
                        def gv(per, i, g=g):
                            return p * (GR * per) + (g * per + i)
                        for d in range(2):
                            act.wait_ge(tr, gv(2, d + 1))
                            nc.scalar.activation(flat(tok[d][:, :, :]), bank[6 + d][:, :], ACT.Copy).then_inc(tr_ok, 1)
                        for lev in range(1, LV + 1):
                            for d in range(2):
                                act.wait_ge(tps, gv(2 * LV, 2 * (lev - 1) + d + 1))
                                dst = T[d] if lev == 1 else W[d]
                                nc.scalar.activation(flat(dst[:, :, :]), bank[4 + d][:, 0:2 * P],
                                                     ACT.Copy).then_inc(tt_ok, 1)
                        act.wait_ge(xt, gv(2, 2))
                        for d in range(2):
                            nc.scalar.activation(XT[d][:, :], bank[6][:, d * P:(d + 1) * P],
                                                 ACT.Copy).then_inc(xt_ok, 1)
                        for d in range(2):
                            act.wait_ge(ops, gv(2, d + 1))
                            at = chunk_of(d, g) * P
                            nc.scalar.activation((t0, t1)[d][:, at:at + P], bank[2 + d][:, 0:P],
                                                 ACT.Copy).then_inc(o_ok, 1)
                    act.wait_ge(gate_ps, p + 1)
                    full(sig, 0, ACT.Copy).then_inc(gate_ok, 1)
                    act.wait_ge(centred, p + 1)
                    nc.scalar.activation(t1[:, :], t0[:, :], ACT.Square).then_inc(sqd, 1)
                    act.wait_ge(var_ps, p + 1)
                    full(kk, 3, ACT.Sqrt, bias=K.eps[:, 2:3], scale=1.0 / HN).then_inc(root_ok, 1)

            @block.vector
            def _(dve):
                link = Link(dve, v_chain)
                V = nc.vector
                V.memset(raw[:, :], 0.0).then_inc(shifted, 1)
                V.memset(ST[0][:, :], 0.0)
                V.memset(ST[1][:, :], 0.0).then_inc(pair_ok, 1)
                link(V.tensor_tensor(lc[:, :], K.vecT[:, V_MUPL:V_MUPL + 2], K.vecT[:, V_MUNL:V_MUNL + 2], ALU.add))
                link(V.tensor_scalar(lc[:, :], lc[:, :], -1.0, 1.0, ALU.mult, ALU.add))

                def shift(out, c0, mp, mn):
                    for s, at, n in ((SAMPLE, 0, NS), (PROMPT, NS, NP)):
                        last = V.tensor_scalar(out[:, at:at + n], raw[:, s:s + n], c0, None, ALU.mult)
                    link(last)
                    for s, at, n in ((SAMPLE, 0, NS), (PROMPT, NS, NP)):
                        last = V.scalar_tensor_tensor(out[:, at:at + n], raw[:, s - 1:s - 1 + n], mp,
                                                      out[:, at:at + n], ALU.mult, ALU.add)
                    link(last)
                    for s, at, n in ((SAMPLE, 0, NS), (PROMPT, NS, NP)):
                        last = V.scalar_tensor_tensor(out[:, at:at + n], raw[:, s + 1:s + 1 + n], mn,
                                                      out[:, at:at + n], ALU.mult, ALU.add)
                    last.then_inc(shifted, 1)

                for i, out in enumerate((lora, sigg)):
                    dve.wait_ge(rawd, i + 1)
                    shift(out, lc[:, i:i + 1], K.vecT[:, V_MUPL + i:V_MUPL + i + 1],
                          K.vecT[:, V_MUNL + i:V_MUNL + i + 1])
                tot = lambda ap, at: ap[:, :].rearrange("p (c t) -> p c t", t=P)[:, :, at:at + 1]
                wide = lambda ap: ap[:, :].rearrange("p (c t) -> p c t", t=P)
                with dve.Fori(0, PAIRS) as p:
                    link.enter(p, VL)
                    link(V.tensor_copy(pv[:, :], K.vecT[:, 0:60].rearrange("p (v q) -> p v q", q=PAIRS)
                                       [:, :, bass.ds(p, 1)].rearrange("p v q -> p (v q)")))
                    link(V.tensor_tensor(pc[:, 0:3], pv[:, 0:3], pv[:, 3:6], ALU.add))
                    link(V.tensor_scalar(pc[:, 0:3], pc[:, 0:3], -1.0, 1.0, ALU.mult, ALU.add))
                    link(V.tensor_scalar(pc[:, 3:4], pv[:, 11:12], -1.0, 1.0, ALU.mult, ALU.add))
                    for i, out in enumerate((r, k, v)):
                        dve.wait_ge(rawd, p * 3 + (3 + i))
                        shift(out, pc[:, i:i + 1], pv[:, i:i + 1], pv[:, 3 + i:4 + i])
                        dve.wait_ge(shifted, p * 3 + (4 + i))
                        if i == 1:
                            link(V.tensor_scalar(kk[:, :], k[:, :], pv[:, 10:11], None, ALU.mult))
                            V.tensor_tensor(t0[:, :], kk[:, :], kk[:, :], ALU.mult).then_inc(sq_ok, 1)
                    dve.wait_ge(norm_ok, p + 1)
                    V.reciprocal(t1[:, :], sig[:, :]).then_inc(norm_used, 1)
                    dve.wait_ge(norm_used, p + 1)
                    link(V.tensor_tensor(kk[:, :], kk[:, :], t1[:, :], ALU.mult))
                    for d in range(2):
                        dve.wait_ge(wg_ok, p * 2 + (d + 1))
                        link(V.tensor_tensor_scan(t0[:, :], K.scan_keep[:, :], sig[:, :], 0.0, ALU.mult, ALU.add))
                        if d:
                            link(V.tensor_tensor(t1[:, :], sig[:, :], t0[:, :], ALU.subtract))
                            link(V.tensor_tensor(wide(t1), wide(t1), tot(t0, P - 1).broadcast_to([P, TILES, P]), ALU.add))
                            cs, mi, to = t1, P // 2, 0
                        else:
                            cs, mi, to = t0, P // 2 - 1, P - 1
                        V.tensor_copy(mid[:, d, 0, :].unsqueeze(2), tot(cs, mi))
                        link(V.tensor_tensor(mid[:, d, 1, :].unsqueeze(2), tot(cs, to), tot(cs, mi), ALU.subtract))
                        if d == 0:
                            link(V.tensor_tensor(mid[:, d, 1, 0:7], mid[:, d, 1, 0:7], mid[:, d, 0, 1:8], ALU.add))
                        else:
                            link(V.tensor_tensor(mid[:, d, 1, 1:8], mid[:, d, 1, 1:8], mid[:, d, 0, 0:7], ALU.add))
                        link(V.tensor_tensor(wide(t0), wide(cs), mid[:, d, 0, :].unsqueeze(2).broadcast_to([P, TILES, P]),
                                             ALU.subtract))
                        V.tensor_tensor(t1[:, :], t0[:, :], sig[:, :], ALU.subtract).then_inc(exps_in, 1)
                        dve.wait_ge(exps_ok, p * 2 + (d + 1))
                        link(V.tensor_tensor(KB[d][:, :], B[d][:, :], k[:, :], ALU.mult))
                        link(V.tensor_tensor(B[d][:, :], B[d][:, :], kk[:, :], ALU.mult))
                        link(V.tensor_tensor(B[d][:, :], B[d][:, :], aa[:, :], ALU.mult))
                        link(V.tensor_tensor(R[d][:, :], R[d][:, :], r[:, :], ALU.mult))
                        link(V.tensor_tensor(Q[d][:, :], Q[d][:, :], kk[:, :], ALU.mult))
                        link(V.tensor_scalar(aa[:, :], aa[:, :], pv[:, 11:12], pc[:, 3:4], ALU.mult, ALU.add))
                        link(V.tensor_tensor(KB[d][:, :], KB[d][:, :], aa[:, :], ALU.mult))
                        if d == 0:
                            V.tensor_copy(kds[:, :], aa[:, :]).then_inc(gates_used, 1)
                        else:
                            V.tensor_tensor(kds[:, :], kds[:, :], aa[:, :], ALU.add).then_inc(gates_used, 1)
                        dve.wait_ge(gates_used, p * 2 + (d + 1))
                    V.memset(pc[:, 0:1], 0.0).then_inc(prep_ok, 1)
                    dve.wait_ge(st_t, p * 2 + 1)
                    for d in range(2):
                        c = chunk_of(d, 0)
                        V.tensor_scalar(S[d][:, :], bank[6][:, d * P:(d + 1) * P], e1[:, d, c:c + 1], None,
                                        ALU.mult).then_inc(s_ok, 1)
                    for g in range(GR):
                        def gv(per, i, g=g):
                            return p * (GR * per) + (g * per + i)
                        for d in range(2):
                            for h in range(2):
                                dve.wait_ge(mm, gv(4, 2 * d + h + 1))
                                V.tensor_tensor(M[d][h][:, :, :], bank[2 * d + h][:, :].rearrange("p (q t) -> p q t", t=P),
                                                K.causal[:, d, :, :], ALU.mult).then_inc(mm_ok, 1)
                        for d in range(2):
                            dve.wait_ge(mm_ok, gv(4, 2 * d + 2))
                            for h in range(2):
                                last = V.scalar_tensor_tensor(W[d][:, h, :], M[d][h][:, 0, :], -1.0,
                                                              K.level[:, 1 - d, 0, :], ALU.mult, ALU.mult)
                            link(last)
                            V.tensor_tensor(W[d][:, :, :], W[d][:, :, :],
                                            K.ident[:, :].unsqueeze(1).broadcast_to([P, 2, P]), ALU.add).then_inc(w0_ok, 1)
                        for lev in range(1, LV + 1):
                            for d in range(2):
                                dve.wait_ge(xps, gv(2 * LV, 2 * (lev - 1) + d + 1))
                                V.tensor_tensor(X[d][:, :, :], bank[d][:, 0:2 * P].rearrange("p (h t) -> p h t", t=P),
                                                K.level[:, d, lev, :].unsqueeze(1).broadcast_to([P, 2, P]),
                                                ALU.mult).then_inc(x_ok, 1)
                            for d in range(2):
                                dve.wait_ge(yps, gv(2 * LV, 2 * (lev - 1) + d + 1))
                                dst = T[d] if lev < LV else W[d]
                                V.tensor_tensor(dst[:, :, :], dst[:, :, :],
                                                bank[2 + d][:, 0:2 * P].rearrange("p (h t) -> p h t", t=P),
                                                ALU.subtract).then_inc(y_ok, 1)
                        for d in range(2):
                            dve.wait_ge(pps, gv(2, 2))
                            V.tensor_copy(PV[d][:, :], bank[7][:, d * P:(d + 1) * P]).then_inc(p_ok, 1)
                        for d in range(2):
                            dve.wait_ge(ups, gv(2, d + 1))
                            V.tensor_scalar(U[d][:, :], bank[d][:, 0:P], -1.0, None, ALU.mult).then_inc(u_ok, 1)
                        for d in range(2):
                            c = chunk_of(d, g)
                            dve.wait_ge(sps, gv(2, d + 1))
                            if g == GR - 2:
                                V.memset(S[d][:, :], 0.0).then_inc(s_ok, 1)
                                continue
                            V.tensor_scalar(S[d][:, :], S[d][:, :], e12[:, d, c:c + 1], None, ALU.mult)
                            link(V.scalar_tensor_tensor(ST[d][:, :], bank[4 + d][:, 0:P], e12[:, d, c:c + 1],
                                                        K.head_mask[:, :], ALU.mult, ALU.mult))
                            V.tensor_tensor(S[d][:, :], S[d][:, :], ST[d][:, :], ALU.add).then_inc(s_ok, 1)
                    dve.wait_ge(st_t, p * 2 + 2)
                    for d in range(2):
                        V.tensor_copy(ST[d][:, :], bank[6][:, d * P:(d + 1) * P]).then_inc(st_out, 1)
                    link(V.tensor_tensor(kds[:, :], kds[:, :], k[:, :], ALU.mult))
                    V.scalar_tensor_tensor(aa[:, :], r[:, :], pv[:, 12:13], kds[:, :], ALU.mult,
                                           ALU.mult).then_inc(bonus_in, 1)
                    dve.wait_ge(bonus_ps, p + 1)
                    for c, (at, n) in enumerate(PIECES):
                        last = V.tensor_tensor(kds[:, at:at + n], v[:, at:at + n], bank[3 + c][:, 0:n], ALU.mult)
                    link(last)
                    dve.wait_ge(o_ok, p * (2 * GR) + 2 * GR)
                    V.tensor_tensor(t0[:, :], t0[:, :], t1[:, :], ALU.add).then_inc(y_sum, 1)
                    dve.wait_ge(mean_ps, p + 1)
                    for c, (at, n) in enumerate(PIECES):
                        last = V.scalar_tensor_tensor(t0[:, at:at + n], bank[c][:, 0:n], -1.0 / HN, t0[:, at:at + n],
                                                      ALU.mult, ALU.add)
                    last.then_inc(centred, 1)
                    dve.wait_ge(root_ok, p + 1)
                    link(V.reciprocal(t1[:, :], kk[:, :]))
                    link(V.tensor_tensor(t0[:, :], t0[:, :], t1[:, :], ALU.mult))
                    link(V.tensor_scalar(t0[:, :], t0[:, :], pv[:, 13:14], pv[:, 14:15], ALU.mult, ALU.add))
                    link(V.tensor_tensor(t0[:, :], t0[:, :], kds[:, :], ALU.add))
                    V.tensor_tensor(K.yA[:, bass.ds(p, 1), :].rearrange("p a t -> p (a t)"), t0[:, :], sig[:, :],
                                    ALU.mult).then_inc(pair_ok, 1)
                    link.leave(PAIRS)


def attention(K, A):
    nc = K.nc
    ctx = ExitStack()
    ROWS = NS // GRID
    SLOTS = 2 * WR
    TABW = P
    HD = HEADS * (2 * WR - 1)
    units = []
    for u in range(ROWS // 2):
        even, odd = (min(max(x - WR // 2, 0), ROWS - WR) for x in (2 * u, 2 * u + 1))
        nrows = odd + WR - even
        units.append((u, even, nrows, even - 2 * u + WR - 1))
    units.append((ROWS // 2, None, 0, 0))
    seq = [(u, h) for u in units for h in range(2)]
    NU = len(seq)
    with ctx:
        def sb(name, shape, dt=F32):
            return K.sb("t_" + name, shape, dt, ctx=ctx)

        def sem(name):
            return K.sem("t_" + name)

        wblk = [sb(f"w{i}", [P, KD, P]) for i in range(3)]
        q, k, v = (sb(n, [P, NT]) for n in "qkv")
        vtok = sb("vtok", [P, TILES, P])
        kout = sb("kout", [P, P])
        ckrow = sb("ckrow", [P, P])
        ck = sb("ck", [P, P])
        cv = sb("cv", [P, P])
        prow = sb("prow", [HD, TABW])
        tab = sb("tab", [P, 2, SLOTS, GRID])
        tab9 = sb("tab9", [P, 2, WR + 1, GRID])
        s = [sb(f"s{i}", [P, 704]) for i in range(2)]
        pr = [sb(f"p{i}", [P, 704]) for i in range(3)]
        pt = [sb(f"pt{i}", [P, 6, P]) for i in range(2)]
        st = sb("stats", [P, 3, NU])
        bank = K.bank
        w_in = [sem(f"w_in{i}") for i in range(3)]
        c_in = sem("cache_in")
        rp_in, sp_ok, tab_in, tab_ok, tab_base = sem("rpb_in"), sem("spread_ok"), sem("tab_in"), sem("tab_ok"), sem("prow_ok")
        proj, t_ps, t_ok = sem("proj"), sem("tok_psum"), sem("tok_ok")
        q_ok, k_ok, v_ok = sem("q_ok"), sem("k_ok"), sem("v_ok")
        kv_st = sem("kv_stored")
        v_chain, g_chain = sem("dve_chain"), sem("pool_chain")
        s_ps, s_ok, m_ok, e_ok = sem("score_psum"), sem("score_ok"), sem("max_ok"), sem("exp_ok")
        r_ok, n_ok, pt_ps, pta_ok, ptv_ok = (sem(n) for n in ("recip_ok", "probs_ok", "PT_psum", "PT_act", "PT_dve"))
        o_ps, o_ok = sem("O_psum"), sem("O_ok")
        pair_ok = sem("pair_ok")
        w_in_v = A["w_in"].rearrange("l (k p) n -> p (l k) n", p=P)
        L = HD * TABW

        def table(u, h):
            _, even, nrows, slot = u
            if nrows == WR + 1:
                return tab9[:, h, :, :].rearrange("p r c -> p (r c)")
            return tab[:, h, slot:slot + WR, :].rearrange("p r c -> p (r c)")

        with nc.Block() as block:
            @block.sync
            def _(sp):
                sp.wait_ge(tab_base, 1)
                sp.dma_start(prow[:, 48:48 + 2 * WC - 1],
                             A["rpb"].rearrange("l h a b -> (l h a) b")).then_inc(rp_in, 16)
                sp.wait_ge(rp_in, 16)
                sp.dma_start(bass.AP(tensor=K.dram["spread"].tensor, offset=0, ap=[[TABW, HD], [L, GRID], [1, TABW]]),
                             prow[:, :].unsqueeze(1).broadcast_to([HD, GRID, TABW])).then_inc(sp_ok, 16)
                sp.wait_ge(sp_ok, 16)
                with sp.Fori(0, PAIRS) as p:
                    sp.wait_ge(proj, p * 3 + 1)
                    for i in range(3):
                        sp.dma_start(wblk[i][:, :, :], w_in_v[:, :, bass.ds(p * P + (ACOLS + i * DA), P)])\
                          .then_inc(w_in[i], 16)
                    K.hold(sp, pair_ok, p + 1)
                    sp.dma_start(ckrow[:, :], A["cache_na_k"].rearrange("a b t h n -> (a b t) (h n)")
                                 [:, bass.ds(p * P, P)]).then_inc(c_in, 16)
                    sp.dma_start(cv[:, :], A["cache_na_v"].rearrange("a b t h n -> (a b t) (h n)")
                                 [:, bass.ds(p * P, P)]).then_inc(c_in, 16)
                    sv = bass.AP(tensor=K.dram["spread"].tensor, offset=GRID - 1,
                                 ap=[[L - 1, GRID], [TABW, HD], [1, GRID]])
                    for h in range(2):
                        for half in range(2):
                            sp.dma_start(tab[half * GRID:(half + 1) * GRID, h, half:half + SLOTS - 1, :],
                                         sv[:, bass.ds(p * 2 * (SLOTS - 1) + h * (SLOTS - 1), SLOTS - 1), :])\
                              .then_inc(tab_in, 16)
                    sp.wait_ge(t_ok, p * 3 + 3)
                    sp.dma_start(A["new_v"].rearrange("a b t h n -> (a b t) (h n)")[:, bass.ds(p * P, P)],
                                 vtok[:, TILES - 1, :]).then_inc(kv_st, 16)
                    sp.dma_start(A["new_k"].rearrange("a b t h n -> (a b t) (h n)")[:, bass.ds(p * P, P)],
                                 kout[:, :]).then_inc(kv_st, 16)
                    K.hold(sp, kv_st, p * 32 + 32)

            @block.gpsimd
            def _(pool):
                link = Link(pool, g_chain, K)
                pool.memset(prow[:, :], 0.0).then_inc(tab_base, 1)
                with pool.Fori(0, PAIRS) as p:
                    link.enter(p, 9)
                    K.hold(pool, tab_in, p * 64 + 64)
                    for half in range(2):
                        rows = slice(half * GRID, (half + 1) * GRID)
                        at = (SLOTS - 1) * (1 - half)
                        link(pool.memset(tab[rows, :, at:at + 1, :], NEG))
                    for half in range(2):
                        t = tab[half * GRID:(half + 1) * GRID, :, :, :].rearrange("p h r c -> p (h r) c")
                        link(pool.affine_select(out=t[:, :, 0:GRID - WC], in_=t[:, :, 0:GRID - WC],
                                                  compare_op=ALU.is_ge, fill=NEG, base=WC // 2,
                                                  pattern=[[0, 2 * SLOTS], [1, GRID - WC]], channel_multiplier=-1))
                    for half in range(2):
                        t = tab[half * GRID:(half + 1) * GRID, :, :, :].rearrange("p h r c -> p (h r) c")
                        link(pool.affine_select(out=t[:, :, WC:GRID], in_=t[:, :, WC:GRID],
                                                  compare_op=ALU.is_ge, fill=NEG, base=WC // 2 - 1 - WC,
                                                  pattern=[[0, 2 * SLOTS], [-1, GRID - WC]], channel_multiplier=1))
                    link(pool.tensor_copy(tab9[0:GRID, :, 0:WR, :], tab[0:GRID, :, 3:3 + WR, :]))
                    link(pool.tensor_copy(tab9[GRID:P, :, 1:WR + 1, :], tab[GRID:P, :, 4:4 + WR, :]))
                    link(pool.memset(tab9[0:GRID, :, WR:WR + 1, :], NEG))
                    pool.memset(tab9[GRID:P, :, 0:1, :], NEG).then_inc(tab_ok, 1)
                    K.hold(pool, tab_ok, p + 1)
                    K.hold(pool, pair_ok, p + 2)
                    link.leave(PAIRS)

            @block.tensor
            def _(pe):
                with pe.Fori(0, PAIRS) as p:
                    pe.wait_ge(pair_ok, p + 1)
                    for i in range(3):
                        pe.wait_ge(w_in[i], p * 16 + 16)
                        if i == 2:
                            pe.wait_ge(q_ok, p + 1)
                        first = 0 if i != 1 else 3
                        for c, (at, n) in enumerate(PIECES):
                            for kc in range(KD):
                                last = nc.tensor.matmul(bank[first + c][:, 0:n], wblk[i][:, kc, :],
                                                        K.hT[:, kc, at:at + n], start=(kc == 0), stop=(kc == KD - 1))
                        last.then_inc(proj, 1)
                    pe.wait_ge(k_ok, p + 1)
                    pe.wait_ge(v_ok, p + 1)
                    pe.wait_ge(c_in, p * 32 + 32)
                    for t in range(TILES):
                        last = nc.tensor.transpose(bank[3 + t // 4][:, (t % 4) * P:(t % 4 + 1) * P],
                                                   v[:, t * P:(t + 1) * P], K.ident[:, :])
                    nc.tensor.transpose(bank[5][:, P:2 * P], k[:, NS:NT], K.ident[:, :])
                    nc.tensor.transpose(bank[5][:, 2 * P:3 * P], ckrow[:, :], K.ident[:, :]).then_inc(t_ps, 1)
                    pe.wait_ge(t_ok, p * 3 + 3)

                    def scores(i):
                        (u, even, nrows, _), h = seq[i]
                        hs = slice(h * HN, (h + 1) * HN)
                        a, b = bank[2 * (i % 2)], bank[2 * (i % 2) + 1]
                        if i >= 2:
                            pe.wait_ge(s_ok, p * NU + (i - 1))
                        qs = q[hs, u * P:(u + 1) * P]
                        if even is None:
                            last = nc.tensor.matmul(a[:, 0:P], qs, k[hs, NS:NT], start=True, stop=True)
                        else:
                            at = even * GRID
                            nc.tensor.matmul(a[:, :], qs, k[hs, at:at + 512], start=True, stop=True)
                            last = nc.tensor.matmul(b[:, 0:P], qs, ck[hs, :], start=True, stop=True)
                            if nrows > WR:
                                last = nc.tensor.matmul(b[:, P:P + GRID], qs, k[hs, at + 512:at + 576],
                                                        start=True, stop=True)
                        last.then_inc(s_ps, 1)

                    def blocks(i):
                        (u, even, nrows, _), h = seq[i]
                        hs = slice(h * HN, (h + 1) * HN)
                        if even is None:
                            return [(0, P, vtok[:, TILES - 1, hs], 0)]
                        t = even // 2
                        out = [(P * (b + 1), P, vtok[:, t + b, hs], b) for b in range(4)] + [(0, P, cv[:, hs], 4)]
                        if nrows > WR:
                            out.append((P * 5, GRID, vtok[0:GRID, t + 4, hs], 5))
                        return out

                    def turned(i):
                        pe.wait_ge(n_ok, p * NU + (i + 1))
                        if i:
                            pe.wait_ge(pta_ok, p * NU + i)
                            pe.wait_ge(ptv_ok, p * NU + i)
                        for at, n, _, b in blocks(i):
                            last = nc.tensor.transpose(bank[4 + b // 4][0:n, (b % 4) * P:(b % 4 + 1) * P],
                                                       pr[i % 3][:, at:at + n], K.ident[:, :])
                        last.then_inc(pt_ps, 1)

                    def weighted(i):
                        h = seq[i][1]
                        hs = slice(h * HN, (h + 1) * HN)
                        pe.wait_ge(pta_ok, p * NU + (i + 1))
                        pe.wait_ge(ptv_ok, p * NU + (i + 1))
                        if i >= 2:
                            pe.wait_ge(o_ok, p * NU + (i - 1))
                        todo = blocks(i)
                        for j, (at, n, vals, b) in enumerate(todo):
                            last = nc.tensor.matmul(bank[6 + h][hs, 0:P], vals, pt[i % 2][0:n, b, :],
                                                    start=(j == 0), stop=(j == len(todo) - 1))
                        last.then_inc(o_ps, 1)

                    scores(0)
                    scores(1)
                    scores(2)
                    turned(0)
                    for i in range(NU):
                        if i + 3 < NU:
                            scores(i + 3)
                        if i + 1 < NU:
                            turned(i + 1)
                        weighted(i)

            @block.scalar
            def _(act):
                with act.Fori(0, PAIRS) as p:
                    act.wait_ge(proj, p * 3 + 3)
                    for c, (at, n) in enumerate(PIECES):
                        last = nc.scalar.activation(k[:, at:at + n], bank[3 + c][:, 0:n], ACT.Copy)
                    last.then_inc(k_ok, 1)
                    act.wait_ge(t_ps, p + 1)
                    nc.scalar.activation(vtok[:, 0:4, :].rearrange("p a b -> p (a b)"), bank[3][:, :],
                                         ACT.Copy).then_inc(t_ok, 1)

                    def exponentials(i):
                        (_, even, nrows, _), _ = seq[i]
                        n = P if even is None else nrows * GRID + P
                        act.wait_ge(m_ok, p * NU + (i + 1))
                        if i >= 3:
                            act.wait_ge(pt_ps, p * NU + (i - 2))
                        nc.scalar.activation(pr[i % 3][:, 0:n], s[i % 2][:, 0:n], ACT.Exp, bias=st[:, 0, i:i + 1],
                                             accum_out=st[:, 1, i:i + 1]).then_inc(e_ok, 1)

                    def turned(i):
                        act.wait_ge(pt_ps, p * NU + (i + 1))
                        w = P if seq[i][0][1] is None else 512
                        nc.scalar.activation(pt[i % 2][:, 0:w // P, :].rearrange("p a b -> p (a b)"), bank[4][:, 0:w],
                                             ACT.Copy).then_inc(pta_ok, 1)

                    def normalised(i):
                        (_, even, nrows, _), _ = seq[i]
                        n = P if even is None else nrows * GRID + P
                        act.wait_ge(r_ok, p * NU + (i + 1))
                        nc.scalar.activation(pr[i % 3][:, 0:n], pr[i % 3][:, 0:n], ACT.Copy,
                                             scale=st[:, 2, i:i + 1]).then_inc(n_ok, 1)

                    def heads_out(i):
                        (u, _, _, _), h = seq[i]
                        hs = slice(h * HN, (h + 1) * HN)
                        act.wait_ge(o_ps, p * NU + (i + 1))
                        nc.scalar.activation(K.yB[hs, bass.ds(p, 1), u * P:(u + 1) * P].rearrange("p a t -> p (a t)"),
                                             bank[6 + h][hs, 0:P], ACT.Copy).then_inc(o_ok, 1)

                    exponentials(0)
                    exponentials(1)
                    normalised(0)
                    exponentials(2)
                    normalised(1)
                    turned(0)
                    for i in range(NU):
                        if i + 2 < NU:
                            normalised(i + 2)
                        if i:
                            heads_out(i - 1)
                        if i + 1 < NU:
                            turned(i + 1)
                        if i + 3 < NU:
                            exponentials(i + 3)
                    heads_out(NU - 1)

            @block.vector
            def _(dve):
                V = nc.vector
                link = Link(dve, v_chain)
                link(V.memset(st[:, :, :], 0.0))
                V.memset(st[:, 0, 0:1], 0.0).then_inc(proj, 1)
                V.memset(st[:, 0, 1:2], 0.0).then_inc(pair_ok, 1)
                with dve.Fori(0, PAIRS) as p:
                    dve.wait_ge(proj, p * 3 + 2)
                    for c, (at, n) in enumerate(PIECES):
                        last = V.tensor_scalar(q[:, at:at + n], bank[c][:, 0:n], SCALE, None, ALU.mult)
                    last.then_inc(q_ok, 1)
                    dve.wait_ge(proj, p * 3 + 4)
                    for c, (at, n) in enumerate(PIECES):
                        last = V.tensor_copy(v[:, at:at + n], bank[c][:, 0:n])
                    last.then_inc(v_ok, 1)
                    dve.wait_ge(t_ps, p + 1)
                    V.tensor_copy(vtok[:, 4:8, :].rearrange("p a b -> p (a b)"), bank[4][:, :]).then_inc(t_ok, 1)
                    V.tensor_copy(vtok[:, 8, :], bank[5][:, 0:P])
                    V.tensor_copy(kout[:, :], bank[5][:, P:2 * P])
                    V.tensor_copy(ck[:, :], bank[5][:, 2 * P:3 * P]).then_inc(t_ok, 1)
                    dve.wait_ge(tab_ok, p + 1)

                    def biased(i):
                        (u, even, nrows, slot), h = seq[i]
                        a, b, out = bank[2 * (i % 2)], bank[2 * (i % 2) + 1], s[i % 2]
                        dve.wait_ge(s_ps, p * NU + (i + 1))
                        if i >= 2:
                            dve.wait_ge(e_ok, p * NU + (i - 1))
                        if even is None:
                            n = P
                            V.tensor_copy(out[:, 0:P], a[:, 0:P]).then_inc(s_ok, 1)
                        else:
                            n = P + nrows * GRID
                            t = table(seq[i][0], h)
                            V.tensor_tensor(out[:, P:P + 512], a[:, :], t[:, 0:512], ALU.add)
                            if nrows > WR:
                                V.tensor_tensor(out[:, P + 512:n], b[:, P:P + GRID], t[:, 512:576], ALU.add)
                            V.tensor_copy(out[:, 0:P], b[:, 0:P]).then_inc(s_ok, 1)
                        dve.wait_ge(s_ok, p * NU + (i + 1))
                        V.tensor_reduce(st[:, 0, i:i + 1], out[:, 0:n], AX.X, ALU.max, negate=True).then_inc(m_ok, 1)

                    def turned(i):
                        (_, even, nrows, _), _ = seq[i]
                        dve.wait_ge(pt_ps, p * NU + (i + 1))
                        if even is None:
                            V.memset(st[0:1, 0, 0:1], 0.0).then_inc(ptv_ok, 1)
                        else:
                            if nrows > WR:
                                V.tensor_copy(pt[i % 2][0:GRID, 5, :], bank[5][0:GRID, P:2 * P])
                            V.tensor_copy(pt[i % 2][:, 4, :], bank[5][:, 0:P]).then_inc(ptv_ok, 1)

                    def reciprocal(i):
                        dve.wait_ge(e_ok, p * NU + (i + 1))
                        V.reciprocal(st[:, 2, i:i + 1], st[:, 1, i:i + 1]).then_inc(r_ok, 1)

                    biased(0)
                    biased(1)
                    reciprocal(0)
                    biased(2)
                    reciprocal(1)
                    turned(0)
                    for i in range(NU):
                        if i + 2 < NU:
                            reciprocal(i + 2)
                        if i + 3 < NU:
                            biased(i + 3)
                        if i + 1 < NU:
                            turned(i + 1)
                    dve.wait_ge(o_ok, p * NU + NU)
                    V.memset(st[:, 0, 0:1], 0.0).then_inc(pair_ok, 1)


def mod_row(K, part, s):
    return bass.AP(tensor=K.dram["mod_rows"].tensor, offset=(2 * KD * part + s) * P, ap=[[0, P], [2 * P, KD], [1, P]])


def output(K, A):
    nc = K.nc
    ctx = ExitStack()
    with ctx:
        def sb(name, shape, dt=F32):
            return K.sb("o_" + name, shape, dt, ctx=ctx)

        def sem(name):
            return K.sem("o_" + name)

        wo = sb("wo", [P, KD, D])
        router = sb("router", [P, KD, NE])
        gt1, s2, sh2 = (sb(n, [P, 2, D]) for n in ("gt1", "s2", "sh2"))
        g2 = sb("g2", [P, D])
        xt = [sb(f"x{i}", [P, D]) for i in range(2)]
        h2 = [sb(f"h2{i}", [P, D]) for i in range(2)]
        junk = sb("junk", [P, D])
        h2T = sb("h2T", [P, KD, P])
        st = sb("stats", [P, 6, TILES])
        aff = sb("aff", [P, NE])
        bank = K.bank
        wo_in, row_in, x_in = [sem(f"wo_in{i}") for i in range(2)], sem("rows_in"), [sem(f"x_in{i}") for i in range(2)]
        v_chain, x2_ok, sq_ok, ms_ok, rt_ok, h2_ok = (sem(n) for n in ("dve_chain", "x2", "sumsq", "meansq", "root", "h2"))
        o_ps, h_ps, hta_ok, htv_ok, l_ps, max_ok, exp_ok, aff_ok, at_ps, at_ok = (
            sem(n) for n in ("out_psum", "h2T_psum", "h2T_act", "h2T_dve", "logit_psum", "max", "exp", "aff", "affT_psum",
                             "affT"))
        h2_st, z_st = sem("h2_stored"), sem("ffn_zeroed")
        x2 = K.x2

        with nc.Block() as block:
            def store(sp, i):
                sp.wait_ge(h2_ok, i + 1)
                dst = K.dram["h2d"][i * P:(i + 1) * P, :] if i < 8 else K.dram["h2p"][:, :]
                sp.dma_start(dst, h2[i % 2][:, :]).then_inc(h2_st, 16)

            @block.sync
            def _(sp):
                wv = A["w_out"].rearrange("l (k p) n -> p (l k) n", p=P)
                for j in range(2):
                    sp.dma_start(wo[:, 4 * j:4 * j + 4, :], wv[:, 4 * j:4 * j + 4, :]).then_inc(wo_in[j], 16)
                for s in range(2):
                    for part, dst in ((GT1, gt1), (SC2, s2), (SH2, sh2)):
                        sp.dma_start(dst[:, s, :], mod_row(K, part, s)).then_inc(row_in, 16)
                sp.dma_start(g2[:, :], bass.AP(tensor=A["norm2_g"].tensor, offset=0, ap=[[0, P], [1, D]]))\
                  .then_inc(row_in, 16)
                sp.dma_start(router[:, :, :], A["router"].rearrange("l (k p) e -> p (l k) e", p=P))\
                  .then_inc(row_in, 16)
                for i in range(TILES):
                    if i >= 2:
                        sp.wait_ge(x2_ok, i - 1)
                    src = A["x_sample"][0, i * P:(i + 1) * P, :] if i < 8 else A["x_prompt"][0, :, :]
                    sp.dma_start(xt[i % 2][:, :], src).then_inc(x_in[i % 2], 16)
                    dst = K.dram["ffn"][i * P:(i + 1) * P, :] if i < 8 else K.dram["ffnp"][:, :]
                    sp.dma_start(dst, K.zero[:, :]).then_inc(z_st, 16)
                    if i:
                        store(sp, i - 1)
                store(sp, TILES - 1)
                sp.wait_ge(h2_st, 16 * TILES)
                sp.wait_ge(z_st, 16 * TILES)

            @block.tensor
            def _(pe):
                def product(i):
                    for j in range(2):
                        if i == 0:
                            for w in wo_in:
                                pe.wait_ge(w, 16)
                        elif i >= 2:
                            pe.wait_ge(x2_ok, i - 1)
                        for kc in range(KD):
                            y = K.yA[:, kc, i * P:(i + 1) * P] if kc < PAIRS else K.yB[:, kc - PAIRS, i * P:(i + 1) * P]
                            last = nc.tensor.matmul(bank[2 * (i % 2) + j][:, :], y, wo[:, kc, j * 512:(j + 1) * 512],
                                                    start=(kc == 0), stop=(kc == KD - 1))
                    last.then_inc(o_ps, 1)
                product(0)
                for i in range(TILES):
                    if i + 1 < TILES:
                        product(i + 1)
                    pe.wait_ge(h2_ok, i + 1)
                    if i:
                        pe.wait_ge(hta_ok, i)
                        pe.wait_ge(htv_ok, i)
                    for k in range(KD):
                        last = nc.tensor.transpose(bank[4 + k // 4][:, (k % 4) * P:(k % 4 + 1) * P],
                                                   h2[i % 2][:, k * P:(k + 1) * P], K.ident[:, :])
                    last.then_inc(h_ps, 1)
                    pe.wait_ge(hta_ok, i + 1)
                    pe.wait_ge(htv_ok, i + 1)
                    if i == 0:
                        pe.wait_ge(row_in, 16 * 8)
                    else:
                        pe.wait_ge(aff_ok, i)
                    for k in range(KD):
                        last = nc.tensor.matmul(bank[6][:, 0:NE], h2T[:, k, :], router[:, k, :], start=(k == 0),
                                                stop=(k == KD - 1))
                    last.then_inc(l_ps, 1)
                    pe.wait_ge(aff_ok, i + 1)
                    if i:
                        pe.wait_ge(at_ok, i)
                    nc.tensor.transpose(bank[7][0:NE, 0:P], aff[:, :], K.ident[:, :]).then_inc(at_ps, 1)

            @block.scalar
            def _(act):
                for i in range(TILES):
                    act.wait_ge(x2_ok, i + 1)
                    nc.scalar.activation(junk[:, :], x2[:, i, :], ACT.Square, accum_out=st[:, 0, i:i + 1])\
                      .then_inc(sq_ok, 1)
                    act.wait_ge(ms_ok, i + 1)
                    nc.scalar.activation(st[:, 2, i:i + 1], st[:, 1, i:i + 1], ACT.Sqrt).then_inc(rt_ok, 1)
                    act.wait_ge(h_ps, i + 1)
                    nc.scalar.activation(h2T[:, 0:4, :].rearrange("p a b -> p (a b)"), bank[4][:, :], ACT.Copy)\
                      .then_inc(hta_ok, 1)
                    act.wait_ge(max_ok, i + 1)
                    nc.scalar.activation(aff[:, :], bank[6][:, 0:NE], ACT.Exp, bias=st[:, 3, i:i + 1],
                                         accum_out=st[:, 4, i:i + 1]).then_inc(exp_ok, 1)
                    act.wait_ge(at_ps, i + 1)
                    nc.scalar.activation(K.affT[:, i * P:(i + 1) * P], bank[7][0:NE, 0:P], ACT.Copy).then_inc(at_ok, 1)

            @block.vector
            def _(dve):
                V = nc.vector
                link = Link(dve, v_chain)
                dve.wait_ge(row_in, 16 * 8)
                link(V.tensor_scalar(s2[:, :, :], s2[:, :, :], 1.0, None, ALU.add))
                link(V.tensor_tensor(s2[:, :, :], s2[:, :, :], g2[:, :].unsqueeze(1).broadcast_to([P, 2, D]), ALU.mult))

                def residual(i):
                    s = 0 if i < 8 else 1
                    dve.wait_ge(o_ps, i + 1)
                    dve.wait_ge(x_in[i % 2], 16 * (i // 2 + 1))
                    for j in range(2):
                        c = slice(j * 512, (j + 1) * 512)
                        last = V.tensor_tensor(x2[:, i, c], bank[2 * (i % 2) + j][:, :], gt1[:, s, c], ALU.mult)
                    link(last)
                    V.tensor_tensor(x2[:, i, :], x2[:, i, :], xt[i % 2][:, :], ALU.add).then_inc(x2_ok, 1)

                residual(0)
                for i in range(TILES):
                    s = 0 if i < 8 else 1
                    dve.wait_ge(sq_ok, i + 1)
                    V.tensor_scalar(st[:, 1, i:i + 1], st[:, 0, i:i + 1], 1.0 / D, EPS, ALU.mult, ALU.add)\
                     .then_inc(ms_ok, 1)
                    if i + 1 < TILES:
                        residual(i + 1)
                    dve.wait_ge(rt_ok, i + 1)
                    link(V.reciprocal(st[:, 5, i:i + 1], st[:, 2, i:i + 1]))
                    if i >= 2:
                        dve.wait_ge(h2_st, 16 * (i - 1))
                    link(V.scalar_tensor_tensor(h2[i % 2][:, :], x2[:, i, :], st[:, 5, i:i + 1], s2[:, s, :], ALU.mult,
                                                ALU.mult))
                    V.tensor_tensor(h2[i % 2][:, :], h2[i % 2][:, :], sh2[:, s, :], ALU.add).then_inc(h2_ok, 1)
                    dve.wait_ge(h_ps, i + 1)
                    V.tensor_copy(h2T[:, 4:8, :].rearrange("p a b -> p (a b)"), bank[5][:, :]).then_inc(htv_ok, 1)
                    dve.wait_ge(l_ps, i + 1)
                    V.tensor_reduce(st[:, 3, i:i + 1], bank[6][:, 0:NE], AX.X, ALU.max, negate=True).then_inc(max_ok, 1)
                    dve.wait_ge(exp_ok, i + 1)
                    link(V.reciprocal(st[:, 1, i:i + 1], st[:, 4, i:i + 1]))
                    V.tensor_scalar(aff[:, :], aff[:, :], st[:, 1, i:i + 1], None, ALU.mult).then_inc(aff_ok, 1)


def topk(K, A):
    nc = K.nc
    ctx = ExitStack()
    with ctx:
        val = K.sb("k_val", [NE, TOK], ctx=ctx)
        idx = K.sb("k_idx", [NE, TOK], U32, ctx=ctx)
        idxf = K.sb("k_idxf", [NE, TOK], ctx=ctx)
        chain, picked, turned = K.sem("k_chain"), K.sem("k_picked"), K.sem("k_turned")
        with nc.Block() as block:
            @block.vector
            def _(dve):
                V = nc.vector
                link = Link(dve, chain)
                V.memset(K.idx[:, :], 0)
                V.memset(K.idxp[:, :], 0)
                for at, n, col, cap in ((0, NS, 0, CAP), (NS, NP, CAP, CAPP)):
                    a = K.affT[:, at:at + n]
                    for b in range(cap // 8):
                        c = slice(col + 8 * b, col + 8 * b + 8)
                        link(V.max(val[:, c], a))
                        link(V.max_index(idx[:, c], val[:, c], a))
                        link(V.match_replace(a, val[:, c], a, -1.0))
                V.tensor_copy(idxf[:, :], idx[:, :]).then_inc(picked, 1)
                dve.wait_ge(turned, 1)
                V.tensor_copy(K.idx[:, 0:NE], K.bank[0][:, 0:NE])
                V.tensor_copy(K.gate[:, :], K.bank[0][:, NE:2 * NE])
                V.tensor_copy(K.idxp[:, 0:NE], K.bank[1][0:CAPP, 0:NE])
                link(V.tensor_copy(K.gatep[:, :], K.bank[1][0:CAPP, NE:2 * NE]))

            @block.tensor
            def _(pe):
                pe.wait_ge(picked, 1)
                for j, src in enumerate((idxf, val)):
                    c = slice(j * NE, (j + 1) * NE)
                    nc.tensor.transpose(K.bank[0][:, c], src[:, 0:CAP], K.ident[0:NE, 0:NE])
                    last = nc.tensor.transpose(K.bank[1][0:CAPP, c], src[:, CAP:TOK], K.ident[0:NE, 0:NE])
                last.then_inc(turned, 1)


def experts(K, A):
    nc = K.nc
    ctx = ExitStack()
    DEPTH = 11
    assert FB % DEPTH == 0
    PER_BANK = 3
    MID = FB // 2
    with ctx:
        def sb(name, shape, dt=F32):
            return K.sb("e_" + name, shape, dt, ctx=ctx)

        def sem(name):
            return K.sem("e_" + name)

        wg = sb("wg", [P, DEPTH, KD, P])
        wu = sb("wu", [P, DEPTH, KD, P])
        wd = sb("wd", [P, DEPTH, D])
        xe, xp = sb("xe", [P, D]), sb("xp", [CAPP, D])
        xT = sb("xT", [P, KD, TOK])
        sg = [sb(f"sg{i}", [P, TOK]) for i in range(2)]
        tm = [sb(f"tm{i}", [P, TOK]) for i in range(2)]
        hid = sb("hid", [P, 2, TOK])
        yT = sb("yT", [P, KD, TOK])
        ye, yp = sb("ye", [P, D]), sb("yp", [CAPP, D])
        gi, si = sb("gi", [P, 1], U32), sb("si", [P, 1], U32)
        gip, sip = sb("gip", [CAPP, 1], U32), sb("sip", [CAPP, 1], U32)
        gc, gcp = sb("gc", [P, 1]), sb("gcp", [CAPP, 1])
        bank = K.bank
        w_in = [sem(f"w_in{i}") for i in range(DEPTH)]
        used = sem("w_used")
        i_ok, x_in, x_ps, xa_ok, xv_ok = sem("idx_ok"), sem("x_in"), sem("xT_psum"), sem("xT_act"), sem("xT_dve")
        gu_ps, sg_ok, tm_ok, hid_ok = sem("gu_psum"), sem("sigmoid"), sem("tm"), sem("hid")
        ya_ok, yv_ok, y_ps, yp_ps, sa_ok, sv_ok = (sem(n) for n in ("yT_act", "yT_dve", "y_psum", "yp_psum", "y_act",
                                                                    "y_dve"))
        free, sc = sem("y_free"), sem("scattered")

        with nc.Block() as block:
            @block.sync
            def _(sp):
                gv = A["e_gate"].rearrange("l e (k p) f -> p (l e) k f", p=P)
                uv = A["e_up"].rearrange("l e (k p) f -> p (l e) k f", p=P)
                dv = A["e_down"].rearrange("l e (b p) n -> p (l e) b n", p=P)
                with sp.Fori(0, NE) as e:
                    for b in range(FB):
                        s = b % DEPTH
                        sp.wait_ge(used, e * FB + (b + 1))
                        sp.dma_start(wg[:, s, :, :], gv[:, bass.ds(e, 1), :, b * P:(b + 1) * P]
                                     .rearrange("p e k f -> p (e k) f")).then_inc(w_in[s], 16)
                        sp.dma_start(wu[:, s, :, :], uv[:, bass.ds(e, 1), :, b * P:(b + 1) * P]
                                     .rearrange("p e k f -> p (e k) f")).then_inc(w_in[s], 16)
                        sp.dma_start(wd[:, s, :], dv[:, bass.ds(e, 1), b, :].rearrange("p e n -> p (e n)"))\
                          .then_inc(w_in[s], 16)

            @block.gpsimd
            def _(pool):
                def gather():
                    for dst, src, ix in ((xe, K.dram["h2d"], gi), (xp, K.dram["h2p"], gip)):
                        pool.indirect_dma_start(out=dst[:, :], out_offset=None, in_=src[:, :],
                                                in_offset=bass.IndirectOffsetOnAxis(ap=ix[:, :], axis=0))\
                            .then_inc(x_in, 16)

                pool.tensor_copy(gi[:, :], K.idx[:, 0:1])
                pool.tensor_copy(gip[:, :], K.idxp[:, 0:1]).then_inc(i_ok, 1)
                pool.wait_ge(i_ok, 1)
                gather()
                pool.sem_inc(free, 1)
                with pool.Fori(0, NE) as e:
                    K.hold(pool, x_in, e * 32 + 32)
                    pool.tensor_copy(gi[:, :], K.idx[:, bass.ds(e + 1, 1)])
                    pool.tensor_copy(gip[:, :], K.idxp[:, bass.ds(e + 1, 1)])
                    pool.tensor_copy(si[:, :], K.idx[:, bass.ds(e, 1)])
                    pool.tensor_copy(gc[:, :], K.gate[:, bass.ds(e, 1)])
                    pool.tensor_copy(gcp[:, :], K.gatep[:, bass.ds(e, 1)])
                    pool.tensor_copy(sip[:, :], K.idxp[:, bass.ds(e, 1)]).then_inc(i_ok, 1)
                    K.hold(pool, i_ok, e + 2)
                    K.hold(pool, x_ps, e + 1)
                    gather()
                    K.hold(pool, sa_ok, e * 2 + 4)
                    K.hold(pool, sv_ok, e * 2 + 4)
                    for src, dst, ix in ((ye, K.dram["ffn"], si), (yp, K.dram["ffnp"], sip)):
                        pool.indirect_dma_start(out=dst[:, :], out_offset=bass.IndirectOffsetOnAxis(ap=ix[:, :], axis=0),
                                                in_=src[:, :], in_offset=None, compute_op=ALU.add).then_inc(sc, 16)
                    K.hold(pool, sc, e * 32 + 32)
                    pool.sem_inc(free, 1)
                pool.wait_ge(x_in, 32 * (NE + 1))

            @block.tensor
            def _(pe):
                def tokens(e):
                    pe.wait_ge(x_in, e * 32 + 32)
                    for k in range(KD):
                        b, c = 3 + k // PER_BANK, (k % PER_BANK) * TOK
                        nc.tensor.transpose(bank[b][:, c:c + CAP], xe[:, k * P:(k + 1) * P], K.ident[:, :])
                        last = nc.tensor.transpose(bank[b][:, c + CAP:c + TOK], xp[:, k * P:(k + 1) * P],
                                                   K.ident[0:CAPP, 0:CAPP])
                    last.then_inc(x_ps, 1)

                def gate_up(e, b):
                    e, b = (e, b) if b < FB else (e + 1, b - FB)
                    s = b % DEPTH
                    pe.wait_ge(w_in[s], e * 96 + 48 * (b // DEPTH + 1))
                    if b == 0:
                        pe.wait_ge(xa_ok, e + 1)
                        pe.wait_ge(xv_ok, e + 1)
                    pe.wait_ge(hid_ok, e * FB + (b + 1))
                    for j, w in enumerate((wg, wu)):
                        for k in range(KD):
                            last = nc.tensor.matmul(bank[6 + b % 2][:, j * TOK:(j + 1) * TOK], w[:, s, k, :],
                                                    xT[:, k, :], start=(k == 0), stop=(k == KD - 1))
                    last.then_inc(gu_ps, 1)

                def down(e, b):
                    s = b % DEPTH
                    pe.wait_ge(hid_ok, e * FB + (b + 3))
                    if b == 0:
                        pe.wait_ge(ya_ok, e + 1)
                        pe.wait_ge(yv_ok, e + 1)
                    for k in range(KD):
                        c = (k % PER_BANK) * TOK
                        last = nc.tensor.matmul(bank[k // PER_BANK][:, c:c + TOK], wd[:, s, k * P:(k + 1) * P],
                                                hid[:, b % 2, :], start=(b == 0 and k % PER_BANK == 0),
                                                stop=(b == FB - 1), skip_group_check=True)
                    last.then_inc(used, 1)

                def outputs(e):
                    def prompt(j):
                        for k in range(4):
                            last = nc.tensor.transpose(bank[5][0:CAPP, k * P:(k + 1) * P], yT[:, 4 * j + k, CAP:TOK],
                                                       K.ident[:, :])
                        last.then_inc(yp_ps, 1)

                    pe.wait_ge(ya_ok, e + 2)
                    pe.wait_ge(yv_ok, e + 2)
                    prompt(0)
                    for j in range(2):
                        for k in range(4):
                            last = nc.tensor.transpose(bank[3 + j][:, k * P:(k + 1) * P], yT[:, 4 * j + k, 0:CAP],
                                                       K.ident[:, :])
                        last.then_inc(y_ps, 1)
                    pe.wait_ge(sa_ok, e * 2 + 3)
                    prompt(1)

                def expert(e, last=False):
                    for b in range(FB):
                        down(e, b)
                        if b + 2 < FB or not last:
                            gate_up(e, b + 2)
                        if b == MID and not last:
                            pe.wait_ge(sa_ok, e * 2 + 2)
                            pe.wait_ge(sv_ok, e * 2 + 2)
                            tokens(e + 1)
                    outputs(e)

                pe.sem_inc(used, DEPTH)
                tokens(0)
                gate_up(0, 0)
                gate_up(0, 1)
                with pe.Fori(0, NE - 1) as e:
                    expert(e)
                expert(NE - 1, last=True)

            @block.scalar
            def _(act):
                def tokens(e):
                    act.wait_ge(x_ps, e + 1)
                    nc.scalar.activation(xT[:, 0:3, :].rearrange("p a b -> p (a b)"), bank[3][:, 0:3 * TOK], ACT.Copy)
                    nc.scalar.activation(xT[:, 6:8, :].rearrange("p a b -> p (a b)"), bank[5][:, 0:2 * TOK], ACT.Copy)\
                      .then_inc(xa_ok, 1)

                def hidden(e, b):
                    act.wait_ge(gu_ps, e * FB + (b + 1))
                    nc.scalar.activation(sg[b % 2][:, :], bank[6 + b % 2][:, 0:TOK], ACT.Sigmoid).then_inc(sg_ok, 1)

                def outputs(e):
                    act.wait_ge(used, e * FB + (FB + DEPTH))
                    nc.scalar.activation(yT[:, 6:8, :].rearrange("p a b -> p (a b)"), bank[2][:, 0:2 * TOK], ACT.Copy)
                    nc.scalar.activation(yT[:, 0:3, :].rearrange("p a b -> p (a b)"), bank[0][:, 0:3 * TOK], ACT.Copy)\
                      .then_inc(ya_ok, 1)

                def scaled(e):
                    act.wait_ge(free, e + 1)
                    act.wait_ge(i_ok, e + 2)
                    for j in range(2):
                        act.wait_ge(yp_ps, e * 2 + (j + 1))
                        nc.scalar.activation(yp[:, j * 512:(j + 1) * 512], bank[5][0:CAPP, :], ACT.Copy,
                                             scale=gcp[:, :]).then_inc(sa_ok, 1)

                def expert(e, last=False):
                    for b in range(2, FB):
                        hidden(e, b)
                        if b == FB - 1 and not last:
                            tokens(e + 1)
                    if not last:
                        hidden(e, FB)
                    outputs(e)
                    if not last:
                        hidden(e, FB + 1)
                    scaled(e)

                act.sem_inc(ya_ok, 1)
                act.sem_inc(sa_ok, 2)
                tokens(0)
                hidden(0, 0)
                hidden(0, 1)
                with act.Fori(0, NE - 1) as e:
                    expert(e)
                expert(NE - 1, last=True)

            @block.vector
            def _(dve):
                V = nc.vector

                def tokens(e):
                    dve.wait_ge(x_ps, e + 1)
                    V.tensor_copy(xT[:, 3:6, :].rearrange("p a b -> p (a b)"), bank[4][:, 0:3 * TOK]).then_inc(xv_ok, 1)

                def hidden(e, b):
                    dve.wait_ge(sg_ok, e * FB + (b + 1))
                    V.tensor_tensor(tm[b % 2][:, :], bank[6 + b % 2][:, 0:TOK], sg[b % 2][:, :], ALU.mult)\
                     .then_inc(tm_ok, 1)
                    dve.wait_ge(tm_ok, e * FB + (b + 1))
                    V.tensor_tensor(hid[:, b % 2, :], bank[6 + b % 2][:, TOK:2 * TOK], tm[b % 2][:, :], ALU.mult)\
                     .then_inc(hid_ok, 1)

                def outputs(e):
                    dve.wait_ge(used, e * FB + (FB + DEPTH))
                    V.tensor_copy(yT[:, 3:6, :].rearrange("p a b -> p (a b)"), bank[1][:, 0:3 * TOK]).then_inc(yv_ok, 1)

                def scaled(e):
                    dve.wait_ge(free, e + 1)
                    dve.wait_ge(i_ok, e + 2)
                    for j in range(2):
                        dve.wait_ge(y_ps, e * 2 + (j + 1))
                        V.tensor_scalar(ye[:, j * 512:(j + 1) * 512], bank[3 + j][:, :], gc[:, :], None, ALU.mult)\
                         .then_inc(sv_ok, 1)

                def expert(e, last=False):
                    for b in range(2, FB):
                        hidden(e, b)
                        if b == FB - 1 and not last:
                            dve.wait_ge(gu_ps, e * FB + FB)
                            tokens(e + 1)
                    if not last:
                        hidden(e, FB)
                    outputs(e)
                    if not last:
                        hidden(e, FB + 1)
                    scaled(e)

                dve.sem_inc(hid_ok, 2)
                dve.sem_inc(yv_ok, 1)
                dve.sem_inc(sv_ok, 2)
                tokens(0)
                hidden(0, 0)
                hidden(0, 1)
                with dve.Fori(0, NE - 1) as e:
                    expert(e)
                expert(NE - 1, last=True)


def final(K, A):
    nc = K.nc
    ctx = ExitStack()
    with ctx:
        def sb(name, shape, dt=F32):
            return K.sb("f_" + name, shape, dt, ctx=ctx)

        def sem(name):
            return K.sem("f_" + name)

        gt2 = sb("gt2", [P, 2, D])
        gf = sb("gf", [P, D])
        f = [sb(f"f{i}", [P, D]) for i in range(4)]
        junk = sb("junk", [P, D])
        st = sb("stats", [P, 4, TILES])
        rows, f_in = sem("rows_in"), [sem(f"f_in{i}") for i in range(4)]
        chain, x_ok, sq_ok, ms_ok, rt_ok, y_ok = (sem(n) for n in ("chain", "x3", "sumsq", "meansq", "root", "y"))
        y_st = [sem(f"y_stored{i}") for i in range(4)]
        with nc.Block() as block:
            @block.sync
            def _(sp):
                for s in range(2):
                    sp.dma_start(gt2[:, s, :], mod_row(K, GT2, s)).then_inc(rows, 16)
                sp.dma_start(gf[:, :], bass.AP(tensor=A["final_norm_g"].tensor, offset=0, ap=[[0, P], [1, D]]))\
                  .then_inc(rows, 16)
                for i in range(TILES):
                    if i >= 4:
                        sp.wait_ge(y_st[i % 4], 16 * (i // 4))
                    src = K.dram["ffn"][i * P:(i + 1) * P, :] if i < 8 else K.dram["ffnp"][:, :]
                    sp.dma_start(f[i % 4][:, :], src).then_inc(f_in[i % 4], 16)

            @block.scalar
            def _(act):
                for i in range(TILES + 1):
                    if i < TILES:
                        act.wait_ge(x_ok, i + 1)
                        nc.scalar.activation(junk[:, :], K.x2[:, i, :], ACT.Square, accum_out=st[:, 0, i:i + 1])\
                          .then_inc(sq_ok, 1)
                        act.wait_ge(ms_ok, i + 1)
                        nc.scalar.activation(st[:, 2, i:i + 1], st[:, 1, i:i + 1], ACT.Sqrt).then_inc(rt_ok, 1)
                    if i:
                        t = i - 1
                        act.wait_ge(y_ok, t + 1)
                        dst = A["y_sample"][0, t * P:(t + 1) * P, :] if t < 8 else A["y_prompt"][0, :, :]
                        act.dma_start(dst, f[t % 4][:, :]).then_inc(y_st[t % 4], 16)
                for i in range(4):
                    act.wait_ge(y_st[i], 16 * len(range(i, TILES, 4)))

            @block.vector
            def _(dve):
                V = nc.vector
                link = Link(dve, chain)
                dve.wait_ge(rows, 48)

                def add(i):
                    s = 0 if i < 8 else 1
                    dve.wait_ge(f_in[i % 4], 16 * (i // 4 + 1))
                    link(V.tensor_tensor(f[i % 4][:, :], f[i % 4][:, :], gt2[:, s, :], ALU.mult))
                    V.tensor_tensor(K.x2[:, i, :], K.x2[:, i, :], f[i % 4][:, :], ALU.add).then_inc(x_ok, 1)
                    dve.wait_ge(sq_ok, i + 1)
                    V.tensor_scalar(st[:, 1, i:i + 1], st[:, 0, i:i + 1], 1.0 / D, EPS, ALU.mult, ALU.add)\
                     .then_inc(ms_ok, 1)

                add(0)
                for i in range(TILES):
                    if i + 1 < TILES:
                        add(i + 1)
                    dve.wait_ge(rt_ok, i + 1)
                    link(V.reciprocal(st[:, 3, i:i + 1], st[:, 2, i:i + 1]))
                    V.scalar_tensor_tensor(f[i % 4][:, :], K.x2[:, i, :], st[:, 3, i:i + 1], gf[:, :], ALU.mult,
                                           ALU.mult).then_inc(y_ok, 1)


def trunk(nc, A):
    ctx = ExitStack()
    with ctx:
        K = Chip(nc, ctx)
        for name, shape in (("mod_rows", (96, P)), ("spread", (GRID, HEADS * (2 * WR - 1) * P)), ("h2d", (NS, D)),
                            ("h2p", (NP, D)), ("ffn", (NS, D)), ("ffnp", (NP, D))):
            K.dram[name] = nc.dram_tensor("scratch_" + name, shape, F32, kind="Internal").ap()
        K.ident = K.sb("ident", [P, P])
        K.eps = K.sb("eps", [P, 3])
        K.zero = K.sb("zero", [P, D])
        K.vecT = K.sb("vecT", [P, V_ROWS])
        K.modT = K.sb("modT", [P, 16, 2])
        K.s1 = K.sb("s1", [P, KD, 2])
        K.affT = K.sb("affT", [NE, NT])
        K.idx = K.sb("idx", [P, NE + 1], U32)
        K.idxp = K.sb("idxp", [CAPP, NE + 1], U32)
        K.gate = K.sb("gate", [P, NE])
        K.gatep = K.sb("gatep", [CAPP, NE])
        big = K.sb("hT_x2", [P, KD * NT])
        K.hT = big[:, :].rearrange("p (k t) -> p k t", k=KD)
        K.x2 = big[:, :].rearrange("p (i n) -> p i n", i=TILES)
        mixed = ExitStack()
        with mixed:
            K.yA = K.sb("yA", [P, PAIRS, NT], ctx=mixed)
            scan = ExitStack()
            with scan:
                K.head_ones = K.sb("head_ones", [P, P], ctx=scan)
                K.head_mask = K.sb("head_mask", [P, P], ctx=scan)
                K.causal = K.sb("causal", [P, 2, 4, P], BF16, ctx=scan)
                K.level = K.sb("level", [P, 2, 7, P], BF16, ctx=scan)
                K.scan_keep = K.sb("scan_keep", [P, NT], BF16, ctx=scan)
                modulation(K, A)
                K.next_stage()
                norm1(K, A)
                K.next_stage()
                rwkv(K, A)
                K.next_stage()
            K.yB = K.sb("yB", [P, PAIRS, NT], ctx=mixed)
            attention(K, A)
            K.next_stage()
            output(K, A)
            K.next_stage()
        topk(K, A)
        K.next_stage()
        experts(K, A)
        K.next_stage()
        final(K, A)


_INS = ["x_prompt", "x_sample", "cache_na_k", "cache_na_v", "state_rwkv", "c", "c_ctx", "final_norm_g", "norm1_g",
        "norm2_g", "w_mod", "b_mod", "w_in", "mu_prev", "mu_next", "w0", "w_up", "a0", "a_up", "g_up", "k_k", "k_a",
        "r_k", "gn_g", "gn_b", "rpb", "w_out", "router", "e_gate", "e_up", "e_down"]
_OUTS = [("y_prompt", (1, NP, D)), ("y_sample", (1, NS, D)), ("new_k", (1, 1, NP, HEADS, HN)),
         ("new_v", (1, 1, NP, HEADS, HN)), ("new_s", (1, 1, 2, HEADS, HN, HN))]


def kernel(**inputs):
    import numpy as np
    import concourse.bacc as bacc
    from concourse.bass_utils import run_bass_kernel_spmd

    nc = bacc.Bacc("TRN2", target_bir_lowering=False, num_devices=1)
    arrays, A = {}, {}
    for name in _INS:
        a = np.ascontiguousarray(inputs[name])
        arrays["in_" + name] = a
        A[name] = nc.dram_tensor("in_" + name, a.shape, mybir.dt.from_np(a.dtype), kind="ExternalInput").ap()
    for name, shape in _OUTS:
        A[name] = nc.dram_tensor("out_" + name, shape, F32, kind="ExternalOutput").ap()
    trunk(nc, A)
    r = run_bass_kernel_spmd(nc, [arrays], core_ids=[0])
    return tuple(r.results[0]["out_" + name] for name, _ in _OUTS)
```
